# Optimizing a Trainium2 kernel written in Bass

```python
import jax
import jax.numpy as jnp
from jax import lax
import numpy as np

D_MODEL = 1024
BATCH = 1
SEQ = 1024
DEPTH = 2
DEC_BATCH = 8
DEC_SEQ = 1
PAST_LEN = 4096
PAGE_SIZE = 128

N_EVEN = (DEPTH + 1) // 2
N_ODD = DEPTH // 2
MIX_W = D_MODEL
A_W = MIX_W // 2
B_W = MIX_W - A_W
H_B = 8
HD_B = B_W // H_B
CONV_A_W = 3
Q_BLOCK = 128
E_IN = 3 * A_W + 3 * B_W + H_B
C_W = MIX_W // 2
H_C = 4
DK_C = C_W // H_C
CHUNK = 128
P_W = MIX_W - C_W
POOL_WINDOWS = (2, 4, 8, 16)
POOL_G = P_W // len(POOL_WINDOWS)
POOL_PREV = max(POOL_WINDOWS) - 1
O_IN = 4 * C_W + 2 * H_C + P_W
D_FF = ((8 * D_MODEL // 3 + 127) // 128) * 128
FFN_CONV_W = 3
EPS = 1e-6

kernel_name = 'hybrid_conv_fox_mlstm_pool_step'

def rms_norm(x, g):
    xf = x.astype(jnp.float32)
    y = xf * lax.rsqrt(jnp.mean(xf * xf, axis=-1, keepdims=True) + EPS)
    return (y * g.astype(jnp.float32)).astype(x.dtype)

def causal_dwconv(u, prev, w):
    width = w.shape[0]
    t_len = u.shape[1]
    ext = jnp.concatenate([prev.astype(u.dtype), u], axis=1)
    y = w[0] * ext[:, 0:t_len]
    for j in range(1, width):
        y = y + w[j] * ext[:, j:j + t_len]
    return y, ext[:, ext.shape[1] - (width - 1):]

def gather_pages(cache, page_table):
    g = cache[page_table]
    return g.reshape((g.shape[0], g.shape[1] * g.shape[2]) + g.shape[3:])

def even_project(h, w_in, b_f, conv_w, conv_prev):
    z = h @ w_in
    cuts = np.cumsum([A_W, A_W, A_W, B_W, B_W, B_W]).tolist()
    u, gb, gc, q, k, v, fz = jnp.split(z, cuts, axis=-1)
    a, conv_new = causal_dwconv(gc * u, conv_prev, conv_w)
    a = gb * a
    logf = jax.nn.log_sigmoid(fz.astype(jnp.float32) + b_f.astype(jnp.float32))
    shp = h.shape[:2] + (H_B, HD_B)
    return a, q.reshape(shp), k.reshape(shp), v.reshape(shp), logf, conv_new

def fox_prompt(q, k, v, logf):
    b, s = q.shape[:2]
    nb = s // Q_BLOCK
    f_cum = jnp.cumsum(logf, axis=1).transpose(0, 2, 1)
    qb = q.reshape(b, nb, Q_BLOCK, H_B, HD_B).transpose(1, 0, 2, 3, 4)
    fb = f_cum.reshape(b, H_B, nb, Q_BLOCK).transpose(2, 0, 1, 3)
    k_pos = jnp.arange(s)
    scale = HD_B ** -0.5

    def block(args):
        i, q_i, f_i = args
        sc = jnp.einsum('bqhd,bkhd->bhqk', q_i, k).astype(jnp.float32) * scale
        sc = sc + (f_i[..., :, None] - f_cum[..., None, :])
        q_pos = i * Q_BLOCK + jnp.arange(Q_BLOCK)
        sc = jnp.where(k_pos[None, :] <= q_pos[:, None], sc, -jnp.inf)
        p = jax.nn.softmax(sc, axis=-1).astype(v.dtype)
        return jnp.einsum('bhqk,bkhd->bqhd', p, v)

    o = lax.map(block, (jnp.arange(nb), qb, fb))
    return o.transpose(1, 0, 2, 3, 4).reshape(b, s, H_B * HD_B)

def fox_sample(q, k, v, logf, k_past, v_past, logf_past):
    p_len, t_len = k_past.shape[1], q.shape[1]
    f_cum = jnp.cumsum(jnp.concatenate([logf_past.astype(jnp.float32), logf], axis=1), axis=1).transpose(0, 2, 1)
    f_q = f_cum[..., p_len:]
    scale = HD_B ** -0.5
    s_past = (jnp.einsum('bqhd,bkhd->bhqk', q, k_past.astype(q.dtype)).astype(jnp.float32) * scale
              + (f_q[..., :, None] - f_cum[..., None, :p_len]))
    s_new = (jnp.einsum('bqhd,bkhd->bhqk', q, k).astype(jnp.float32) * scale
             + (f_q[..., :, None] - f_q[..., None, :]))
    causal = jnp.tril(jnp.ones((t_len, t_len), dtype=bool))
    s_new = jnp.where(causal, s_new, -jnp.inf)
    p = jax.nn.softmax(jnp.concatenate([s_past, s_new], axis=-1), axis=-1).astype(v.dtype)
    o = (jnp.einsum('bhqk,bkhd->bqhd', p[..., :p_len], v_past.astype(v.dtype))
         + jnp.einsum('bhqk,bkhd->bqhd', p[..., p_len:], v))
    return o.reshape(q.shape[0], t_len, H_B * HD_B)

def odd_project(h, w_in, b_i, b_f):
    z = h @ w_in
    cuts = np.cumsum([C_W, C_W, C_W, C_W, H_C, H_C]).tolist()
    q, k, v, o, iz, fz, p = jnp.split(z, cuts, axis=-1)
    shp = h.shape[:2] + (H_C, DK_C)
    log_i = iz.astype(jnp.float32) + b_i.astype(jnp.float32)
    log_f = jax.nn.log_sigmoid(fz.astype(jnp.float32) + b_f.astype(jnp.float32))
    return (q.reshape(shp), (k * DK_C ** -0.5).reshape(shp), v.reshape(shp),
            jax.nn.sigmoid(o), log_i, log_f, p)

def mlstm_chunk(carry, inp):
    c, n, m = carry
    q, k, v, li, lf = inp
    l_len = q.shape[2]
    bcum = jnp.cumsum(lf, axis=-1)
    causal = jnp.tril(jnp.ones((l_len, l_len), dtype=bool))
    dlog = jnp.where(causal, bcum[..., :, None] - bcum[..., None, :] + li[..., None, :], -jnp.inf)
    inter = bcum + m[..., None]
    m_t = jnp.maximum(inter, jnp.max(dlog, axis=-1))
    sc = jnp.einsum('bhtd,bhsd->bhts', q, k) * jnp.exp(dlog - m_t[..., None])
    w_inter = jnp.exp(inter - m_t)
    num = jnp.einsum('bhts,bhse->bhte', sc, v) + w_inter[..., None] * jnp.einsum('bhtd,bhde->bhte', q, c)
    den = jnp.sum(sc, axis=-1) + w_inter * jnp.einsum('bhtd,bhd->bht', q, n)
    h = num / jnp.maximum(jnp.abs(den), jnp.exp(-m_t))[..., None]
    g = bcum[..., -1:] - bcum + li
    m_new = jnp.maximum(bcum[..., -1] + m, jnp.max(g, axis=-1))
    a = jnp.exp(bcum[..., -1] + m - m_new)
    wg = jnp.exp(g - m_new[..., None])
    c_new = a[..., None, None] * c + jnp.einsum('bhs,bhsd,bhse->bhde', wg, k, v)
    n_new = a[..., None] * n + jnp.einsum('bhs,bhsd->bhd', wg, k)
    return (c_new, n_new, m_new), h

def mlstm_prompt(q, k, v, log_i, log_f):
    b, s = q.shape[:2]
    nc = s // CHUNK

    def chunks(x):
        return x.reshape((b, nc, CHUNK) + x.shape[2:]).swapaxes(0, 1).swapaxes(2, 3).astype(jnp.float32)

    init = (jnp.zeros((b, H_C, DK_C, DK_C), jnp.float32),
            jnp.zeros((b, H_C, DK_C), jnp.float32),
            jnp.zeros((b, H_C), jnp.float32))
    (c, n, m), hs = lax.scan(mlstm_chunk, init, (chunks(q), chunks(k), chunks(v), chunks(log_i), chunks(log_f)))
    h = hs.transpose(1, 0, 3, 2, 4).reshape(b, s, C_W)
    return h, c, n, m

def mlstm_sample(q, k, v, log_i, log_f, c0, n0, m0):
    def heads_first(x):
        return jnp.swapaxes(x, 1, 2).astype(jnp.float32)

    carry = (c0.astype(jnp.float32), n0.astype(jnp.float32), m0.astype(jnp.float32))
    (c, n, m), h = mlstm_chunk(carry, (heads_first(q), heads_first(k), heads_first(v),
                                       heads_first(log_i), heads_first(log_f)))
    h = h.transpose(0, 2, 1, 3).reshape(q.shape[0], q.shape[1], C_W)
    return h, c, n, m

def pool_mix(p, prev, pos0, w_pool, scale):
    b, t_len = p.shape[:2]
    ext = jnp.concatenate([prev.astype(p.dtype), p], axis=1)
    ext32 = ext.astype(jnp.float32)
    csum = jnp.concatenate([jnp.zeros((b, 1, P_W), jnp.float32), jnp.cumsum(ext32, axis=1)], axis=1)
    upto = csum[:, POOL_PREV + 1:]
    cur = ext32[:, POOL_PREV:]
    pos = (pos0 + jnp.arange(t_len)).astype(jnp.float32)
    outs = []
    for gi, win in enumerate(POOL_WINDOWS):
        sl = slice(gi * POOL_G, (gi + 1) * POOL_G)
        lo = POOL_PREV + 1 - win
        window_sum = upto[..., sl] - csum[:, lo:lo + t_len, sl]
        mean = window_sum / jnp.minimum(float(win), pos + 1.0)[None, :, None]
        outs.append(jnp.einsum('btc,cd->btd', mean - cur[..., sl], w_pool[gi].astype(jnp.float32)))
    y = jnp.concatenate(outs, axis=-1) * scale.astype(jnp.float32)
    return y.astype(p.dtype), ext[:, ext.shape[1] - POOL_PREV:]

def conv_ffn(h, w_up, conv_w, conv_b, w_down, prev):
    z = h @ w_up
    g, u = jnp.split(z, [D_FF], axis=-1)
    g_c, new_prev = causal_dwconv(g, prev, conv_w)
    return (jax.nn.silu(g_c + conv_b) * u) @ w_down, new_prev

def setup_inputs(seed: int = 0) -> dict:
    key = jax.random.key(seed)
    ks = jax.random.split(key, 32)
    f32 = jnp.float32
    n_pages = PAST_LEN // PAGE_SIZE
    n_used = DEC_BATCH * n_pages
    n_phys = n_used + n_used // 4

    def nrm(k, shape, s=1.0):
        return s * jax.random.normal(k, shape, f32)

    inputs = {}
    inputs['x_prompt'] = nrm(ks[0], (BATCH, SEQ, D_MODEL))
    inputs['x_sample'] = nrm(ks[1], (DEC_BATCH, DEC_SEQ, D_MODEL))
    inputs['cache_k'] = nrm(ks[2], (N_EVEN, n_phys, PAGE_SIZE, H_B, HD_B))
    inputs['cache_v'] = nrm(ks[3], (N_EVEN, n_phys, PAGE_SIZE, H_B, HD_B))
    inputs['cache_logf'] = jax.nn.log_sigmoid(nrm(ks[4], (N_EVEN, n_phys, PAGE_SIZE, H_B)) + 3.0)
    inputs['state_conv_a'] = nrm(ks[5], (N_EVEN, DEC_BATCH, CONV_A_W - 1, A_W))
    inputs['state_mlstm_c'] = nrm(ks[6], (N_ODD, DEC_BATCH, H_C, DK_C, DK_C), 0.1)
    inputs['state_mlstm_n'] = nrm(ks[7], (N_ODD, DEC_BATCH, H_C, DK_C))
    inputs['state_mlstm_m'] = nrm(ks[8], (N_ODD, DEC_BATCH, H_C))
    inputs['state_pool'] = nrm(ks[9], (N_ODD, DEC_BATCH, POOL_PREV, P_W))
    inputs['state_ffn_conv'] = nrm(ks[10], (DEPTH, DEC_BATCH, FFN_CONV_W - 1, D_FF))
    inputs['page_table'] = jax.random.permutation(ks[11], n_phys)[:n_used].reshape(DEC_BATCH, n_pages).astype(jnp.int32)
    inputs['norm_mix'] = 1.0 + nrm(ks[12], (DEPTH, D_MODEL), 0.02)
    inputs['norm_ffn'] = 1.0 + nrm(ks[13], (DEPTH, D_MODEL), 0.02)
    inputs['norm_final'] = 1.0 + nrm(ks[14], (D_MODEL,), 0.02)
    inputs['w_in_even'] = nrm(ks[15], (N_EVEN, D_MODEL, E_IN), D_MODEL ** -0.5)
    inputs['b_forget_even'] = jax.random.uniform(ks[16], (N_EVEN, H_B), f32, 1.0, 4.0)
    inputs['conv_a'] = nrm(ks[17], (N_EVEN, CONV_A_W, A_W), CONV_A_W ** -0.5)
    inputs['w_out_even'] = nrm(ks[18], (N_EVEN, A_W + B_W, D_MODEL), (A_W + B_W) ** -0.5)
    inputs['w_in_odd'] = nrm(ks[19], (N_ODD, D_MODEL, O_IN), D_MODEL ** -0.5)
    inputs['b_igate_odd'] = nrm(ks[20], (N_ODD, H_C), 0.1)
    inputs['b_fgate_odd'] = jax.random.uniform(ks[21], (N_ODD, H_C), f32, 3.0, 6.0)
    inputs['w_pool_odd'] = nrm(ks[22], (N_ODD, len(POOL_WINDOWS), POOL_G, POOL_G), POOL_G ** -0.5)
    inputs['pool_scale_odd'] = 1.0 + nrm(ks[23], (N_ODD, P_W), 0.1)
    inputs['w_out_odd'] = nrm(ks[24], (N_ODD, C_W + P_W, D_MODEL), (C_W + P_W) ** -0.5)
    inputs['w_up'] = nrm(ks[25], (DEPTH, D_MODEL, 2 * D_FF), D_MODEL ** -0.5)
    inputs['ffn_conv_w'] = nrm(ks[26], (DEPTH, FFN_CONV_W, D_FF), FFN_CONV_W ** -0.5)
    inputs['ffn_conv_b'] = nrm(ks[27], (DEPTH, D_FF), 0.02)
    inputs['w_down'] = nrm(ks[28], (DEPTH, D_FF, D_MODEL), D_FF ** -0.5)
    return inputs

def reference(x_prompt, x_sample, cache_k, cache_v, cache_logf, state_conv_a, state_mlstm_c,
              state_mlstm_n, state_mlstm_m, state_pool, state_ffn_conv, page_table,
              norm_mix, norm_ffn, norm_final, w_in_even, b_forget_even, conv_a, w_out_even,
              w_in_odd, b_igate_odd, b_fgate_odd, w_pool_odd, pool_scale_odd, w_out_odd,
              w_up, ffn_conv_w, ffn_conv_b, w_down):
    xp, xs = x_prompt, x_sample
    b = xp.shape[0]
    k_p, k_s, v_p, v_s, lf_p, lf_s, ca_p, ca_s = [], [], [], [], [], [], [], []
    c_p, c_s, n_p, n_s, m_p, m_s, pl_p, pl_s = [], [], [], [], [], [], [], []
    ff_p, ff_s = [], []
    for layer in range(DEPTH):
        hp = rms_norm(xp, norm_mix[layer])
        hs = rms_norm(xs, norm_mix[layer])
        if layer % 2 == 0:
            e = layer // 2
            a, q, k, v, lf, cnew = even_project(hp, w_in_even[e], b_forget_even[e], conv_a[e],
                                                jnp.zeros((b, CONV_A_W - 1, A_W), hp.dtype))
            att = fox_prompt(q, k, v, lf)
            xp = xp + jnp.concatenate([a, att], axis=-1) @ w_out_even[e]
            k_p.append(k)
            v_p.append(v)
            lf_p.append(lf)
            ca_p.append(cnew)
            a, q, k, v, lf, cnew = even_project(hs, w_in_even[e], b_forget_even[e], conv_a[e], state_conv_a[e])
            att = fox_sample(q, k, v, lf,
                             gather_pages(cache_k[e], page_table),
                             gather_pages(cache_v[e], page_table),
                             gather_pages(cache_logf[e], page_table))
            xs = xs + jnp.concatenate([a, att], axis=-1) @ w_out_even[e]
            k_s.append(k)
            v_s.append(v)
            lf_s.append(lf)
            ca_s.append(cnew)
        else:
            o = layer // 2
            q, k, v, og, li, lf, pin = odd_project(hp, w_in_odd[o], b_igate_odd[o], b_fgate_odd[o])
            hc, c, n, m = mlstm_prompt(q, k, v, li, lf)
            pout, pnew = pool_mix(pin, jnp.zeros((b, POOL_PREV, P_W), hp.dtype), 0,
                                  w_pool_odd[o], pool_scale_odd[o])
            xp = xp + jnp.concatenate([og * hc.astype(og.dtype), pout], axis=-1) @ w_out_odd[o]
            c_p.append(c)
            n_p.append(n)
            m_p.append(m)
            pl_p.append(pnew)
            q, k, v, og, li, lf, pin = odd_project(hs, w_in_odd[o], b_igate_odd[o], b_fgate_odd[o])
            hc, c, n, m = mlstm_sample(q, k, v, li, lf, state_mlstm_c[o], state_mlstm_n[o], state_mlstm_m[o])
            pout, pnew = pool_mix(pin, state_pool[o], PAST_LEN, w_pool_odd[o], pool_scale_odd[o])
            xs = xs + jnp.concatenate([og * hc.astype(og.dtype), pout], axis=-1) @ w_out_odd[o]
            c_s.append(c)
            n_s.append(n)
            m_s.append(m)
            pl_s.append(pnew)
        hp = rms_norm(xp, norm_ffn[layer])
        hs = rms_norm(xs, norm_ffn[layer])
        f, fnew = conv_ffn(hp, w_up[layer], ffn_conv_w[layer], ffn_conv_b[layer], w_down[layer],
                           jnp.zeros((b, FFN_CONV_W - 1, D_FF), hp.dtype))
        xp = xp + f
        ff_p.append(fnew)
        f, fnew = conv_ffn(hs, w_up[layer], ffn_conv_w[layer], ffn_conv_b[layer], w_down[layer],
                           state_ffn_conv[layer])
        xs = xs + f
        ff_s.append(fnew)
    y_prompt = rms_norm(xp, norm_final)
    y_sample = rms_norm(xs, norm_final)
    return (y_prompt, y_sample,
            jnp.stack(k_p), jnp.stack(k_s), jnp.stack(v_p), jnp.stack(v_s),
            jnp.stack(lf_p), jnp.stack(lf_s), jnp.stack(ca_p), jnp.stack(ca_s),
            jnp.stack(c_p), jnp.stack(c_s), jnp.stack(n_p), jnp.stack(n_s),
            jnp.stack(m_p), jnp.stack(m_s), jnp.stack(pl_p), jnp.stack(pl_s),
            jnp.stack(ff_p), jnp.stack(ff_s))


_drawn_inputs = setup_inputs


def setup_inputs(seed=0):
    import zlib

    import numpy as np

    out = dict(_drawn_inputs(seed))
    spreads = {}
    factors = {}
    for name, (base, spread) in spreads.items():
        noise = np.random.default_rng([zlib.crc32(name.encode()), seed]).standard_normal(out[name].shape)
        drawn = base * np.exp(spread * noise) if base else spread * noise
        out[name] = jnp.asarray(drawn.astype(out[name].dtype))
    for name, factor in factors.items():
        out[name] = (out[name] * factor).astype(out[name].dtype)
    return out
```

```python
from contextlib import ExitStack

import numpy as np

import concourse.bass as bass
from concourse import mybir

F32 = mybir.dt.float32
F32R = mybir.dt.float32r
I32 = mybir.dt.int32
ALU = mybir.AluOpType
ACT = mybir.ActivationFunctionType
AX = mybir.AxisListType
RMAX = bass.bass_isa.ReduceOp.max

P = 128
D = 1024
ND = D // P
TP = 1024
NB = TP // P
B = 8
T = TP + B
BANKS = 3
TC = T // BANKS
PAGES = 32
PG = 4
GROUPS = B * PAGES // PG
HB, HD = 8, 64
HC, DK = 4, 128
NW = 4
FF = 2816
NF = FF // P
FI = NF // 2
SLOTS = 3
UNIT = 1024
WINS = (2, 4, 8, 16)
PREV = 15
EPS = 1e-6
NEG = -1.0e30

O_GMIX, O_GFFN, O_GFIN = 0, 2 * ND, 4 * ND
O_CONVA = 5 * ND
O_PSCALE = O_CONVA + NW * 3
O_GB = O_PSCALE + NW
O_SCONVA = O_GB + 2
O_RCP = O_SCONVA + NW * B * 2
O_N0 = O_RCP + NW * PREV
O_M0 = O_N0 + HC * B
O_EPS = O_M0 + B
O_END = O_EPS + 1
FCH = 4 + 2 * B
C_ID, C_ONE, C_MASK, C_MASKT, C_LATER, C_PLATER, C_BLK = range(7)
NCON = 7
CVW = 2 + T + 6
PXW = PREV + T + 1

U_IE = 0
U_OE = U_IE + 24
U_F = (U_OE + 8, 0)
U_IO = U_F[0] + 6 * FI
U_OO = U_IO + 20
U_F = (U_F[0], U_OO + 8)
U_END = U_F[1] + 6 * FI
T_N0, T_GE, T_IE = 0, 1, 2
T_OE = T_IE + 24
T_N1 = T_OE + 8
T_F0 = T_N1 + 1
T_N2 = T_F0 + 12 * FI
T_GO = T_N2 + 1
T_IO = T_GO + 1
T_P = [T_IO + 16 + x for x in (0, 1, 3, 5)]
T_PM = [T_IO + 16 + x for x in (2, 4, 6, 7)]
T_OO = T_IO + 24
T_N3 = T_OO + 8
T_F1 = T_N3 + 1
T_N4 = T_F1 + 12 * FI
T_F = (T_F0, T_F1)
T_N = (T_N0, T_N1, T_N2, T_N3, T_N4)
GAINS = (O_GMIX, O_GFFN, O_GMIX + ND, O_GFFN + ND, O_GFIN)
T_X = (None, T_OE, T_N2 - 8, T_OO, T_N4 - 8)


def after_unit(n_in, u0, t0):
    return {u0 + j: t0 + j for j in range(n_in)}


LAST_TILE = {**after_unit(24, U_IE, T_IE), **after_unit(8, U_OE, T_OE), **after_unit(20, U_IO, T_IO),
             **after_unit(8, U_OO, T_OO)}
for _j in range(4):
    LAST_TILE[U_IO + 16 + _j] = T_P[_j]


def last_tile(u):
    if u in LAST_TILE:
        return LAST_TILE[u]
    layer = int(u >= U_F[1])
    v, t = u - U_F[layer], T_F[layer]
    if v < 4:
        return t + v
    i, r = divmod(v - 4, 6)
    if i == FI - 1:
        return t + 12 * FI - 1
    return t + 4 + 12 * i + (r if r < 4 else 11)


def attention_order():
    order = [("n", 0)]
    for h in range(HB):
        for qb in range(NB):
            order.append(("s", h, qb))
            if qb == 5 and h + 1 < HB:
                order.append(("n", h + 1))
            if qb == 0 and h % 2 == 0 and h:
                order.append(("t", h // 2 - 1))
    order.append(("t", HB // 2 - 1))
    return order


ORDER = attention_order()
ROUNDS = []
for _k in range(HB * NB):
    ROUNDS.append((ROUNDS[-1] if ROUNDS else 0) + (_k % NB) // 4 + 1)
PT_ROUNDS = ROUNDS[-1]
PAR_LOADS = 5
ACT_OUTS = 8
K_PLAN = {u: (4 if u < 12 else 3) for u in range(5, 24)}


def wait(eng, sem, value):
    if not isinstance(value, int) or value > 0:
        eng.wait_ge(sem, value)


class Own:

    def __init__(self, eng, sem):
        self.eng, self.sem, self.n = eng, sem, 0

    def link(self, ins):
        ins.then_inc(self.sem, 1)
        self.n = self.n + 1
        self.eng.wait_ge(self.sem, self.n)

    def enter(self, i, per):
        self.base, self.per, self.n = self.n, per, i * per + self.n
        self.start, self.made = self.n, 0

    def leave(self, times):
        self.n = self.base + self.per * times


def trunk(nc, a, o):
    with ExitStack() as ctx:
        E = ctx.enter_context

        def sb(name, shape, dt=F32):
            return E(nc.sbuf_tensor(name, shape, dt))

        def sem(name):
            return E(nc.semaphore(name))

        XT = sb("XT", [P, ND, T])
        HHI = sb("HHI", [P, ND, T], F32R)
        HLO = sb("HLO", [P, ND, T], F32R)
        WHI = sb("WHI", [P, SLOTS, UNIT], F32R)
        WLO = sb("WLO", [P, SLOTS, UNIT], F32R)
        WRAW = sb("WRAW", [P, SLOTS, UNIT])
        VTOK = sb("VTOK", [P, NB, NW * P])
        KT = sb("KT", [P, NW, T])
        with nc.sbuf_tensor("QT", [P, NW, T], F32) as QT:
            pass
        HIDH = sb("HIDH", [P, 2, T], F32R)
        HIDL = sb("HIDL", [P, 2, T], F32R)
        SCR = sb("SCR", [P, B, PAGES, HB])
        QB = sb("QB", [P, 2, NW * P])
        GA = sb("GA", [HB, T])
        GB = sb("GB", [HB, T])
        PRM = sb("PRM", [P, O_END])
        FPRM = sb("FPRM", [P, NF, FCH])
        FPB = sb("FPB", [P, 2, FCH])
        FOUT = sb("FOUT", [P, NF, 2 + 2 * B])
        CON = sb("CON", [P, NCON, P])
        SELC = sb("SELC", [HB, NW, P])
        GWR = sb("GWR", [P, 2, ND, HB])
        GWH = sb("GWH", [P, 2, ND, HB], F32R)
        GWL = sb("GWL", [P, 2, ND, HB], F32R)
        PT = sb("PT", [1, B * PAGES], I32)
        PTI = sb("PTI", [P, 2], I32)
        TOT = sb("TOT", [P, 2, HB])
        KTMP = sb("KTMP", [P, PG, HB])
        MX = sb("MX", [P, B, HB])
        MXA = sb("MXA", [P, B, HB])
        RSS = sb("RSS", [P, B, HB])
        LSB = sb("LSB", [P, B, HB])
        SM = sb("SM", [P, 11, NW * B])
        VTS = sb("VTS", [P, NW, B])
        SROW = sb("SROW", [HB, NW * P])
        FMX = sb("FMX", [P, 4, 2])
        ACOL = sb("ACOL", [P, NB, HC])
        APV = sb("APV", [P, HC])
        WG = sb("WG", [P, 2])
        SROWS = sb("SROWS", [HC, 7, B])
        AS = sb("AS", [P, NW, B])
        SXS = sb("SXS", [P, B])
        PW = sb("PW", [P, NW, P])
        SBC = sb("SBC", [P, HC, 3, B])

        G = [E(nc.psum_tensor(f"G{s}", [P, BANKS, 512], F32)) for s in range(2)]
        M0 = E(nc.psum_tensor("M0", [P, 512], F32))
        M1 = E(nc.psum_tensor("M1", [P, 512], F32))

        XF = XT[:].rearrange("p c t -> p (c t)")
        KF = KT[:].rearrange("p c t -> p (c t)")
        VF = VTOK[:].rearrange("p c t -> p (c t)")
        GF = [g[:].rearrange("p a b -> p (a b)") for g in G]
        ident = CON[:, C_ID]
        ones = CON[:, C_ONE]
        RING = XF[:, 0:2 * PG * 512].rearrange("p (s g f) -> p s g f", s=2, g=PG)
        SQ = [KT[:, 0], KT[:, 1]]
        ACC, RSTD = KT[:, 2], KT[:, 3]
        HN = [QT[:, c] for c in range(4)]
        LG = VF[:, 0:2048].rearrange("p (s q h) -> p s q h", s=2, h=HB)
        LT = VF[:, 2048:4096].rearrange("p (s h g) -> p s h g", s=2, h=HB)
        TMP = [XT[:, 4], XT[:, 5]]
        CVX = XF[:, 6 * T:6 * T + CVW]
        NEGF = [XT[:, 4, 0:TP], XT[:, 7, 0:TP]]
        SC = [XT[:, 5], XT[:, 6]]
        PTS = [WRAW[:, 0], WRAW[:, 1]]
        OT = WRAW[:, 2].rearrange("p (q f) -> p q f", f=P)
        CV = [KF[:, 0:CVW], KF[:, CVW:2 * CVW]]
        CC = [KF[:, 2 * CVW:2 * CVW + T], VF[:, 2 * T:3 * T]]
        HR = [VF[:, 0:T], VF[:, T:2 * T]]
        PX = XF[:, 0:PXW]
        PD = [XF[:, PXW:2 * PXW], XF[:, 2 * PXW:3 * PXW]]
        SX = XF[:, 3 * PXW:3 * PXW + B * 16].rearrange("p (b r) -> p b r", r=16)
        PZ = [XT[:, 6], XT[:, 7]]
        C0 = XF[:, 0:HC * B * DK].rearrange("p (s e) -> p s e", e=DK)
        VB = XF[:, NW * T:NW * T + B * 512].rearrange("p (b f) -> p b f", b=B)
        AROW, MROW = GA[0:HC, 0:TP], GB[0:HC, 0:TP]
        TROW = SCR[:].rearrange("p b g h -> p (b g h)")[0:HC, 0:T]
        MAXROW = TROW[:, 0:TP]
        SPOOL = SCR[:].rearrange("p b g h -> p (b g h)")[:, 1548:1548 + NW * B * PREV].rearrange(
            "p (c b r) -> p c b r", c=NW, b=B)
        CST = SCR[:].rearrange("p b g h -> p (b g h)")[:, T:T + HC * (DK + 1)].rearrange(
            "p (h e) -> p h e", h=HC)
        BROW = QB[:].rearrange("p s f -> p (s f)")[0:HC, 0:TP]
        XA = [WRAW[:, 0, 0:512], WRAW[:, 0, 512:1024]]
        XW = [WRAW[:, 1, 0:512], WRAW[:, 1, 512:1024]]
        XE = [WRAW[:, 2, 0:512], WRAW[:, 2, 512:1024]]
        HCT = XT[:, 4:8]

        def psum_tile(t, rows=P):
            return G[t % 2][0:rows, :, 0:TC]

        def by3(x):
            return x.rearrange("p (b t) -> p b t", b=BANKS)

        def freed(t):
            return t // 2 + 1

        x_in = sem("x_in")
        par_in = sem("par_in")
        pages_in = sem("pages_in")
        fpar_in = sem("fpar_in")
        kv_loaded = [sem(f"kv_loaded{s}") for s in range(2)]
        qrow_sbuf = sem("qrow_sbuf")
        row_dram = sem("row_dram")
        qb_loaded = sem("qb_loaded")
        h_raw = sem("h_raw")
        k_red = sem("k_red")
        v_used = sem("v_used")
        p_ready = sem("p_ready")
        pt_psum = sem("pt_psum")
        fout_ready = sem("fout_ready")
        outs = sem("outs")
        fpb_ready = sem("fpb_ready")
        x_saved = sem("x_saved")
        spool_in = sem("spool_in")
        tile_free = [sem(f"tile_free{s}") for s in range(2)]
        gmoved = sem("gmoved")
        vrow_sbuf = sem("vrow_sbuf")
        tmp_out = [sem(f"tmp_out{s}") for s in range(2)]
        c0_in = sem("c0_in")
        vb_in = sem("vb_in")
        c_new = sem("c_new")
        c_out = sem("c_out")
        snum_psum = sem("snum_psum")
        og_in = sem("og_in")
        cst_ready = sem("cst_ready")
        y_psum = sem("y_psum")
        pool_back = sem("pool_back")
        hc_lo = sem("hc_lo")
        y_ready = sem("y_ready")
        act_outs = sem("act_outs")
        fconv_out = sem("fconv_out")
        pool_out = sem("pool_out")
        w_lo = sem("w_lo")
        tile_done = sem("tile_done")
        h_lo_dve = sem("h_lo_dve")
        h_lo_pool = sem("h_lo_pool")
        sq_summed = sem("sq_summed")
        gw_lo = sem("gw_lo")
        vt_sbuf = sem("vt_sbuf")
        vt_psum = sem("vt_psum")
        logf_in = sem("logf_in")
        lt_sbuf = sem("lt_sbuf")
        lt_psum = sem("lt_psum")
        tot_ready = sem("tot_ready")
        bias_sbuf = sem("bias_sbuf")
        bias_psum = sem("bias_psum")
        qrow_psum = sem("qrow_psum")
        sprob = sem("sprob")
        s_done = sem("s_done")
        pt_sbuf = sem("pt_sbuf")
        o_sbuf = sem("o_sbuf")
        o_done = sem("o_done")
        fcum_ready = sem("fcum_ready")
        s_free = [sem(f"s_free{s}") for s in range(2)]
        ssum = sem("ssum")
        qk_new = sem("qk_new")
        fin_psum = sem("fin_psum")
        back_lo = sem("back_lo")
        sfeat = sem("sfeat")
        hid_lo = sem("hid_lo")
        arow_ready = sem("arow_ready")
        acol_psum = sem("acol_psum")
        acol_ready = sem("acol_ready")
        vts_ready = sem("vts_ready")
        vrow_psum = sem("vrow_psum")
        pz_ready = sem("pz_ready")
        srows_ready = sem("srows_ready")
        srows_psum = sem("srows_psum")
        sbc_ready = sem("sbc_ready")
        qn_ready = sem("qn_ready")
        mrow_ready = sem("mrow_ready")
        xa_sbuf = sem("xa_sbuf")
        xa_psum = sem("xa_psum")
        hc_ready = sem("hc_ready")
        kw_ready = sem("kw_ready")
        own_act = sem("own_act")
        w_loaded = [sem(f"w_loaded{s}") for s in range(SLOTS)]
        w_hi = sem("w_hi")
        sq_ready = sem("sq_ready")
        h_hi = sem("h_hi")
        gw_hi = sem("gw_hi")
        logsig_in = sem("logsig_in")
        a_saved = sem("a_saved")
        logf_ready = sem("logf_ready")
        fout_conv = sem("fout_conv")
        sshift = sem("sshift")
        sc_ready = sem("sc_ready")
        att_hi = sem("att_hi")
        back_in = [sem(f"back_in{s}") for s in range(NW)]
        back_hi = sem("back_hi")
        fin_args = sem("fin_args")
        fin_exp = sem("fin_exp")
        fin_att = sem("fin_att")
        fin_hi = sem("fin_hi")
        conv_done = sem("conv_done")
        silu_done = sem("silu_done")
        hid_hi = sem("hid_hi")
        px_zero = sem("px_zero")
        px_ready = sem("px_ready")
        sx_ready = sem("sx_ready")
        sgate_args = sem("sgate_args")
        wm_ready = sem("wm_ready")
        w_exp = sem("w_exp")
        den_abs = sem("den_abs")
        apv_ready = sem("apv_ready")
        hc_gated = sem("hc_gated")
        hc_hi = sem("hc_hi")
        own_dve = sem("own_dve")
        k_mul = sem("k_mul")
        cvx_zero = sem("cvx_zero")
        smax_ready = sem("smax_ready")
        smax_all = sem("smax_all")
        cv_zero = sem("cv_zero")
        hcs_ready = sem("hcs_ready")
        pages_in_pool = sem("pages_in_pool")

        block = E(nc.Block())

        @block.sync
        def _(sp):
            sp.dma_start(XT[:, :, 0:TP], a["xp"]).then_inc(x_in, 16)
            sp.dma_start(XT[:, :, TP:T], a["xs"]).then_inc(x_in, 16)
            sp.dma_start(CON[:], a["con"]).then_inc(par_in, 16)
            sp.dma_start(PT[:], a["pt"]).then_inc(pages_in, 16)
            sp.dma_start(GWR[:], a["gw"]).then_inc(par_in, 16)
            sp.dma_start(PRM[:], a["prm"]).then_inc(par_in, 16)
            sp.dma_start(SELC[:], a["selc"]).then_inc(par_in, 16)
            sp.dma_start(PW[:], a["pw"]).then_inc(par_in, 16)
            sp.dma_start(FPRM[:], a["fprm"][0]).then_inc(fpar_in, 16)

            def bcast_row(t, row):
                return t[bass.ds(row, 1), :].to_broadcast([P, NW * P])

            def kv_load(cache, g, slot, used, value):
                for j in range(PG):
                    page = sp.value_load(PT[0:1, bass.ds(g * PG + j, 1)], min_val=0, max_val=cache.shape[0] - 1)
                    if j == 0:
                        wait(sp, used, value)
                    sp.dma_start(RING[:, slot, j], cache[bass.ds(page, 1)].rearrange("a p f -> (a p) f")
                                 ).then_inc(kv_loaded[slot], 16)

            sp.wait_ge(qrow_sbuf, 1)
            sp.dma_start(o["q_scr"], SROW[:]).then_inc(row_dram, 16)
            sp.wait_ge(row_dram, 16)
            sp.dma_start(QB[:, 0], bcast_row(o["q_scr"], 0)).then_inc(qb_loaded, 16)
            sp.wait_ge(h_raw, ND)
            sp.wait_ge(pages_in, 16)

            def keys(g0, first, last):
                for g in range(16):
                    for at, n in ((2, 1), (10, 2)):
                        if g == at and not (last and n == 2):
                            b = g0 // 8 + n if first else None
                            if first:
                                sp.wait_ge(qb_loaded, b * 16)
                                row = b
                            else:
                                row = sp.snap(g0[1] + n)
                                sp.wait_ge(qb_loaded, g0[1] * 16 + n * 16)
                            sp.dma_start(QB[:, n % 2], bcast_row(o["q_scr"], row)).then_inc(qb_loaded, 16)
                    gg = g0 + g if first else g0[0] + g
                    kv_load(a["ck"], gg, g % 2, k_red, gg - 1 if first else g0[0] + (g - 1))

            keys(0, True, False)
            with sp.Fori(1, B // 2 - 1) as i:
                keys((i * 16, i * 2), False, False)
            keys(GROUPS - 16, True, True)

            for g in range(8):
                kv_load(a["cv"], g, g % 2, *((k_red, GROUPS - 1 + g) if g < 2 else (v_used, g - 1)))
            with sp.Fori(1, B) as b:
                for g in range(8):
                    kv_load(a["cv"], b * 8 + g, g % 2, v_used, b * 8 + (g - 1))

            sp.wait_ge(v_used, GROUPS)
            sp.wait_ge(p_ready, HB * NB)
            sp.wait_ge(pt_psum, PT_ROUNDS)
            sp.dma_start(XT[:, :, 0:TP], a["xp"]).then_inc(x_in, 16)
            sp.dma_start(XT[:, :, TP:T], a["xs"]).then_inc(x_in, 16)

            sp.wait_ge(fout_ready, NF)
            sp.dma_start(o["ffn"][0], FOUT[:]).then_inc(outs, 16)
            sp.wait_ge(fpb_ready, FI)
            sp.dma_start(FPRM[:], a["fprm"][1]).then_inc(fpar_in, 16)

            sp.wait_ge(h_raw, 3 * ND)
            sp.dma_start(o["x_scr"], XT[:]).then_inc(x_saved, 16)
            sp.dma_start(SPOOL, a["spool"]).then_inc(spool_in, 16)
            sp.wait_ge(tile_free[T_GO % 2], freed(T_GO))
            sp.dma_start(GB[0:HC, :], GA[HC:2 * HC, :]).then_inc(gmoved, 16)
            sp.wait_ge(vrow_sbuf, 1)
            sp.dma_start(o["v_scr"], SROW[:]).then_inc(row_dram, 16)
            sp.wait_ge(row_dram, 32)
            for s in range(2):
                sp.wait_ge(tmp_out[s], 96)
            sp.wait_ge(tile_free[T_PM[3] % 2], freed(T_PM[3]))
            sp.dma_start(C0, a["c0"]).then_inc(c0_in, 16)
            for b in range(B):
                sp.dma_start(VB[:, b], bcast_row(o["v_scr"], b)).then_inc(vb_in, 16)
            sp.wait_ge(c_new, HC * B)
            sp.dma_start(o["c_s"], C0).then_inc(c_out, 16)
            sp.wait_ge(c_out, 16)
            sp.wait_ge(snum_psum, 1)
            for s in range(2):
                sp.wait_ge(tmp_out[s], 64)
            sp.dma_start(XT[:, 0:NW], o["o_scr"].rearrange("c p t -> p c t")).then_inc(og_in, 16)
            sp.wait_ge(cst_ready, HC * NB)
            sp.dma_start(o["c_p"], CST).then_inc(outs, 16)
            sp.wait_ge(y_psum, HC * NB)
            sp.dma_start(QT[:], o["p_scr"].rearrange("c p t -> p c t")).then_inc(pool_back, 16)
            sp.wait_ge(hc_lo, NW)
            sp.wait_ge(x_saved, 16)
            sp.dma_start(XT[:], o["x_scr"]).then_inc(x_in, 16)

            sp.wait_ge(fout_ready, 2 * NF)
            sp.dma_start(o["ffn"][1], FOUT[:]).then_inc(outs, 16)
            for c in range(ND):
                sp.wait_ge(y_ready, c + 1)
                sp.dma_start(o["y"][c], XT[:, c]).then_inc(outs, 16)
            sp.wait_ge(outs, 16 * (3 + ND))
            sp.wait_ge(act_outs, 16 * ACT_OUTS)
            sp.wait_ge(fconv_out, 16)
            sp.wait_ge(pool_out, 32 * NW)

        @block.tensor
        def _(pe):
            def passes(out, whi, wlo, xhi, xlo, first, last):
                for n, (w, x) in enumerate(((whi, xhi), (whi, xlo), (wlo, xhi))):
                    for c in range(BANKS):
                        mm = pe.matmul(out[:, c], w, x[:, c * TC:(c + 1) * TC], start=first and n == 0,
                                       stop=last and n == 2)
                return mm

            def unit(u, t, free, lo, ready=None):
                slot = u % SLOTS
                pe.wait_ge(w_lo, lo)
                wait(pe, tile_free[t % 2], free)
                for k in range(ND):
                    if ready:
                        ready(k)
                    mm = passes(psum_tile(t), WHI[:, slot, k * P:(k + 1) * P], WLO[:, slot, k * P:(k + 1) * P],
                                HHI[:, k], HLO[:, k], k == 0, k == ND - 1)
                mm.then_inc(tile_done, 1)

            def plain_unit(u, t, ready=None):
                unit(u, t, t // 2, u + 1, ready)

            def normed(n):
                def ready(k):
                    pe.wait_ge((h_lo_dve, h_lo_pool)[k % 2], n * (ND // 2) + k // 2 + 1)
                return ready

            def norm(n):
                t = T_N[n]
                pe.wait_ge(sq_summed, (n + 1) * (ND - 1))
                wait(pe, tile_free[t % 2], t // 2)
                for c in range(BANKS):
                    mm = pe.matmul(psum_tile(t)[:, c], ones, ACC[:, c * TC:(c + 1) * TC], start=True, stop=True)
                mm.then_inc(tile_done, 1)

            def gates(layer, t, n):
                pe.wait_ge(gw_lo, 1)
                pe.wait_ge(tile_free[t % 2], t // 2)
                for k in range(ND):
                    normed(n)(k)
                    mm = passes(psum_tile(t, HB), GWH[:, layer, k], GWL[:, layer, k], HHI[:, k], HLO[:, k],
                                k == 0, k == ND - 1)
                mm.then_inc(tile_done, 1)

            def values_turned(j, layer):
                t = (T_IE if layer == 0 else T_IO) + 8 + j
                pe.wait_ge(tile_free[t % 2], freed(t))
                for r in range(2):
                    n = (layer * NW + j) * 2 + r
                    wait(pe, vt_sbuf, n)
                    for q in range(4):
                        mm = pe.transpose(M0[:, q * P:(q + 1) * P], TMP[j % 2][:, (r * 4 + q) * P:(r * 4 + q + 1) * P],
                                          ident)
                    mm.then_inc(vt_psum, 1)

            pe.wait_ge(par_in, 16 * PAR_LOADS)
            pe.wait_ge(logf_in, 32)
            for r in range(4):
                half, hq = r // 2, r % 2
                wait(pe, lt_sbuf, r)
                for q in range(4):
                    mm = pe.transpose(M0[:, q * P:(q + 1) * P], LG[:, half, :, hq * 4 + q], ident)
                mm.then_inc(lt_psum, 1)
            pe.wait_ge(tot_ready, 1)
            for r in range(4):
                half, hq = r // 2, r % 2
                pe.wait_ge(lt_sbuf, r + 1)
                wait(pe, bias_sbuf, r)
                for q in range(4):
                    h = hq * 4 + q
                    dst = M1[:, q * P:(q + 1) * P]
                    pe.matmul(dst, CON[:, C_LATER], LT[:, half, h], start=True, stop=False)
                    mm = pe.matmul(dst, TOT[:, half, h:h + 1].to_broadcast([P, P]), CON[:, C_PLATER],
                                   start=False, stop=True)
                mm.then_inc(bias_psum, 1)

            norm(0)
            gates(0, T_GE, 0)
            for u in range(24):
                plain_unit(U_IE + u, T_IE + u, normed(0) if u == 0 else None)
                if u == 4:
                    pe.wait_ge(lt_sbuf, 4)
                    for s in range(2):
                        pe.wait_ge(tile_free[s], freed(T_IE + 2 + s))
                    for j in range(NW):
                        mm = pe.transpose(M0[0:B, j * P:(j + 1) * P], QT[:, j, TP:T], ident)
                    mm.then_inc(qrow_psum, 1)
                    pe.wait_ge(qrow_sbuf, 1)
                if 9 <= u <= 12:
                    values_turned(u - 9, 0)

            def value_group(g):
                b, slot = g // 8, g % 2
                pe.wait_ge(kv_loaded[slot], 16 * PG * (GROUPS // 2 + g // 2 + 1))
                if g == 0:
                    pe.wait_ge(sprob, 1)
                    pe.wait_ge(bias_sbuf, 4)
                for j in range(PG):
                    page = (g % 8) * PG + j
                    for c in range(NW):
                        mm = pe.matmul(M1[:, (b * NW + c) * 2:(b * NW + c) * 2 + 2], RING[:, slot, j, c * P:(c + 1) * P],
                                       SCR[:, b, page, 2 * c:2 * c + 2], start=(g == 0 and j == 0 and c == 0),
                                       stop=True, skip_group_check=True)
                mm.then_inc(v_used, 1)

            def scores(x, h, qb):
                rows = slice(HD * (h % 2), HD * (h % 2) + HD)
                n = (qb + 1) * P
                for c0 in range(0, n, 512):
                    c1 = min(n, c0 + 512)
                    pe.matmul(GF[x % 2][:, c0:c1], QT[rows, h // 2, qb * P:(qb + 1) * P], KT[rows, h // 2, c0:c1],
                              start=True, stop=c1 < n)
                pe.matmul(GF[x % 2][:, n - P:n], ident, CON[:, C_MASK], start=False, stop=True).then_inc(s_done, 1)

            rounds = [0]

            def results(h, qb, k):
                pe.wait_ge(p_ready, k + 1)
                for r in range(qb // 4 + 1):
                    n = rounds[0]
                    wait(pe, pt_sbuf, n - 1)
                    for q in range(r * 4, min(r * 4 + 4, qb + 1)):
                        mm = pe.transpose(G[n % 2][:, 2, (q % 4) * P:(q % 4 + 1) * P], SC[k % 2][:, q * P:(q + 1) * P],
                                          ident)
                    mm.then_inc(pt_psum, 1)
                    rounds[0] = n + 1
                value_group(k)
                pe.wait_ge(pt_sbuf, rounds[0])
                wait(pe, o_sbuf, k)
                for q in range(qb + 1):
                    mm = pe.matmul(M0[:, 0:HD], PTS[k % 2][:, q * P:(q + 1) * P], VTOK[:, q, h * HD:(h + 1) * HD],
                                   start=q == 0, stop=q == qb)
                mm.then_inc(o_done, 1)

            pe.wait_ge(vt_sbuf, 2 * NW)
            pe.wait_ge(fcum_ready, 1)
            for s in range(2):
                pe.wait_ge(tile_free[s], (T_OE + 1 - s) // 2)
            before = None
            for x, item in enumerate(ORDER + [None]):
                if item:
                    wait(pe, s_free[x % 2], x // 2)
                if item and item[0] == "n":
                    for c0 in (0, 512):
                        mm = pe.matmul(GF[x % 2][:, c0:c0 + 512], ident[0:HB, item[1]:item[1] + 1].to_broadcast([HB, P]),
                                       GB[:, c0:c0 + 512], start=True, stop=True)
                    mm.then_inc(s_done, 1)
                    continue
                elif item and item[0] == "s":
                    scores(x, item[1], item[2])
                elif item:
                    j = item[1]
                    if x == len(ORDER) - 1:
                        results(*before)
                        before = None
                    pe.wait_ge(o_sbuf, (2 * j + 2) * NB)
                    for qb in range(NB):
                        mm = pe.transpose(GF[x % 2][:, qb * P:(qb + 1) * P], OT[:, qb], ident)
                    mm.then_inc(s_done, 1)
                    continue
                if before:
                    results(*before)
                    before = None
                if item and item[0] == "s":
                    before = (item[1], item[2], item[1] * NB + item[2])

            pe.wait_ge(ssum, 1)
            pe.wait_ge(qk_new, 1)
            pe.matmul(M0[:, 0:B * HB], ones, RSS[:].rearrange("p b h -> p (b h)"), start=True, stop=True)
            pe.matmul(M0[:, 64:96], CON[:, C_BLK], SM[:, 0], start=True, stop=True)
            for c in range(NW):
                mm = pe.matmul(M0[:, 96 + c * B:96 + (c + 1) * B], SELC[:, c], GA[:, TP:T], start=True, stop=True)
            mm.then_inc(fin_psum, 1)

            pe.wait_ge(back_lo, NW + 1)
            pe.wait_ge(sfeat, 1)
            for s in range(2):
                pe.wait_ge(s_free[s], (len(ORDER) + 1 - s) // 2)
            for m in range(ND):
                plain_unit(U_OE + m, T_OE + m)

            def mlp(layer):
                tb, ub = T_F[layer], U_F[layer]
                norm(2 * layer + 1)

                def down(t, u, plus, hid):
                    pe.wait_ge(hid_lo, hid)
                    for m in range(ND):
                        tt = t + m
                        pe.wait_ge(tile_free[tt % 2], plus(tt // 2))
                        for jj in range(2):
                            slot = (u + jj) % SLOTS
                            mm = passes(psum_tile(tt), WHI[:, slot, m * P:(m + 1) * P], WLO[:, slot, m * P:(m + 1) * P],
                                        HIDH[:, jj], HIDL[:, jj], jj == 0, jj == 1)
                        mm.then_inc(tile_done, 1)

                for r in range(4):
                    plain_unit(ub + r, tb + r, normed(2 * layer + 1) if r == 0 else None)
                with pe.Fori(0, FI - 1) as i:
                    for r in range(4):
                        t = tb + 4 + r
                        unit(ub + 4 + r, t, i * 6 + t // 2, i * 6 + (ub + 4 + r + 1))
                    pe.wait_ge(w_lo, i * 6 + (ub + 10))
                    down(tb + 8, ub + 8, lambda v: i * 6 + v, i * 2 + (layer * NF + 2))
                pe.wait_ge(w_lo, ub + 6 * FI)
                down(tb + 12 * FI - 8, ub + 6 * FI - 2, lambda v: v, (layer + 1) * NF)

            mlp(0)

            norm(2)
            gates(1, T_GO, 2)
            for u in range(20):
                t = T_IO + u if u < 16 else T_P[u - 16]
                plain_unit(U_IO + u, t)
                if u == 4:
                    pe.wait_ge(arow_ready, 1)
                    pe.wait_ge(sfeat, 1)
                    for ch in range(NB):
                        mm = pe.transpose(M0[:, ch * HC:(ch + 1) * HC], AROW[:, ch * P:(ch + 1) * P], ident[0:HC, 0:HC])
                    mm.then_inc(acol_psum, 1)
                    pe.wait_ge(acol_ready, 1)
                if 9 <= u <= 12:
                    values_turned(u - 9, 1)
                if u == 13:
                    pe.wait_ge(vt_sbuf, 4 * NW)
                    pe.wait_ge(vts_ready, 2 * NW)
                    for j in range(NW):
                        mm = pe.transpose(M0[0:B, j * P:(j + 1) * P], VTS[:, j], ident)
                    mm.then_inc(vrow_psum, 1)
                if u >= 17:
                    for g in ([u - 17] if u < 19 else [2, 3]):
                        t = T_PM[g]
                        pe.wait_ge(pz_ready, g + 1)
                        pe.wait_ge(tile_free[t % 2], t // 2)
                        for c in range(BANKS):
                            mm = pe.matmul(psum_tile(t)[:, c], PW[:, g], PZ[g % 2][:, c * TC:(c + 1) * TC],
                                           start=True, stop=True)
                        mm.then_inc(tile_done, 1)

            pe.wait_ge(vrow_sbuf, 1)
            pe.wait_ge(srows_ready, 1)
            for h in range(HC):
                mm = pe.matmul(M0[:, h * 3 * B:(h + 1) * 3 * B], ident[0:HC, h:h + 1].to_broadcast([HC, P]),
                               SROWS[:].rearrange("p k b -> p (k b)")[:, 0:3 * B], start=True, stop=True)
            mm.then_inc(srows_psum, 1)
            pe.wait_ge(sbc_ready, 1)
            pe.wait_ge(c_new, HC * B)
            pe.wait_ge(qn_ready, 1)
            pe.matmul(M0[:, 128:128 + HC * B], ones, SM[:, 2], start=True, stop=True)
            for s in range(HC * B):
                b, h = s // HC, s % HC
                mm = pe.matmul(M0[:, 192 + h * B + b:193 + h * B + b], C0[:, s], QT[:, h, TP + b:TP + b + 1],
                               start=True, stop=True)
            mm.then_inc(snum_psum, 1)

            for s in range(2):
                pe.wait_ge(tile_free[s], (T_OO + 1 - s) // 2)
            pe.wait_ge(mrow_ready, 1)

            def chunk_in(i):
                ch, h = divmod(i, HC)
                cols = slice(ch * P, (ch + 1) * P)
                wait(pe, xa_sbuf, i - 1)
                x = G[i % 2][:, 0]
                sel = ident[0:HC, h:h + 1].to_broadcast([HC, P])
                pe.matmul(x[:, 0:P], sel, MAXROW[:, cols], start=True, stop=True)
                pe.matmul(x[:, P:2 * P], sel, MROW[:, cols], start=True, stop=True)
                pe.matmul(x[:, 2 * P:3 * P], KT[:, h, cols], QT[:, h, cols], start=True, stop=True)
                pe.transpose(x[:, 3 * P:4 * P], KT[:, h, cols], ident).then_inc(xa_psum, 1)

            def chunk_out(i):
                ch, h = divmod(i, HC)
                y = G[i % 2][:, 1]
                v = VTOK[:, ch, h * DK:(h + 1) * DK]
                w = XW[i % 2]
                wait(pe, cst_ready, i - 3)
                wait(pe, hc_ready, i - 1)
                wait(pe, cst_ready, i - 1)
                pe.wait_ge(kw_ready, i + 1)
                pe.matmul(y[:, 0:P], v, w[:, P:2 * P], start=True, stop=False)
                pe.matmul(y[:, 0:P], CST[:, h, 0:DK], w[:, 2 * P:3 * P], start=False, stop=True)
                pe.matmul(y[:, P:2 * P], ones, w[:, P:2 * P], start=True, stop=False)
                pe.matmul(y[:, P:2 * P], CST[:, h, DK:DK + 1].to_broadcast([P, P]), w[:, 2 * P:3 * P],
                          start=False, stop=True)
                pe.matmul(y[:, 2 * P:3 * P], w[:, 3 * P:4 * P], v, start=True, stop=True)
                pe.matmul(y[:, 3 * P:3 * P + 1], w[:, 3 * P:4 * P], ones[:, 0:1], start=True, stop=True
                          ).then_inc(y_psum, 1)

            chunk_in(0)
            for i in range(HC * NB):
                if i + 1 < HC * NB:
                    chunk_in(i + 1)
                chunk_out(i)

            pe.wait_ge(hc_lo, NW)
            pe.wait_ge(back_lo, 2 * NW + 1)
            pe.wait_ge(hc_ready, HC * NB)
            pe.wait_ge(cst_ready, HC * NB)
            for m in range(ND):
                plain_unit(U_OO + m, T_OO + m)

            mlp(1)
            norm(4)

        @block.scalar
        def _(act):
            own = Own(act, own_act)
            A = nc.scalar.activation

            def load(u):
                if u < U_END:
                    wait(act, w_lo, u - SLOTS + 1)
                    act.dma_start(WRAW[:, u % SLOTS], a["w"][u]).then_inc(w_loaded[u % SLOTS], 16)

            def load_at(u, i):
                act.wait_ge(w_lo, i * 6 + (u - SLOTS + 1))
                act.dma_start(WRAW[:, u % SLOTS], a["w"][bass.ds(i * 6 + u, 1)].rearrange("a p f -> (a p) f")
                              ).then_inc(w_loaded[u % SLOTS], 16)

            def high(u):
                if u < U_END:
                    act.wait_ge(w_loaded[u % SLOTS], 16 * (u // SLOTS + 1))
                    if u >= SLOTS:
                        act.wait_ge(tile_done, last_tile(u - SLOTS) + 1)
                    A(WHI[:, u % SLOTS], WRAW[:, u % SLOTS], ACT.Copy).then_inc(w_hi, 1)

            def unit_used(u, deferred=()):
                high(u + SLOTS)
                if u + 5 not in deferred:
                    load(u + 5)

            def evacuate(out, t, func=ACT.Copy, rows=P, **kw):
                act.wait_ge(tile_done, t + 1)
                A(by3(out), psum_tile(t, rows), func, **kw).then_inc(tile_free[t % 2], 1)
                act.wait_ge(tile_free[t % 2], freed(t))

            def norm(n, halves=True):
                t = T_N[n]
                for c in range(ND):
                    if n == 0:
                        act.wait_ge(x_in, 32)
                    else:
                        act.wait_ge(tile_free[(T_X[n] + c) % 2], freed(T_X[n] + c))
                    if c >= 3:
                        act.wait_ge(sq_summed, n * (ND - 1) + c - 2)
                    A(ACC if c == 0 else SQ[c % 2], XT[:, c], ACT.Square).then_inc(sq_ready, 1)
                act.wait_ge(tile_done, t + 1)
                A(by3(RSTD), psum_tile(t), ACT.Sqrt, bias=PRM[:, O_EPS:O_EPS + 1], scale=1.0 / D).then_inc(tile_free[t % 2], 1)
                if halves:
                    for c in range(ND):
                        act.wait_ge(h_raw, n * ND + c + 1)
                        A(HHI[:, c], HN[c % 4], ACT.Copy).then_inc(h_hi, 1)

            def values_turned(j, layer):
                for r in range(2):
                    n = (layer * NW + j) * 2 + r
                    act.wait_ge(vt_psum, n + 1)
                    A(VTOK[:, r * 4:r * 4 + 4, j * P:(j + 1) * P], M0[:].rearrange("p (q f) -> p q f", f=P),
                      ACT.Copy).then_inc(vt_sbuf, 1)

            for u in range(SLOTS):
                load(u)
            act.wait_ge(par_in, 16 * PAR_LOADS)
            A(GWH[:], GWR[:], ACT.Copy).then_inc(gw_hi, 1)
            for u in range(SLOTS):
                high(u)
            for u in range(SLOTS, 5):
                load(u)

            for r in range(4):
                half, hq = r // 2, r % 2
                act.wait_ge(lt_psum, r + 1)
                A(LT[:, half, hq * 4:hq * 4 + 4], M0[:].rearrange("p (h g) -> p h g", g=P), ACT.Copy).then_inc(lt_sbuf, 1)
            for r in range(4):
                half, hq = r // 2, r % 2
                act.wait_ge(bias_psum, r + 1)
                A(SCR[:, half * 4:half * 4 + 4, :, hq * 4:hq * 4 + 4].rearrange("p b g h -> p h (b g)"),
                  M1[:].rearrange("p (h g) -> p h g", g=P), ACT.Copy).then_inc(bias_sbuf, 1)

            norm(0)
            t = T_GE
            act.wait_ge(tile_done, t + 1)
            A(by3(GA[:]), psum_tile(t, HB), ACT.Identity, bias=PRM[0:HB, O_GB:O_GB + 1]).then_inc(tile_free[t % 2], 1)
            act.wait_ge(tile_free[t % 2], freed(t))

            def log_sigmoid(z, out):
                own.link(A(out, z, ACT.Abs))
                own.link(A(out, out, ACT.Exp, scale=-1.0))
                A(out, out, ACT.Ln, bias=ones[0:z.shape[0], 0:1]).then_inc(logsig_in, 1)

            log_sigmoid(GA[:], GB[:])

            def store_tmp(s, dst, done):
                act.dma_start(dst, TMP[s]).then_inc(done, 16)

            for u in range(24):
                t, j = T_IE + u, u % 4
                if u < 4:
                    evacuate(QT[:, j], t, scale=HD ** -0.5)
                elif u < 8:
                    evacuate(KT[:, j], t)
                    act.dma_start(o["k"][j], KT[:, j]).then_inc(act_outs, 16)
                elif u < 12:
                    if j >= 2:
                        act.wait_ge(tmp_out[j % 2], 16)
                    evacuate(TMP[j % 2], t)
                    A(VTS[:, j], TMP[j % 2][:, TP:T], ACT.Copy).then_inc(vts_ready, 1)
                    act.dma_start(o["v"][j], TMP[j % 2]).then_inc(tmp_out[j % 2], 16)
                elif (u - 12) % 3 == 0:
                    jc = (u - 12) // 3
                    if jc == 0:
                        act.wait_ge(tmp_out[0], 32)
                    else:
                        act.wait_ge(tile_free[(t - 2) % 2], freed(t - 2))
                    evacuate(TMP[0], t)
                elif (u - 12) % 3 == 2:
                    jc = (u - 12) // 3
                    act.wait_ge(tile_free[t % 2], freed(t))
                    act.dma_start(o["a_scr"][jc], TMP[1]).then_inc(a_saved, 16)
                if u == 4:
                    act.wait_ge(qrow_psum, 1)
                    A(SROW[:], M0[0:B], ACT.Copy).then_inc(qrow_sbuf, 1)
                unit_used(U_IE + u, deferred=(U_OE + 3, U_OE + 4))
                if 9 <= u <= 12:
                    values_turned(u - 9, 0)
                if u == 5:
                    act.wait_ge(logf_ready, 1)
                    act.dma_start(o["logf"], GA[:]).then_inc(act_outs, 16)
            act.wait_ge(fout_conv, NW)
            act.dma_start(o["conv_a"], FOUT[:, 0:NW]).then_inc(fconv_out, 16)

            act.wait_ge(sshift, 1)
            flat = SCR[:].rearrange("p b g h -> p (b g h)")
            A(flat, flat, ACT.Exp).then_inc(sprob, 1)

            rounds = [0]
            act.wait_ge(w_lo, U_OE + SLOTS)

            def turned(h, qb, k):
                for r in range(qb // 4 + 1):
                    n = rounds[0]
                    w = min(4, qb + 1 - 4 * r) * P
                    act.wait_ge(pt_psum, n + 1)
                    wait(act, o_done, k - 1)
                    A(PTS[k % 2][:, r * 512:r * 512 + w], G[n % 2][:, 2, 0:w], ACT.Copy).then_inc(pt_sbuf, 1)
                    rounds[0] = n + 1

            before = None
            for x, item in enumerate(ORDER):
                if item[0] == "n":
                    h = item[1]
                    wait(act, sc_ready, NB * (h - 1))
                    act.wait_ge(s_done, x + 1)
                    A(NEGF[h % 2], GF[x % 2][:, 0:TP], ACT.Copy).then_inc(s_free[x % 2], 1)
                    continue
                if item[0] == "s":
                    k = item[1] * NB + item[2]
                    n = (item[2] + 1) * P
                    act.wait_ge(sc_ready, k + 1)
                    wait(act, o_sbuf, k - 1)
                    A(SC[k % 2][:, 0:n], SC[k % 2][:, 0:n], ACT.Exp, bias=FMX[:, 1, k % 2:k % 2 + 1],
                      accum_out=FMX[:, 2, k % 2:k % 2 + 1]).then_inc(p_ready, 1)
                    if before:
                        turned(*before)
                    before = (item[1], item[2], k)
                    continue
                j = item[1]
                if x == len(ORDER) - 1:
                    turned(*before)
                act.wait_ge(s_done, x + 1)
                A(HHI[:, NW + j, 0:TP], GF[x % 2][:, 0:TP], ACT.Copy).then_inc(att_hi, 1)
                act.wait_ge(a_saved, 16 * NW)
                act.dma_start(QT[:, j, 0:TP], o["a_scr"][j][:, 0:TP]).then_inc(back_in[j], 16)
                act.dma_start(AS[:, j], o["a_scr"][j][:, TP:T]).then_inc(back_in[j], 16)
                if j:
                    act.wait_ge(back_in[j - 1], 32)
                    A(HHI[:, j - 1, 0:TP], QT[:, j - 1, 0:TP], ACT.Copy).then_inc(back_hi, 1)
            act.wait_ge(back_in[NW - 1], 32)
            A(HHI[:, NW - 1, 0:TP], QT[:, NW - 1, 0:TP], ACT.Copy).then_inc(back_hi, 1)
            A(HHI[:, 0:NW, TP:T], AS[:], ACT.Copy).then_inc(back_hi, 1)
            act.wait_ge(o_done, HB * NB)
            act.wait_ge(att_hi, NW)
            load(U_OE + 3)
            load(U_OE + 4)

            act.wait_ge(fin_args, 1)
            A(SM[:, 6:8].rearrange("p k f -> p (k f)"), SM[:, 4:6].rearrange("p k f -> p (k f)"), ACT.Exp
              ).then_inc(fin_exp, 1)
            act.wait_ge(fin_att, 1)
            A(HHI[:, NW:ND, TP:T], SM[:, 10].rearrange("p (c b) -> p c b", c=NW), ACT.Copy).then_inc(fin_hi, 1)

            for m in range(ND):
                act.wait_ge(tile_done, T_OE + m + 1)
                unit_used(U_OE + m)

            def mlp(layer):
                tb, ub = T_F[layer], U_F[layer]
                norm(2 * layer + 1)

                def gate(jj, t, done, free, conv):
                    act.wait_ge(tile_done, done)
                    wait(act, conv_done, conv)
                    wait(act, fout_ready, conv)
                    A(by3(CV[jj][:, 2:2 + T]), psum_tile(t), ACT.Copy).then_inc(tile_free[t % 2], 1)

                def silu(jj, conv):
                    act.wait_ge(conv_done, conv)
                    A(CC[jj], CC[jj], ACT.Silu, bias=FPB[:, jj, 3:4]).then_inc(silu_done, 1)

                def hidden(jj, t, free, hid):
                    act.wait_ge(tile_free[t % 2], free)
                    A(HIDH[:, jj], HR[jj], ACT.Copy).then_inc(hid_hi, 1)

                c0 = layer * NF
                for jj in range(2):
                    t = tb + 2 * jj
                    gate(jj, t, t + 1, None, c0)
                    unit_used(ub + 2 * jj)
                    silu(jj, c0 + jj + 1)
                    act.wait_ge(tile_done, t + 2)
                    unit_used(ub + 2 * jj + 1)
                for jj in range(2):
                    t = tb + 2 * jj + 1
                    hidden(jj, t, freed(t), None)
                def step(i):
                    def used_at(u, done):
                        if isinstance(i, int):
                            act.wait_ge(tile_done, done)
                            return unit_used(u + 6 * i)
                        v = u + SLOTS
                        act.wait_ge(w_loaded[v % SLOTS], i * 32 + 16 * (v // SLOTS + 1))
                        act.wait_ge(tile_done, done)
                        A(WHI[:, v % SLOTS], WRAW[:, v % SLOTS], ACT.Copy).then_inc(w_hi, 1)
                        load_at(u + 5, i)

                    for jj in range(2):
                        t = tb + 4 + 2 * jj
                        gate(jj, t, i * 12 + (t + 1), None, i * 2 + (c0 + jj + 1))
                        used_at(ub + 4 + 2 * jj, i * 12 + (t + 1))
                        silu(jj, i * 2 + (c0 + 2 + jj + 1))
                        used_at(ub + 5 + 2 * jj, i * 12 + (t + 2))
                    for r in range(2):
                        used_at(ub + 8 + r, i * 12 + (tb + 16))
                    for jj in range(2):
                        t = tb + 5 + 2 * jj
                        hidden(jj, t, i * 6 + freed(t), None)

                with act.Fori(0, FI - 2) as i:
                    step(i)
                step(FI - 2)
                act.wait_ge(tile_done, tb + 12 * FI)
                for r in range(2):
                    unit_used(ub + 6 * FI - 2 + r)

            mlp(0)

            norm(2)
            t = T_GO
            act.wait_ge(tile_done, t + 1)
            A(by3(GA[:]), psum_tile(t, HB), ACT.Identity, bias=PRM[0:HB, O_GB + 1:O_GB + 2]).then_inc(tile_free[t % 2], 1)
            act.wait_ge(gmoved, 16)
            log_sigmoid(GB[0:HC, :], TROW)
            for u in range(20):
                t, j = (T_IO + u if u < 16 else T_P[u - 16]), u % 4
                if u < 4:
                    evacuate(QT[:, j], t)
                elif u < 8:
                    evacuate(KT[:, j], t, scale=DK ** -0.5)
                elif u < 12:
                    if u == 8:
                        act.wait_ge(x_saved, 16)
                    act.wait_ge(vt_psum, 2 * (NW + j - 1))
                    evacuate(TMP[j % 2], t)
                    A(VTS[:, j], TMP[j % 2][:, TP:T], ACT.Copy).then_inc(vts_ready, 1)
                elif u < 16:
                    if j < 2:
                        act.wait_ge(vt_psum, 2 * (NW + 3 + (j > 0)))
                    else:
                        act.wait_ge(tmp_out[j % 2], 48)
                    evacuate(TMP[j % 2], t, ACT.Sigmoid)
                    act.dma_start(o["o_scr"][j], TMP[j % 2]).then_inc(tmp_out[j % 2], 16)
                else:
                    if j == 0:
                        act.wait_ge(px_zero, 1)
                    else:
                        act.wait_ge(pz_ready, j)
                        act.wait_ge(pool_out, 32 * j)
                    evacuate(PX[:, PREV:PREV + T], t)
                    A(SX[:, :, PREV], PX[:, PREV + TP:PREV + T], ACT.Copy).then_inc(px_ready, 1)
                    act.wait_ge(px_ready, j + 1)
                    act.wait_ge(sx_ready, j + 1)
                    act.dma_start(o["pool_p"][j], PX[:, TP:TP + PREV]).then_inc(pool_out, 16)
                    act.dma_start(o["pool_s"][j], SX[:, :, 1:16]).then_inc(pool_out, 16)
                if u == 4:
                    act.wait_ge(acol_psum, 1)
                    A(ACOL[:].rearrange("p c h -> p (c h)"), M0[:, 0:NB * HC], ACT.Copy).then_inc(acol_ready, 1)
                unit_used(U_IO + u, deferred=(U_OO + 3, U_OO + 4))
                if 9 <= u <= 12:
                    values_turned(u - 9, 1)
                if u == 13:
                    act.wait_ge(vrow_psum, 1)
                    A(SROW[:], M0[0:B], ACT.Copy).then_inc(vrow_sbuf, 1)
                if u >= 17:
                    for g in ([u - 17] if u < 19 else [2, 3]):
                        t = T_PM[g]
                        act.wait_ge(tmp_out[g % 2], 64 if g < 2 else 80)
                        evacuate(TMP[g % 2], t, ACT.Identity, scale=PRM[:, O_PSCALE + g:O_PSCALE + g + 1])
                        act.dma_start(o["p_scr"][g], TMP[g % 2]).then_inc(tmp_out[g % 2], 16)

            act.wait_ge(sgate_args, 1)
            A(SROWS[:, 0:3].rearrange("p k b -> p (k b)"), SROWS[:, 4:7].rearrange("p k b -> p (k b)"), ACT.Exp
              ).then_inc(srows_ready, 1)
            act.wait_ge(srows_psum, 1)
            A(SBC[:].rearrange("p h k b -> p (h k b)"), M0[:, 0:HC * 3 * B], ACT.Copy).then_inc(sbc_ready, 1)

            def chunk_in(i):
                ch, h = divmod(i, HC)
                x, w, e = XA[i % 2], XW[i % 2], XE[i % 2]
                act.wait_ge(xa_psum, i + 1)
                wait(act, kw_ready, i - 1)
                wait(act, hc_ready, i - 1)
                A(x, G[i % 2][:, 0], ACT.Copy).then_inc(xa_sbuf, 1)
                act.wait_ge(xa_sbuf, i + 1)
                A(e[:, 0:P], x[:, 0:P], ACT.Exp, scale=-1.0, bias=APV[:, h:h + 1])
                A(e[:, P:2 * P], x[:, P:2 * P], ACT.Exp, scale=-1.0)
                A(WG[:, i % 2:i % 2 + 1], x[:, P - 1:P], ACT.Exp, scale=-1.0, bias=ACOL[:, ch, h:h + 1])
                act.wait_ge(wm_ready, i + 1)
                A(w[:, 0:P], w[:, 0:P], ACT.Exp, bias=ACOL[:, ch, h:h + 1]).then_inc(w_exp, 1)

            def chunk_out(i):
                act.wait_ge(y_psum, i + 1)
                A(XE[i % 2][:, 2 * P:3 * P], G[i % 2][:, 1, P:2 * P], ACT.Abs).then_inc(den_abs, 1)

            act.wait_ge(w_lo, U_OO + SLOTS)
            act.wait_ge(mrow_ready, 1)
            for i in range(HC * NB):
                if i >= 1:
                    wait(act, apv_ready, i - HC + 1)
                chunk_in(i)
                if i:
                    chunk_out(i - 1)
            chunk_out(HC * NB - 1)
            act.wait_ge(hc_ready, HC * NB)
            load(U_OO + 3)
            load(U_OO + 4)
            for c in range(NW):
                act.wait_ge(hc_gated, c + 1)
                A(HHI[:, c], HCT[:, c], ACT.Copy).then_inc(hc_hi, 1)
            act.wait_ge(pool_back, 16)
            for c in range(NW):
                A(HHI[:, NW + c], QT[:, c], ACT.Copy).then_inc(back_hi, 1)
            act.dma_start(o["m_p"], GB[0:HC, TP - 1:TP]).then_inc(act_outs, 16)
            act.dma_start(o["m_s"], SROWS[:, 3]).then_inc(act_outs, 16)
            act.wait_ge(qn_ready, 1)
            act.dma_start(o["n_s"], SM[:, 1]).then_inc(act_outs, 16)

            for m in range(ND):
                act.wait_ge(tile_done, T_OO + m + 1)
                unit_used(U_OO + m)
            mlp(1)
            norm(4, halves=False)

        @block.vector
        def _(dve):
            own = Own(dve, own_dve)
            TT, TS, STT = nc.vector.tensor_tensor, nc.vector.tensor_scalar, nc.vector.scalar_tensor_tensor

            def free(ins, t):
                ins.then_inc(tile_free[t % 2], 1)

            def norm(n):
                t = T_N[n]
                for c in range(1, ND):
                    dve.wait_ge(sq_ready, n * ND + c + 1)
                    if c > 1:
                        dve.wait_ge(sq_summed, n * (ND - 1) + c - 1)
                    TT(ACC, ACC, SQ[c % 2], ALU.add).then_inc(sq_summed, 1)
                dve.wait_ge(tile_free[t % 2], freed(t))
                own.link(nc.vector.reciprocal(RSTD, RSTD))

                def low(c):
                    dve.wait_ge(h_hi, n * ND + c + 1)
                    TT(HLO[:, c], HN[c % 4], HHI[:, c].bitcast(F32), ALU.subtract).then_inc(h_lo_dve, 1)

                for c in range(ND):
                    gain = PRM[:, GAINS[n] + c:GAINS[n] + c + 1]
                    if n == 4:
                        STT(out=XT[:, c], in0=XT[:, c], scalar=gain, in1=RSTD, op0=ALU.mult, op1=ALU.mult
                            ).then_inc(y_ready, 1)
                        continue
                    if c >= 4:
                        dve.wait_ge((h_lo_dve, h_lo_pool)[c % 2], n * (ND // 2) + (c - 4) // 2 + 1)
                    STT(out=HN[c % 4], in0=XT[:, c], scalar=gain, in1=RSTD, op0=ALU.mult, op1=ALU.mult
                        ).then_inc(h_raw, 1)
                    if c % 2:
                        low(c - 1)

            def key_group(g):
                b, slot = g // 8, g % 2
                if g == 0:
                    dve.wait_ge(bias_sbuf, 4)
                dve.wait_ge(qb_loaded, 16 * (b + 1))
                dve.wait_ge(kv_loaded[slot], 16 * PG * (g // 2 + 1))
                ring = RING[:, slot, 0:2]
                own.link(TT(ring, ring, QB[:, b % 2:b % 2 + 1, :].to_broadcast([P, 2, NW * P]), ALU.mult))
                dve.wait_ge(k_mul, g + 1)
                nc.vector.tensor_reduce(KTMP[:].rearrange("p g h -> p (g h)"),
                                        RING[:, slot].rearrange("p g (h d) -> p (g h) d", d=HD),
                                        AX.X, ALU.add).then_inc(k_red, 1)
                dve.wait_ge(k_red, g + 1)
                dst = SCR[:, b, (g % 8) * PG:(g % 8 + 1) * PG]
                own.link(TT(dst, dst, KTMP[:], ALU.add))

            dve.wait_ge(logf_in, 32)
            nc.vector.tensor_reduce(TOT[:], LG.rearrange("p s q h -> p s h q"), AX.X, ALU.add).then_inc(tot_ready, 1)

            dve.wait_ge(par_in, 16 * PAR_LOADS)
            norm(0)
            dve.wait_ge(logsig_in, 1)
            STT(out=GA[:], in0=GA[:], scalar=0.0, in1=GB[:], op0=ALU.min, op1=ALU.subtract).then_inc(logf_ready, 1)
            dve.wait_ge(logf_ready, 1)
            nc.vector.tensor_tensor_scan(GB[:, 0:TP], ones[0:HB, 0:1].to_broadcast([HB, TP]), GA[:, 0:TP], 0.0,
                                         ALU.mult, ALU.subtract).then_inc(fcum_ready, 1)

            def conv(cv, out, taps, state, step):
                s0, s1 = state[:, :, 0], state[:, :, 1]
                own.link(TS(out[:, 0:TP], cv[:, 0:TP], taps[0], None, ALU.mult))
                own.link(TS(out[:, TP:T], s0, taps[0], None, ALU.mult))
                own.link(STT(out=out[:, 0:TP], in0=cv[:, 1:TP + 1], scalar=taps[1], in1=out[:, 0:TP],
                             op0=ALU.mult, op1=ALU.add))
                own.link(STT(out=out[:, TP:T], in0=s1, scalar=taps[1], in1=out[:, TP:T], op0=ALU.mult, op1=ALU.add))
                ins = STT(out=out, in0=cv[:, 2:T + 2], scalar=taps[2], in1=out, op0=ALU.mult, op1=ALU.add)
                step(ins)

            key = [0]
            for u in range(24):
                t, jc, kind = T_IE + u, (u - 12) // 3, (u - 12) % 3
                for _ in range(K_PLAN.get(u, 0)):
                    key_group(key[0])
                    key[0] += 1
                if u >= 12 and kind == 1:
                    if jc == 0:
                        dve.wait_ge(tmp_out[1], 32)
                        dve.wait_ge(vt_psum, 2 * NW)
                        dve.wait_ge(cvx_zero, 1)
                    else:
                        dve.wait_ge(a_saved, 16 * jc)
                    dve.wait_ge(tile_free[(t - 1) % 2], freed(t - 1))
                    dve.wait_ge(tile_done, t + 1)
                    free(TT(by3(CVX[:, 2:2 + T]), psum_tile(t), by3(TMP[0]), ALU.mult), t)
                    dve.wait_ge(tile_free[t % 2], freed(t))
                    state = PRM[:, O_SCONVA + jc * 2 * B:O_SCONVA + (jc + 1) * 2 * B].rearrange("p (b r) -> p b r", r=2)
                    conv(CVX, TMP[1], [PRM[:, O_CONVA + jc * 3 + x:O_CONVA + jc * 3 + x + 1] for x in range(3)],
                         state, own.link)
                    nc.vector.tensor_copy(FOUT[:, jc, 0:2], CVX[:, TP:TP + 2])
                    FO = FOUT[:, jc, 2:].rearrange("p (b r) -> p b r", r=2)
                    nc.vector.tensor_copy(FO[:, :, 0], state[:, :, 1])
                    nc.vector.tensor_copy(FO[:, :, 1], CVX[:, TP + 2:T + 2]).then_inc(fout_conv, 1)
                if u >= 12 and kind == 2:
                    dve.wait_ge(tile_done, t + 1)
                    free(TT(by3(TMP[1]), psum_tile(t), by3(TMP[1]), ALU.mult), t)

            nc.vector.tensor_reduce(MX[:], SCR[:].rearrange("p b g h -> p b h g"), AX.X, ALU.max).then_inc(smax_ready, 1)
            dve.wait_ge(smax_all, 1)
            TT(SCR[:], SCR[:], MXA[:].rearrange("p b (a h) -> p b a h", a=1).to_broadcast([P, B, PAGES, HB]),
               ALU.subtract).then_inc(sshift, 1)
            dve.wait_ge(sprob, 1)
            nc.vector.tensor_reduce(RSS[:], SCR[:].rearrange("p b g h -> p b h g"), AX.X, ALU.add).then_inc(ssum, 1)
            c4 = lambda k: SM[:, k].rearrange("p (c b) -> p c b", c=NW)
            TT(c4(0), QT[:, :, TP:T], KT[:, :, TP:T], ALU.mult).then_inc(qk_new, 1)

            def result(h, qb, k):
                dve.wait_ge(p_ready, k + 1)
                own.link(nc.vector.reciprocal(FMX[:, 3, k % 2:k % 2 + 1], FMX[:, 2, k % 2:k % 2 + 1]))
                dve.wait_ge(o_done, k + 1)
                if h >= 2 and h % 2 == 0:
                    dve.wait_ge(s_done, ORDER.index(("t", h // 2 - 1)) + 1)
                TS(OT[:, qb, (h % 2) * HD:(h % 2 + 1) * HD], M0[:, 0:HD], FMX[:, 3, k % 2:k % 2 + 1], None, ALU.mult
                   ).then_inc(o_sbuf, 1)

            before = None
            dve.wait_ge(w_lo, U_OE + SLOTS)
            dve.wait_ge(a_saved, 16 * NW)
            for x, item in enumerate(ORDER):
                if item[0] == "n":
                    continue
                if item[0] == "s":
                    h, qb = item[1:]
                    k, n = h * NB + qb, (qb + 1) * P
                    if qb == 0:
                        xn = ORDER.index(("n", h))
                        dve.wait_ge(s_free[xn % 2], xn // 2 + 1)
                    if k >= 2:
                        dve.wait_ge(pt_psum, ROUNDS[k - 2])
                    dve.wait_ge(s_done, x + 1)
                    nc.vector.tensor_tensor_reduce(SC[k % 2][:, 0:n], GF[x % 2][:, 0:n], NEGF[h % 2][:, 0:n], 1.0,
                                                   -3.0e38, ALU.add, ALU.max, FMX[:, 0, k % 2:k % 2 + 1]
                                                   ).then_inc(s_free[x % 2], 1)
                    dve.wait_ge(s_free[x % 2], x // 2 + 1)
                    TS(FMX[:, 1, k % 2:k % 2 + 1], FMX[:, 0, k % 2:k % 2 + 1], -1.0, None, ALU.mult).then_inc(sc_ready, 1)
                    if before:
                        result(*before)
                    before = (h, qb, k)
                    continue
                j = item[1]
                if x == len(ORDER) - 1:
                    result(*before)
                dve.wait_ge(att_hi, j + 1)
                TT(HLO[:, NW + j, 0:TP], GF[x % 2][:, 0:TP], HHI[:, NW + j, 0:TP].bitcast(F32), ALU.subtract
                   ).then_inc(s_free[x % 2], 1)

            dve.wait_ge(vts_ready, NW)
            dve.wait_ge(fin_psum, 1)
            dve.wait_ge(v_used, GROUPS)
            for par in range(2):
                r = slice(64 * par, 64 * par + 64)
                by_b = lambda v: v.rearrange("p b (c two) -> p c b two", two=2)[:, :, :, par]
                own.link(nc.vector.tensor_copy(c4(2)[r], by_b(MXA[r])))
                own.link(nc.vector.tensor_copy(c4(3)[r], by_b(M0[r, 0:64].rearrange("p (b h) -> p b h", b=B))))
                own.link(nc.vector.tensor_copy(c4(8)[r], by_b(M1[r, 0:64].rearrange("p (b h) -> p b h", b=B))))
            own.link(nc.vector.tensor_copy(SM[:, 9], M0[:, 96:128]))
            own.link(TT(SM[:, 1], M0[:, 64:96], SM[:, 9], ALU.subtract))
            own.link(TT(SM[:, 9], SM[:, 1], SM[:, 2], ALU.max))
            own.link(TT(SM[:, 4], SM[:, 2], SM[:, 9], ALU.subtract))
            TT(SM[:, 5], SM[:, 1], SM[:, 9], ALU.subtract).then_inc(fin_args, 1)
            dve.wait_ge(fin_exp, 1)
            own.link(TT(SM[:, 9], SM[:, 6], SM[:, 3], ALU.mult))
            own.link(TT(SM[:, 9], SM[:, 9], SM[:, 7], ALU.add))
            own.link(nc.vector.reciprocal(SM[:, 9], SM[:, 9]))
            own.link(TT(SM[:, 8], SM[:, 8], SM[:, 6], ALU.mult))
            own.link(TT(SM[:, 10], VTS[:].rearrange("p c b -> p (c b)"), SM[:, 7], ALU.mult))
            own.link(TT(SM[:, 8], SM[:, 8], SM[:, 10], ALU.add))
            TT(SM[:, 10], SM[:, 8], SM[:, 9], ALU.mult).then_inc(fin_att, 1)
            dve.wait_ge(fin_att, 1)
            dve.wait_ge(fin_hi, 1)
            TT(HLO[:, NW:ND, TP:T], c4(10), HHI[:, NW:ND, TP:T].bitcast(F32), ALU.subtract).then_inc(sfeat, 1)

            def residual(t, loads):
                dve.wait_ge(x_in, loads)
                for m in range(ND):
                    dve.wait_ge(tile_done, t + m + 1)
                    free(TT(by3(XT[:, m]), by3(XT[:, m]), psum_tile(t + m), ALU.add), t + m)

            residual(T_OE, 64)

            def mlp(layer):
                tb, n0 = T_F[layer], layer * NF
                norm(2 * layer + 1)

                def up(jj, t, gate_free, fpb, up_done, silu, hid):
                    dve.wait_ge(cv_zero, layer + 1)
                    dve.wait_ge(fpb_ready, fpb)
                    dve.wait_ge(tile_free[t % 2], gate_free)
                    state = FPB[:, jj, 4:].rearrange("p (b r) -> p b r", r=2)
                    conv(CV[jj], CC[jj], [FPB[:, jj, x:x + 1] for x in range(3)], state,
                         lambda ins: ins.then_inc(conv_done, 1))
                    dve.wait_ge(silu_done, silu)
                    dve.wait_ge(tile_done, up_done)
                    wait(dve, hid_lo, hid)
                    free(TT(by3(HR[jj]), psum_tile(t + 1), by3(CC[jj]), ALU.mult), t + 1)

                def down(t, done):
                    for m in range(ND):
                        dve.wait_ge(tile_done, done(m))
                        free(TT(by3(XT[:, m]), by3(XT[:, m]), psum_tile(t + m), ALU.add), t + m)

                for jj in range(2):
                    t = tb + 2 * jj
                    up(jj, t, freed(t), layer * FI + 1, t + 2, n0 + jj + 1, n0)
                with dve.Fori(0, FI - 1) as i:
                    own.enter(i, 8)
                    for jj in range(2):
                        t = tb + 4 + 2 * jj
                        up(jj, t, i * 6 + freed(t), i + (layer * FI + 2), i * 12 + (t + 2), i * 2 + (n0 + jj + 3),
                           i * 2 + (n0 + jj + 1))
                    down(tb + 8, lambda m: i * 12 + (tb + 9 + m))
                own.leave(FI - 1)
                t = tb + 12 * FI - 8
                down(t, lambda m: t + m + 1)

            mlp(0)

            norm(2)
            dve.wait_ge(logsig_in, 2)
            own.link(STT(out=GB[0:HC, :], in0=GB[0:HC, :], scalar=0.0, in1=TROW, op0=ALU.min, op1=ALU.subtract))
            one_row = ones[0:HC, 0:1].to_broadcast([HC, TP])
            own.link(nc.vector.tensor_tensor_scan(BROW, one_row, GB[0:HC, 0:TP], 0.0, ALU.mult, ALU.add))
            TT(AROW, AROW, BROW, ALU.subtract).then_inc(arow_ready, 1)
            dve.wait_ge(arow_ready, 1)
            own.link(nc.vector.tensor_tensor_scan(MAXROW, one_row, AROW, 0.0, ALU.mult, ALU.max))
            own.link(TT(MROW, BROW, MAXROW, ALU.add))
            m0 = PRM[0:HC, O_M0:O_M0 + B]
            li, lf = GA[0:HC, TP:T], GB[0:HC, TP:T]
            own.link(TT(SROWS[:, 4], lf, m0, ALU.add))
            own.link(TT(SROWS[:, 3], SROWS[:, 4], li, ALU.max))
            own.link(TT(SROWS[:, 4], SROWS[:, 4], SROWS[:, 3], ALU.subtract))
            own.link(TT(SROWS[:, 5], li, SROWS[:, 3], ALU.subtract))
            TS(SROWS[:, 6], SROWS[:, 3], -1.0, None, ALU.mult).then_inc(sgate_args, 1)
            nc.vector.memset(APV[:], 0.0)
            nc.vector.memset(CST[:], 0.0).then_inc(mrow_ready, 1)
            dve.wait_ge(mrow_ready, 1)

            for g, win in enumerate(WINS):
                t = T_P[g]
                if g >= 2:
                    dve.wait_ge(tile_done, T_PM[g - 2] + 1)
                dve.wait_ge(px_ready, g + 1)
                dve.wait_ge(sx_ready, g + 1)
                src, lo = PX, 0
                for lev in range(g + 1):
                    s = 1 << lev
                    lo += s
                    dst = PD[lev % 2]
                    own.link(TT(dst[:, lo:PREV + TP], src[:, lo:PREV + TP], src[:, lo - s:PREV + TP - s], ALU.add))
                    src = dst
                z = PZ[g % 2]
                own.link(STT(out=z[:, 0:TP], in0=src[:, PREV:PREV + TP], scalar=1.0 / win, in1=PX[:, PREV:PREV + TP],
                             op0=ALU.mult, op1=ALU.subtract))
                own.link(TT(z[:, 0:PREV], src[:, PREV:2 * PREV], PRM[:, O_RCP + g * PREV:O_RCP + (g + 1) * PREV], ALU.mult))
                own.link(TT(z[:, 0:PREV], z[:, 0:PREV], PX[:, PREV:2 * PREV], ALU.subtract))
                own.link(nc.vector.tensor_reduce(SXS[:], SX[:, :, 16 - win:16], AX.X, ALU.add))
                STT(out=z[:, TP:T], in0=SXS[:], scalar=1.0 / win, in1=SX[:, :, PREV], op0=ALU.mult, op1=ALU.subtract
                    ).then_inc(pz_ready, 1)

            dve.wait_ge(sbc_ready, 1)
            hb = lambda k: SM[:, k].rearrange("p (h b) -> p h b", h=HC)
            n0v = PRM[:, O_N0:O_N0 + HC * B].rearrange("p (h b) -> p h b", h=HC)
            own.link(TT(hb(0), KT[:, :, TP:T], SBC[:, :, 1], ALU.mult))
            own.link(TT(hb(1), n0v, SBC[:, :, 0], ALU.mult))
            own.link(TT(hb(1), hb(1), hb(0), ALU.add))
            TT(hb(2), hb(1), QT[:, :, TP:T], ALU.mult).then_inc(qn_ready, 1)
            dve.wait_ge(c0_in, 16)
            dve.wait_ge(vb_in, 16 * B)
            for s in range(HC * B):
                b, h = divmod(s, HC)
                own.link(TS(C0[:, s], C0[:, s], SBC[:, h, 0, b:b + 1], None, ALU.mult))
                STT(out=C0[:, s], in0=VB[:, b, h * DK:(h + 1) * DK], scalar=SM[:, 0, h * B + b:h * B + b + 1],
                    in1=C0[:, s], op0=ALU.mult, op1=ALU.add).then_inc(c_new, 1)
            dve.wait_ge(snum_psum, 1)
            own.link(nc.vector.tensor_copy(SM[:, 3], M0[:, 192:224]))
            own.link(nc.vector.tensor_copy(SM[:, 4], M0[:, 128:160]))
            own.link(STT(out=SM[:, 5], in0=SM[:, 4], scalar=-1.0, in1=SM[:, 4], op0=ALU.mult, op1=ALU.max))
            own.link(TT(hb(4), hb(5), SBC[:, :, 2], ALU.max))
            own.link(nc.vector.reciprocal(SM[:, 4], SM[:, 4]))
            dve.wait_ge(c_new, HC * B)
            TT(HCT[:, :, TP:T], hb(3), hb(4), ALU.mult).then_inc(hcs_ready, 1)

            def chunk_in(i):
                ch, h = divmod(i, HC)
                x, w, e = XA[i % 2], XW[i % 2], XE[i % 2]
                wait(dve, y_psum, i - 1)
                dve.wait_ge(xa_sbuf, i + 1)
                STT(out=w[:, 0:P], in0=x[:, 0:P], scalar=-1.0, in1=CON[:, C_MASKT], op0=ALU.mult, op1=ALU.add
                    ).then_inc(wm_ready, 1)
                dve.wait_ge(w_exp, i + 1)
                nc.vector.tensor_copy(APV[:, h:h + 1], x[:, P - 1:P]).then_inc(apv_ready, 1)
                TT(w[:, P:2 * P], x[:, 2 * P:3 * P], w[:, 0:P], ALU.mult)
                TT(w[:, 2 * P:3 * P], QT[:, h, ch * P:(ch + 1) * P], e[:, 0:P], ALU.mult)
                TS(w[:, 3 * P:4 * P], x[:, 3 * P:4 * P], WG[:, i % 2:i % 2 + 1], None, ALU.mult).then_inc(kw_ready, 1)

            def chunk_out(i):
                ch, h = divmod(i, HC)
                y, e = G[i % 2][:, 1], XE[i % 2]
                dve.wait_ge(den_abs, i + 1)
                STT(out=CST[:, h], in0=CST[:, h], scalar=e[:, P - 1:P], in1=y[:, 2 * P:3 * P + 1], op0=ALU.mult,
                    op1=ALU.add).then_inc(cst_ready, 1)
                own.link(TT(e[:, 2 * P:3 * P], e[:, 2 * P:3 * P], e[:, P:2 * P], ALU.max))
                own.link(nc.vector.reciprocal(e[:, 2 * P:3 * P], e[:, 2 * P:3 * P]))
                TT(HCT[:, h, ch * P:(ch + 1) * P], y[:, 0:P], e[:, 2 * P:3 * P], ALU.mult).then_inc(hc_ready, 1)

            for i in range(HC * NB):
                chunk_in(i)
                if i:
                    chunk_out(i - 1)
            chunk_out(HC * NB - 1)
            dve.wait_ge(og_in, 16)
            dve.wait_ge(hcs_ready, 1)
            dve.wait_ge(hc_ready, HC * NB)
            for c in range(NW):
                TT(HCT[:, c], HCT[:, c], XT[:, c], ALU.mult).then_inc(hc_gated, 1)
            for c in range(NW):
                dve.wait_ge(hc_gated, c + 1)
                dve.wait_ge(hc_hi, c + 1)
                TT(HLO[:, c], HCT[:, c], HHI[:, c].bitcast(F32), ALU.subtract).then_inc(hc_lo, 1)

            residual(T_OO, 80)
            mlp(1)
            norm(4)

        @block.gpsimd
        def _(pool):
            TT = nc.gpsimd.tensor_tensor

            def low(u, value=None):
                if u < U_END or value is not None:
                    pool.wait_ge(w_hi, u + 1 if value is None else value)
                    s = u % SLOTS
                    TT(WLO[:, s], WRAW[:, s], WHI[:, s].bitcast(F32), ALU.subtract).then_inc(w_lo, 1)

            def norm(n):
                for c in range(1, ND, 2):
                    pool.wait_ge(h_hi, n * ND + c + 1)
                    TT(HLO[:, c], HN[c % 4], HHI[:, c].bitcast(F32), ALU.subtract).then_inc(h_lo_pool, 1)

            pool.dma_start(PTI[:], a["pti"]).then_inc(pages_in_pool, 16)
            pool.wait_ge(pages_in_pool, 16)
            for s in range(2):
                pool.indirect_dma_start(out=VF[:, s * 1024:(s + 1) * 1024], out_offset=None, in_=a["clf"],
                                        in_offset=bass.IndirectOffsetOnAxis(ap=PTI[:, s:s + 1], axis=0),
                                        ).then_inc(logf_in, 16)
            pool.wait_ge(gw_hi, 1)
            TT(GWL[:], GWR[:], GWH[:].bitcast(F32), ALU.subtract).then_inc(gw_lo, 1)
            for u in range(SLOTS):
                low(u)
            norm(0)
            pool.wait_ge(h_raw, ND)
            nc.gpsimd.memset(CVX[:, 0:2], 0.0).then_inc(cvx_zero, 1)

            key = [0]
            for u in range(24):
                for _ in range(K_PLAN.get(u, 0)):
                    g = key[0]
                    b, slot = g // 8, g % 2
                    pool.wait_ge(qb_loaded, 16 * (b + 1))
                    pool.wait_ge(kv_loaded[slot], 16 * PG * (g // 2 + 1))
                    ring = RING[:, slot, 2:4]
                    TT(ring, ring, QB[:, b % 2:b % 2 + 1, :].to_broadcast([P, 2, NW * P]), ALU.mult).then_inc(k_mul, 1)
                    key[0] += 1
                low(U_IE + u + SLOTS)

            pool.wait_ge(smax_ready, 1)
            nc.gpsimd.partition_all_reduce(MXA[:].rearrange("p b h -> p (b h)"), MX[:].rearrange("p b h -> p (b h)"),
                                           P, RMAX).then_inc(smax_all, 1)

            for j in range(NW):
                pool.wait_ge(back_hi, j + 1)
                TT(HLO[:, j, 0:TP], QT[:, j, 0:TP], HHI[:, j, 0:TP].bitcast(F32), ALU.subtract).then_inc(back_lo, 1)
            pool.wait_ge(back_hi, NW + 1)
            TT(HLO[:, 0:NW, TP:T], AS[:], HHI[:, 0:NW, TP:T].bitcast(F32), ALU.subtract).then_inc(back_lo, 1)

            for m in range(ND):
                low(U_OE + m + SLOTS)

            def mlp(layer):
                ub, n0 = U_F[layer], layer * NF
                norm(2 * layer + 1)
                pool.wait_ge(sq_summed, (2 * layer + 2) * (ND - 1))
                pool.wait_ge(tile_done, T_N[2 * layer + 1] + 1)
                nc.gpsimd.memset(CV[0][:, 0:2], 0.0)
                nc.gpsimd.memset(CV[1][:, 0:2], 0.0).then_inc(cv_zero, 1)
                pool.wait_ge(fpar_in, 16 * (layer + 1))
                if layer == 0:
                    pool.wait_ge(fconv_out, 16)
                else:
                    pool.wait_ge(outs, 16)

                def params(i, silu):
                    wait(pool, silu_done, silu)
                    wait(pool, fout_ready, silu)
                    src = FPRM[:, bass.ds(i * 2, 2)]
                    nc.gpsimd.tensor_copy(FPB[:], src).then_inc(fpb_ready, 1)

                def states(i, jj, free, fpb):
                    t = T_F[layer] + 2 * jj
                    pool.wait_ge(tile_free[t % 2], free)
                    pool.wait_ge(fpb_ready, fpb)
                    dst = FOUT[:, bass.ds(i * 2 + jj, 1)].rearrange("p a f -> p (a f)")
                    nc.gpsimd.tensor_copy(dst[:, 0:2], CV[jj][:, TP:TP + 2])
                    pairs = dst[:, 2:].rearrange("p (b r) -> p b r", r=2)
                    nc.gpsimd.tensor_copy(pairs[:, :, 0], FPB[:, jj, 4:].rearrange("p (b r) -> p b r", r=2)[:, :, 1])
                    nc.gpsimd.tensor_copy(pairs[:, :, 1], CV[jj][:, TP + 2:T + 2]).then_inc(fout_ready, 1)

                def hidden(jj, hi):
                    pool.wait_ge(hid_hi, hi)
                    TT(HIDL[:, jj], HR[jj], HIDH[:, jj].bitcast(F32), ALU.subtract).then_inc(hid_lo, 1)

                params(0, n0)
                for jj in range(2):
                    t = T_F[layer] + 2 * jj
                    low(ub + 2 * jj + SLOTS)
                    states(0, jj, freed(t), layer * FI + 1)
                    low(ub + 2 * jj + 1 + SLOTS)
                for jj in range(2):
                    hidden(jj, n0 + jj + 1)
                def step(i):
                    def low_at(u):
                        low(u + 6 * i) if isinstance(i, int) else low(u, i * 6 + (u + 1))

                    params(i + 1, i * 2 + (n0 + 2))
                    for jj in range(2):
                        t = T_F[layer] + 4 + 2 * jj
                        u = ub + 4 + 2 * jj + SLOTS
                        low_at(u)
                        states(i + 1, jj, i * 6 + freed(t), i + (layer * FI + 2))
                        low_at(u + 1)
                    for r in range(2):
                        low_at(ub + 8 + r + SLOTS)
                    for jj in range(2):
                        hidden(jj, i * 2 + (n0 + jj + 3))

                with pool.Fori(0, FI - 2) as i:
                    step(i)
                step(FI - 2)
                for r in range(2):
                    low(ub + 6 * FI - 2 + r + SLOTS)

            mlp(0)
            norm(2)

            for u in range(20):
                if u >= 16:
                    j = u - 16
                    if j == 0:
                        pool.wait_ge(x_saved, 16)
                        pool.wait_ge(spool_in, 16)
                        nc.gpsimd.memset(PX[:, 0:PREV], 0.0).then_inc(px_zero, 1)
                    else:
                        pool.wait_ge(pz_ready, j)
                        pool.wait_ge(pool_out, 32 * j)
                    nc.gpsimd.tensor_copy(SX[:, :, 0:PREV], SPOOL[:, j]).then_inc(sx_ready, 1)
                low(U_IO + u + SLOTS)
            for c in range(NW):
                pool.wait_ge(back_hi, NW + 1 + c + 1)
                TT(HLO[:, NW + c], QT[:, c], HHI[:, NW + c].bitcast(F32), ALU.subtract).then_inc(back_lo, 1)
            for m in range(ND):
                low(U_OO + m + SLOTS)
            mlp(1)
            assert key[0] == GROUPS


_SCRATCH = {"q_scr": (B, NW * P), "v_scr": (B, NW * P), "a_scr": (NW, P, T), "o_scr": (NW, P, T),
            "p_scr": (NW, P, T), "x_scr": (P, ND, T)}
_OUTS = {"y": (ND, P, T), "k": (NW, P, T), "v": (NW, P, T), "logf": (HB, T), "conv_a": (P, NW, 2 + 2 * B),
         "c_p": (P, HC, DK + 1), "c_s": (P, HC * B, DK), "n_s": (P, HC * B), "m_p": (HC, 1), "m_s": (HC, B),
         "pool_p": (NW, P, PREV), "pool_s": (NW, P, B, PREV), "ffn": (2, P, NF, 2 + 2 * B)}


def _chunks(x):
    return np.ascontiguousarray(np.moveaxis(x.reshape((-1, P) + x.shape[1:]), 0, 1))


def _units(w):
    n = w.shape[1] // P
    return w.reshape(ND, P, n, P).transpose(2, 1, 0, 3).reshape(n, P, UNIT)


def _mlp_units(w_up, w_down):
    up, down = _units(w_up), w_down.reshape(NF, P, UNIT)
    out = []
    for i in range(FI + 1):
        if i < FI:
            for j in (2 * i, 2 * i + 1):
                out += [up[j], up[NF + j]]
        if i:
            out += [down[2 * i - 2], down[2 * i - 1]]
    return np.stack(out)


def _weights(x):
    we, wo = x["w_in_even"][0], x["w_in_odd"][0]
    a, w, k = 512, _units(we[:, 0:6 * 512]), 4
    conv = [w[g * k + j] for j in range(k) for g in (0, 2, 1)]
    odd = np.concatenate([wo[:, 0:4 * a], wo[:, 4 * a + 2 * HC:]], axis=1)
    return np.concatenate([w[3 * k:], np.stack(conv), _units(x["w_out_even"][0]), _mlp_units(x["w_up"][0], x["w_down"][0]),
                           _units(odd), _units(x["w_out_odd"][0]), _mlp_units(x["w_up"][1], x["w_down"][1])])


def _params(x):
    p = np.zeros((P, O_END), np.float32)
    for n in range(2):
        p[:, O_GMIX + n * ND:O_GMIX + (n + 1) * ND] = _chunks(x["norm_mix"][n])
        p[:, O_GFFN + n * ND:O_GFFN + (n + 1) * ND] = _chunks(x["norm_ffn"][n])
    p[:, O_GFIN:O_GFIN + ND] = _chunks(x["norm_final"])
    p[:, O_CONVA:O_CONVA + NW * 3] = _chunks(x["conv_a"][0].T).reshape(P, -1)
    p[:, O_PSCALE:O_PSCALE + NW] = _chunks(x["pool_scale_odd"][0])
    p[0:HB, O_GB] = x["b_forget_even"][0]
    p[0:HC, O_GB + 1] = x["b_igate_odd"][0]
    p[HC:2 * HC, O_GB + 1] = x["b_fgate_odd"][0]
    p[:, O_SCONVA:O_SCONVA + NW * B * 2] = _chunks(x["state_conv_a"][0].transpose(2, 0, 1)).reshape(P, -1)
    for g, win in enumerate(WINS):
        for t in range(PREV):
            p[:, O_RCP + g * PREV + t] = 1.0 / min(win, t + 1)
    p[:, O_N0:O_N0 + HC * B] = x["state_mlstm_n"][0].transpose(2, 1, 0).reshape(P, -1)
    p[0:HC, O_M0:O_M0 + B] = x["state_mlstm_m"][0].T
    p[:, O_EPS] = EPS
    return p


def _mlp_params(x):
    taps = x["ffn_conv_w"].transpose(0, 2, 1)
    bias = x["ffn_conv_b"][:, :, None]
    state = x["state_ffn_conv"].transpose(0, 3, 1, 2).reshape(2, FF, 2 * B)
    return np.stack([_chunks(np.concatenate([taps[n], bias[n], state[n]], axis=1)) for n in range(2)])


def _constants():
    i = np.arange(P)
    c = np.zeros((P, NCON, P), np.float32)
    c[:, C_ID] = np.eye(P)
    c[:, C_ONE] = 1.0
    c[:, C_MASK] = np.where(i[None, :] > i[:, None], NEG, 0.0)
    c[:, C_MASKT] = np.where(i[:, None] > i[None, :], NEG, 0.0)
    c[:, C_LATER] = i[:, None] > i[None, :]
    same = i[:, None] // PAGES == i[None, :] // PAGES
    c[:, C_PLATER] = same & (i[:, None] > i[None, :])
    c[:, C_BLK] = i[:, None] // HD == i[None, :] // HD
    s = np.zeros((HB, NW, P), np.float32)
    for h in range(HB):
        s[h, h // 2, (h % 2) * HD:(h % 2 + 1) * HD] = 1.0
    return c, s


def kernel(**inputs):
    import concourse.bacc as bacc
    from concourse.bass_utils import run_bass_kernel_spmd

    x = {k: np.asarray(v) for k, v in inputs.items()}
    con, selc = _constants()
    gw = np.stack([_chunks(x["w_in_even"][0][:, 3072:3080]), _chunks(x["w_in_odd"][0][:, 2048:2056])], axis=1)
    phys = x["cache_k"].shape[1]
    arrays = {
        "xp": _chunks(x["x_prompt"][0].T), "xs": _chunks(x["x_sample"][:, 0].T),
        "ck": x["cache_k"].reshape(phys, P, 512), "cv": x["cache_v"].reshape(phys, P, 512),
        "clf": x["cache_logf"].reshape(phys, P * HB), "pt": x["page_table"].reshape(1, -1),
        "pti": x["page_table"].reshape(2, P).T, "w": _weights(x), "gw": gw, "prm": _params(x),
        "fprm": _mlp_params(x), "con": con, "selc": selc, "pw": x["w_pool_odd"][0].transpose(1, 0, 2),
        "c0": x["state_mlstm_c"][0].transpose(2, 0, 1, 3).reshape(P, HC * B, DK),
        "spool": _chunks(x["state_pool"][0].transpose(2, 0, 1)),
    }
    arrays = {k: np.ascontiguousarray(v) for k, v in arrays.items()}
    nc = bacc.Bacc("TRN2", target_bir_lowering=False, num_devices=1, dynamic_dma_scratch_size=2048)
    ins = {k: nc.dram_tensor(f"in_{k}", v.shape, mybir.dt.from_np(v.dtype), kind="ExternalInput").ap()
           for k, v in arrays.items()}
    outs = {k: nc.dram_tensor(f"out_{k}", s, F32, kind="ExternalOutput").ap() for k, s in _OUTS.items()}
    outs |= {k: nc.dram_tensor(k, s, F32, kind="Internal").ap() for k, s in _SCRATCH.items()}
    trunk(nc, ins, outs)
    r = run_bass_kernel_spmd(nc, [{f"in_{k}": v for k, v in arrays.items()}], core_ids=[0]).results[0]
    g = {k: np.asarray(r[f"out_{k}"]).reshape(s) for k, s in _OUTS.items()}

    def tokens(v):
        v = v.reshape(-1, T).T
        return v[:TP], v[TP:]

    yp, ys = tokens(g["y"])
    kp, ks = tokens(g["k"])
    vp, vs = tokens(g["v"])
    lp, ls = tokens(g["logf"])

    def states(v):
        v = v.transpose(2, 1, 0).reshape(2 + 2 * B, -1)
        return v[None, 0:2], v[2:].reshape(B, 2, -1)

    cp, cs = states(g["conv_a"])
    fp, fs = zip(*(states(g["ffn"][n]) for n in range(2)))
    c_p = g["c_p"].transpose(1, 0, 2)
    pool_p = g["pool_p"].reshape(512, PREV).T
    pool_s = g["pool_s"].reshape(512, B, PREV).transpose(1, 2, 0)
    out = (yp[None], ys[:, None],
           kp.reshape(1, 1, TP, HB, HD), ks.reshape(1, B, 1, HB, HD),
           vp.reshape(1, 1, TP, HB, HD), vs.reshape(1, B, 1, HB, HD),
           lp.reshape(1, 1, TP, HB), ls.reshape(1, B, 1, HB), cp[None], cs[None],
           c_p[None, None, :, :, 0:DK], g["c_s"].reshape(P, B, HC, DK).transpose(1, 2, 0, 3)[None],
           c_p[None, None, :, :, DK], g["n_s"].reshape(P, HC, B).transpose(2, 1, 0)[None],
           g["m_p"].reshape(1, 1, HC), g["m_s"].T[None],
           pool_p[None, None], pool_s[None], np.stack(fp), np.stack(fs))
    return tuple(np.ascontiguousarray(v) for v in out)
```

```python
from contextlib import ExitStack

import numpy as np

import concourse.bass as bass
from concourse import mybir

F32 = mybir.dt.float32
F32R = mybir.dt.float32r
I32 = mybir.dt.int32
ALU = mybir.AluOpType
ACT = mybir.ActivationFunctionType
AX = mybir.AxisListType
RMAX = bass.bass_isa.ReduceOp.max

P = 128
D = 1024
ND = D // P
TP = 1024
NB = TP // P
B = 8
T = TP + B
BANKS = 3
TC = T // BANKS
PAGES = 32
PG = 4
GROUPS = B * PAGES // PG
HB, HD = 8, 64
HC, DK = 4, 128
NW = 4
FF = 2816
NF = FF // P
FI = NF // 2
SLOTS = 3
UNIT = 1024
WINS = (2, 4, 8, 16)
PREV = 15
EPS = 1e-6
NEG = -1.0e30

O_GMIX, O_GFFN, O_GFIN = 0, 2 * ND, 4 * ND
O_CONVA = 5 * ND
O_PSCALE = O_CONVA + NW * 3
O_GB = O_PSCALE + NW
O_SCONVA = O_GB + 2
O_RCP = O_SCONVA + NW * B * 2
O_N0 = O_RCP + NW * PREV
O_M0 = O_N0 + HC * B
O_EPS = O_M0 + B
O_END = O_EPS + 1
FCH = 4 + 2 * B
C_ID, C_ONE, C_MASK, C_MASKT, C_LATER, C_PLATER, C_BLK = range(7)
NCON = 7
CVW = 2 + T + 6
PXW = PREV + T + 1

U_IE = 0
U_OE = U_IE + 24
U_F = (U_OE + 8, 0)
U_IO = U_F[0] + 6 * FI
U_OO = U_IO + 20
U_F = (U_F[0], U_OO + 8)
U_END = U_F[1] + 6 * FI
T_N0, T_GE, T_IE = 0, 1, 2
T_OE = T_IE + 24
T_N1 = T_OE + 8
T_F0 = T_N1 + 1
T_N2 = T_F0 + 12 * FI
T_GO = T_N2 + 1
T_IO = T_GO + 1
T_P = [T_IO + 16 + x for x in (0, 1, 3, 5)]
T_PM = [T_IO + 16 + x for x in (2, 4, 6, 7)]
T_OO = T_IO + 24
T_N3 = T_OO + 8
T_F1 = T_N3 + 1
T_N4 = T_F1 + 12 * FI
T_F = (T_F0, T_F1)
T_N = (T_N0, T_N1, T_N2, T_N3, T_N4)
GAINS = (O_GMIX, O_GFFN, O_GMIX + ND, O_GFFN + ND, O_GFIN)
T_X = (None, T_OE, T_N2 - 8, T_OO, T_N4 - 8)


def after_unit(n_in, u0, t0):
    return {u0 + j: t0 + j for j in range(n_in)}


LAST_TILE = {**after_unit(24, U_IE, T_IE), **after_unit(8, U_OE, T_OE), **after_unit(20, U_IO, T_IO),
             **after_unit(8, U_OO, T_OO)}
for _j in range(4):
    LAST_TILE[U_IO + 16 + _j] = T_P[_j]


def last_tile(u):
    if u in LAST_TILE:
        return LAST_TILE[u]
    layer = int(u >= U_F[1])
    v, t = u - U_F[layer], T_F[layer]
    if v < 4:
        return t + v
    i, r = divmod(v - 4, 6)
    if i == FI - 1:
        return t + 12 * FI - 1
    return t + 4 + 12 * i + (r if r < 4 else 11)


def attention_order():
    order = [("n", 0)]
    for h in range(HB):
        for qb in range(NB):
            order.append(("s", h, qb))
            if qb == 5 and h + 1 < HB:
                order.append(("n", h + 1))
            if qb == 1 and h % 2 == 0 and h:
                order.append(("t", h // 2 - 1))
    order.append(("t", HB // 2 - 1))
    return order


ORDER = attention_order()
ROUNDS = []
for _k in range(HB * NB):
    ROUNDS.append((ROUNDS[-1] if ROUNDS else 0) + (_k % NB) // 4 + 1)
PT_ROUNDS = ROUNDS[-1]
PAR_LOADS = 5
ACT_OUTS = 8
KD = 2
V_POOL = (2, 2)
K_PLAN = {u: (4 if u < 12 else 3) for u in range(5, 24)}


def wait(eng, sem, value):
    if not isinstance(value, int) or value > 0:
        eng.wait_ge(sem, value)


class Own:

    def __init__(self, eng, sem):
        self.eng, self.sem, self.n = eng, sem, 0

    def link(self, ins):
        ins.then_inc(self.sem, 1)
        self.n = self.n + 1
        self.eng.wait_ge(self.sem, self.n)

    def enter(self, i, per):
        self.base, self.per, self.n = self.n, per, i * per + self.n
        self.start, self.made = self.n, 0

    def leave(self, times):
        self.n = self.base + self.per * times


def trunk(nc, a, o):
    with ExitStack() as ctx:
        E = ctx.enter_context

        def sb(name, shape, dt=F32):
            return E(nc.sbuf_tensor(name, shape, dt))

        def sem(name):
            return E(nc.semaphore(name))

        XT = sb("XT", [P, ND, T])
        with nc.sbuf_tensor("HF", [P, 2, ND * T], F32) as HF:
            pass
        HHI = sb("HHI", [P, ND, T], F32R)
        HLO = sb("HLO", [P, ND, T], F32R)
        WHI = sb("WHI", [P, SLOTS, UNIT], F32R)
        WLO = sb("WLO", [P, SLOTS, UNIT], F32R)
        WRAW = sb("WRAW", [P, SLOTS, UNIT])
        VTOK = sb("VTOK", [P, NB, NW * P])
        KT = sb("KT", [P, NW, T])
        with nc.sbuf_tensor("QT", [P, NW, T], F32) as QT:
            pass
        HIDH = sb("HIDH", [P, 2, T], F32R)
        HIDL = sb("HIDL", [P, 2, T], F32R)
        SCR = sb("SCR", [P, B, PAGES, HB])
        QB = sb("QB", [P, 2, NW * P])
        GA = sb("GA", [HB, T])
        GB = sb("GB", [HB, T])
        PRM = sb("PRM", [P, O_END])
        FPRM = sb("FPRM", [P, NF, FCH])
        FPB = sb("FPB", [P, 2, FCH])
        FOUT = sb("FOUT", [P, NF, 2 + 2 * B])
        CON = sb("CON", [P, NCON, P])
        SELC = sb("SELC", [HB, NW, P])
        GWR = sb("GWR", [P, 2, ND, HB])
        GWH = sb("GWH", [P, 2, ND, HB], F32R)
        GWL = sb("GWL", [P, 2, ND, HB], F32R)
        PT = sb("PT", [1, B * PAGES], I32)
        PTI = sb("PTI", [P, 2], I32)
        TOT = sb("TOT", [P, 2, HB])
        KTMP = sb("KTMP", [P, 2, PG, HB])
        MX = sb("MX", [P, B, HB])
        MXA = sb("MXA", [P, B, HB])
        RSS = sb("RSS", [P, B, HB])
        LSB = sb("LSB", [P, B, HB])
        SM = sb("SM", [P, 11, NW * B])
        VTS = sb("VTS", [P, NW, B])
        SROW = sb("SROW", [HB, NW * P])
        FMX = sb("FMX", [P, 4, 4])
        ACOL = sb("ACOL", [P, NB, HC])
        APV = sb("APV", [P, HC])
        WG = sb("WG", [P, 2])
        SROWS = sb("SROWS", [HC, 7, B])
        AS = sb("AS", [P, NW, B])
        SXS = sb("SXS", [P, B])
        PW = sb("PW", [P, NW, P])
        SBC = sb("SBC", [P, HC, 3, B])

        G = [E(nc.psum_tensor(f"G{s}", [P, BANKS, 512], F32)) for s in range(2)]
        M0 = E(nc.psum_tensor("M0", [P, 512], F32))
        M1 = E(nc.psum_tensor("M1", [P, 512], F32))

        XF = XT[:].rearrange("p c t -> p (c t)")
        KF = KT[:].rearrange("p c t -> p (c t)")
        VF = VTOK[:].rearrange("p c t -> p (c t)")
        GF = [g[:].rearrange("p a b -> p (a b)") for g in G]
        ident = CON[:, C_ID]
        ones = CON[:, C_ONE]
        RING = XF[:, 0:2 * PG * 512].rearrange("p (s g f) -> p s g f", s=2, g=PG)
        SQ = [KT[:, 0], KT[:, 1]]
        ACC, RSTD = KT[:, 2], KT[:, 3]
        HN = [QT[:, c] for c in range(4)]
        LG = VF[:, 0:2048].rearrange("p (s q h) -> p s q h", s=2, h=HB)
        LT = VF[:, 2048:4096].rearrange("p (s h g) -> p s h g", s=2, h=HB)
        TMP = [XT[:, 4], XT[:, 5]]
        CVX = XF[:, 6 * T:6 * T + CVW]
        NEGF = [XT[:, 4, 0:TP], XT[:, 7, 0:TP]]
        SC = [XT[:, 5], XT[:, 6]]
        PTS = [WRAW[:, 0], WRAW[:, 1]]
        OT = WRAW[:, 2].rearrange("p (q f) -> p q f", f=P)
        VSLOT = [RING[:, 0], RING[:, 1]] + [
            HF[:, 1, s * PG * 512:(s + 1) * PG * 512].rearrange("p (g f) -> p g f", g=PG) for s in range(2)]
        VACC = [[QB[:, 0], QB[:, 1]],
                [HF[:, 0, s * 512:(s + 1) * 512] for s in range(2)]]
        CV = [KF[:, 0:CVW], KF[:, CVW:2 * CVW]]
        CC = [KF[:, 2 * CVW:2 * CVW + T], VF[:, 2 * T:3 * T]]
        HR = [VF[:, 0:T], VF[:, T:2 * T]]
        PX = XF[:, 0:PXW]
        PD = [XF[:, PXW:2 * PXW], XF[:, 2 * PXW:3 * PXW]]
        SX = XF[:, 3 * PXW:3 * PXW + B * 16].rearrange("p (b r) -> p b r", r=16)
        PZ = [XT[:, 6], XT[:, 7]]
        C0 = XF[:, 0:HC * B * DK].rearrange("p (s e) -> p s e", e=DK)
        VB = XF[:, NW * T:NW * T + B * 512].rearrange("p (b f) -> p b f", b=B)
        AROW, MROW = GA[0:HC, 0:TP], GB[0:HC, 0:TP]
        TROW = SCR[:].rearrange("p b g h -> p (b g h)")[0:HC, 0:T]
        MAXROW = TROW[:, 0:TP]
        SPOOL = SCR[:].rearrange("p b g h -> p (b g h)")[:, 1548:1548 + NW * B * PREV].rearrange(
            "p (c b r) -> p c b r", c=NW, b=B)
        CST = SCR[:].rearrange("p b g h -> p (b g h)")[:, T:T + HC * (DK + 1)].rearrange(
            "p (h e) -> p h e", h=HC)
        BROW = QB[:].rearrange("p s f -> p (s f)")[0:HC, 0:TP]
        XA = [WRAW[:, 0, 0:512], WRAW[:, 0, 512:1024]]
        XW = [WRAW[:, 1, 0:512], WRAW[:, 1, 512:1024]]
        XE = [WRAW[:, 2, 0:512], WRAW[:, 2, 512:1024]]
        HCT = XT[:, 4:8]

        def psum_tile(t, rows=P):
            return G[t % 2][0:rows, :, 0:TC]

        def by3(x):
            return x.rearrange("p (b t) -> p b t", b=BANKS)

        def freed(t):
            return t // 2 + 1

        x_in = sem("x_in")
        par_in = sem("par_in")
        pages_in = sem("pages_in")
        fpar_in = sem("fpar_in")
        loaded = sem("loaded")
        qrow_sbuf = sem("qrow_sbuf")
        row_dram = sem("row_dram")
        qb_loaded = sem("qb_loaded")
        h_raw = sem("h_raw")
        kd_loaded = [sem(f"kd_loaded{s}") for s in range(2)]
        kd_red = sem("kd_red")
        kp_loaded = [sem(f"kp_loaded{s}") for s in range(2)]
        kp_red = sem("kp_red")
        v_loaded = [sem(f"v_loaded{s}") for s in range(4)]
        tile_done = sem("tile_done")
        v_used_dve = sem("v_used_dve")
        v_used_pool = sem("v_used_pool")
        p_ready = sem("p_ready")
        pt_psum = sem("pt_psum")
        fout_ready = sem("fout_ready")
        outs = sem("outs")
        fpb_ready = sem("fpb_ready")
        x_saved = sem("x_saved")
        spool_in = sem("spool_in")
        tile_free = [sem(f"tile_free{s}") for s in range(2)]
        gmoved = sem("gmoved")
        vrow_sbuf = sem("vrow_sbuf")
        tmp_out = [sem(f"tmp_out{s}") for s in range(2)]
        c0_in = sem("c0_in")
        vb_in = sem("vb_in")
        c_new = sem("c_new")
        c_out = sem("c_out")
        snum_psum = sem("snum_psum")
        og_in = sem("og_in")
        cst_ready = sem("cst_ready")
        y_psum = sem("y_psum")
        pool_back = sem("pool_back")
        hc_lo = sem("hc_lo")
        y_ready = sem("y_ready")
        act_outs = sem("act_outs")
        fconv_out = sem("fconv_out")
        pool_out = sem("pool_out")
        w_lo = sem("w_lo")
        sq_summed = sem("sq_summed")
        gw_lo = sem("gw_lo")
        h_lo_dve = sem("h_lo_dve")
        h_lo_pool = sem("h_lo_pool")
        vt_sbuf = sem("vt_sbuf")
        vt_psum = sem("vt_psum")
        logf_in = sem("logf_in")
        lt_sbuf = sem("lt_sbuf")
        lt_psum = sem("lt_psum")
        tot_ready = sem("tot_ready")
        bias_sbuf = sem("bias_sbuf")
        bias_psum = sem("bias_psum")
        qrow_psum = sem("qrow_psum")
        summed = sem("summed")
        v_summed = sem("v_summed")
        s_done = sem("s_done")
        pt_sbuf = sem("pt_sbuf")
        o_sbuf = sem("o_sbuf")
        o_done = sem("o_done")
        fcum_ready = sem("fcum_ready")
        s_free = [sem(f"s_free{s}") for s in range(2)]
        ssum = sem("ssum")
        qk_new = sem("qk_new")
        fin_psum = sem("fin_psum")
        back_lo = sem("back_lo")
        sfeat = sem("sfeat")
        hid_lo = sem("hid_lo")
        arow_ready = sem("arow_ready")
        acol_psum = sem("acol_psum")
        acol_ready = sem("acol_ready")
        vts_ready = sem("vts_ready")
        vrow_psum = sem("vrow_psum")
        pz_ready = sem("pz_ready")
        srows_ready = sem("srows_ready")
        srows_psum = sem("srows_psum")
        sbc_ready = sem("sbc_ready")
        qn_ready = sem("qn_ready")
        mrow_ready = sem("mrow_ready")
        xa_sbuf = sem("xa_sbuf")
        xa_psum = sem("xa_psum")
        hc_ready = sem("hc_ready")
        kw_ready = sem("kw_ready")
        own_act = sem("own_act")
        w_loaded = [sem(f"w_loaded{s}") for s in range(SLOTS)]
        w_hi = sem("w_hi")
        sq_ready = sem("sq_ready")
        h_hi = sem("h_hi")
        gw_hi = sem("gw_hi")
        logsig_in = sem("logsig_in")
        a_saved = sem("a_saved")
        logf_ready = sem("logf_ready")
        fout_conv = sem("fout_conv")
        sshift = sem("sshift")
        sprob = sem("sprob")
        rsum_ready = sem("rsum_ready")
        sc_ready = sem("sc_ready")
        att_hi = sem("att_hi")
        back_in = [sem(f"back_in{s}") for s in range(NW)]
        back_hi = sem("back_hi")
        fin_args = sem("fin_args")
        fin_exp = sem("fin_exp")
        fin_att = sem("fin_att")
        fin_hi = sem("fin_hi")
        conv_done = sem("conv_done")
        silu_done = sem("silu_done")
        hid_hi = sem("hid_hi")
        px_zero = sem("px_zero")
        px_ready = sem("px_ready")
        sx_ready = sem("sx_ready")
        sgate_args = sem("sgate_args")
        wm_ready = sem("wm_ready")
        w_exp = sem("w_exp")
        den_abs = sem("den_abs")
        apv_ready = sem("apv_ready")
        hc_gated = sem("hc_gated")
        hc_hi = sem("hc_hi")
        own_dve = sem("own_dve")
        kd_mul = sem("kd_mul")
        k_mul = sem("k_mul")
        k_added = sem("k_added")
        cvx_zero = sem("cvx_zero")
        smax_ready = sem("smax_ready")
        smax_all = sem("smax_all")
        cv_zero = sem("cv_zero")
        hcs_ready = sem("hcs_ready")
        pages_in_pool = sem("pages_in_pool")
        own_pool = sem("own_pool")

        block = E(nc.Block())

        def slice_of_dve(g):
            return slice(V_POOL[g % 2], PG)

        def slice_of_pool(g):
            return slice(0, V_POOL[g % 2])

        def values_of(eng, multiply_add, pages_of, which, used, own):
            def group(g):
                b, slot, pages = g // 8, VSLOT[g % 4], pages_of(g)
                acc = VACC[b % 2][which]
                n = pages.stop - pages.start
                if g == 0:
                    eng.wait_ge(sprob, 1)
                eng.wait_ge(v_loaded[g % 4], 16 * PG * (g // 4 + 1))
                v = slot[:, pages].rearrange("p g (h d) -> p (g h) d", d=HD)
                p0 = (g % 8) * PG
                prob = SCR[:, b, p0 + pages.start:p0 + pages.stop].rearrange("p g (h a) -> p (g h) a", a=1)
                own.link(multiply_add(v, v, prob.to_broadcast([P, n * HB, HD]), ALU.mult))
                page = [slot[:, pages.start + j] for j in range(n)]
                if g % 8 == 0:
                    wait(eng, v_summed, b - 1)
                    if n == 1:
                        (nc.vector if eng is nc.vector else nc.gpsimd).tensor_copy(acc, page[0]).then_inc(used, 1)
                        eng.wait_ge(used, g + 1)
                        return
                    own_or_used = page[1:]
                    first = multiply_add(acc, page[0], page[1], ALU.add)
                    rest = page[2:]
                else:
                    first = multiply_add(acc, acc, page[0], ALU.add)
                    rest = page[1:]
                for x in rest:
                    own.link(first)
                    first = multiply_add(acc, acc, x, ALU.add)
                first.then_inc(used, 1)
                eng.wait_ge(used, g + 1)
            return group

        @block.sync
        def _(sp):
            sp.dma_start(XT[:, :, 0:TP], a["xp"]).then_inc(x_in, 16)
            sp.dma_start(XT[:, :, TP:T], a["xs"]).then_inc(x_in, 16)
            sp.dma_start(CON[:], a["con"]).then_inc(par_in, 16)
            sp.dma_start(PT[:], a["pt"]).then_inc(pages_in, 16)
            sp.dma_start(GWR[:], a["gw"]).then_inc(par_in, 16)
            sp.dma_start(PRM[:], a["prm"]).then_inc(par_in, 16)
            sp.dma_start(SELC[:], a["selc"]).then_inc(par_in, 16)
            sp.dma_start(PW[:], a["pw"]).then_inc(par_in, 16)
            sp.dma_start(FPRM[:], a["fprm"][0]).then_inc(fpar_in, 16)

            def bcast_row(t, row):
                return t[bass.ds(row, 1), :].to_broadcast([P, NW * P])

            def kv_load(cache, g, dst, pg, loaded, *used):
                pages = [sp.value_load(PT[0:1, bass.ds(g * PG + j, 1)], min_val=0, max_val=cache.shape[0] - 1)
                         for j in pg]
                for done, value in used:
                    wait(sp, done, value)
                for j, page in zip(pg, pages):
                    sp.dma_start(dst[:, j], cache[bass.ds(page, 1)].rearrange("a p f -> (a p) f")
                                 ).then_inc(loaded, 16)

            sp.wait_ge(qrow_sbuf, 1)
            sp.dma_start(o["q_scr"], SROW[:]).then_inc(row_dram, 16)
            sp.wait_ge(row_dram, 16)
            sp.dma_start(QB[:, 0], bcast_row(o["q_scr"], 0)).then_inc(qb_loaded, 16)
            sp.wait_ge(h_raw, ND)
            sp.wait_ge(pages_in, 16)

            def keys(g0, first, last):
                for g in range(16):
                    for at, n in ((2, 1), (10, 2)):
                        if g == at and not (last and n == 2):
                            b = g0 // 8 + n if first else None
                            if first:
                                sp.wait_ge(qb_loaded, b * 16)
                                row = b
                            else:
                                row = sp.snap(g0[1] + n)
                                sp.wait_ge(qb_loaded, g0[1] * 16 + n * 16)
                            sp.dma_start(QB[:, n % 2], bcast_row(o["q_scr"], row)).then_inc(qb_loaded, 16)
                    gg = g0 + g if first else g0[0] + g
                    before = gg - 1 if first else g0[0] + (g - 1)
                    kv_load(a["ck"], gg, RING[:, g % 2], range(KD), kd_loaded[g % 2], (kd_red, before))
                    kv_load(a["ck"], gg, RING[:, g % 2], range(KD, PG), kp_loaded[g % 2], (kp_red, before))

            keys(0, True, False)
            with sp.Fori(1, B // 2 - 1) as i:
                keys((i * 16, i * 2), False, False)
            keys(GROUPS - 16, True, True)

            for g in range(8):
                kv_load(a["cv"], g, VSLOT[g % 4], range(PG), v_loaded[g % 4],
                        *([(kd_red, GROUPS - 1 + g), (kp_red, GROUPS - 1 + g)] if g < 2 else [(tile_done, T_IE + 24)] if g < 4 else
                          [(v_used_dve, g - 3), (v_used_pool, g - 3)]))
            with sp.Fori(1, B) as b:
                for g in range(8):
                    kv_load(a["cv"], b * 8 + g, VSLOT[g % 4], range(PG), v_loaded[g % 4], (v_used_dve, b * 8 + (g - 3)),
                            (v_used_pool, b * 8 + (g - 3)))

            sp.wait_ge(v_used_dve, GROUPS)
            sp.wait_ge(v_used_pool, GROUPS)
            sp.wait_ge(p_ready, HB * NB)
            sp.wait_ge(pt_psum, PT_ROUNDS)
            sp.dma_start(XT[:, :, 0:TP], a["xp"]).then_inc(x_in, 16)
            sp.dma_start(XT[:, :, TP:T], a["xs"]).then_inc(x_in, 16)

            sp.wait_ge(fout_ready, NF)
            sp.dma_start(o["ffn"][0], FOUT[:]).then_inc(outs, 16)
            sp.wait_ge(fpb_ready, FI)
            sp.dma_start(FPRM[:], a["fprm"][1]).then_inc(fpar_in, 16)

            sp.wait_ge(h_raw, 3 * ND)
            sp.dma_start(o["x_scr"], XT[:]).then_inc(x_saved, 16)
            sp.dma_start(SPOOL, a["spool"]).then_inc(spool_in, 16)
            sp.wait_ge(tile_free[T_GO % 2], freed(T_GO))
            sp.dma_start(GB[0:HC, :], GA[HC:2 * HC, :]).then_inc(gmoved, 16)
            sp.wait_ge(vrow_sbuf, 1)
            sp.dma_start(o["v_scr"], SROW[:]).then_inc(row_dram, 16)
            sp.wait_ge(row_dram, 32)
            for s in range(2):
                sp.wait_ge(tmp_out[s], 96)
            sp.wait_ge(tile_free[T_PM[3] % 2], freed(T_PM[3]))
            sp.dma_start(C0, a["c0"]).then_inc(c0_in, 16)
            for b in range(B):
                sp.dma_start(VB[:, b], bcast_row(o["v_scr"], b)).then_inc(vb_in, 16)
            sp.wait_ge(c_new, HC * B)
            sp.dma_start(o["c_s"], C0).then_inc(c_out, 16)
            sp.wait_ge(c_out, 16)
            sp.wait_ge(snum_psum, 1)
            for s in range(2):
                sp.wait_ge(tmp_out[s], 64)
            sp.dma_start(XT[:, 0:NW], o["o_scr"].rearrange("c p t -> p c t")).then_inc(og_in, 16)
            sp.wait_ge(cst_ready, HC * NB)
            sp.dma_start(o["c_p"], CST).then_inc(outs, 16)
            sp.wait_ge(y_psum, HC * NB)
            sp.dma_start(QT[:], o["p_scr"].rearrange("c p t -> p c t")).then_inc(pool_back, 16)
            sp.wait_ge(hc_lo, NW)
            sp.wait_ge(x_saved, 16)
            sp.dma_start(XT[:], o["x_scr"]).then_inc(x_in, 16)

            sp.wait_ge(fout_ready, 2 * NF)
            sp.dma_start(o["ffn"][1], FOUT[:]).then_inc(outs, 16)
            for c in range(ND):
                sp.wait_ge(y_ready, c + 1)
                sp.dma_start(o["y"][c], XT[:, c]).then_inc(outs, 16)
            sp.wait_ge(outs, 16 * (3 + ND))
            sp.wait_ge(act_outs, 16 * ACT_OUTS)
            sp.wait_ge(fconv_out, 16)
            sp.wait_ge(pool_out, 32 * NW)

        @block.tensor
        def _(pe):
            def passes(out, whi, wlo, xhi, xlo, first, last):
                for n, (w, x) in enumerate(((whi, xhi), (whi, xlo), (wlo, xhi))):
                    for c in range(BANKS):
                        mm = pe.matmul(out[:, c], w, x[:, c * TC:(c + 1) * TC], start=first and n == 0,
                                       stop=last and n == 2)
                return mm

            def unit(u, t, free, lo):
                slot = u % SLOTS
                pe.wait_ge(w_lo, lo)
                wait(pe, tile_free[t % 2], free)
                for k in range(ND):
                    mm = passes(psum_tile(t), WHI[:, slot, k * P:(k + 1) * P], WLO[:, slot, k * P:(k + 1) * P],
                                HHI[:, k], HLO[:, k], k == 0, k == ND - 1)
                mm.then_inc(tile_done, 1)

            def plain_unit(u, t):
                unit(u, t, t // 2, u + 1)

            def norm(n):
                t = T_N[n]
                pe.wait_ge(sq_summed, (n + 1) * (ND - 1))
                wait(pe, tile_free[t % 2], t // 2)
                for c in range(BANKS):
                    mm = pe.matmul(psum_tile(t)[:, c], ones, ACC[:, c * TC:(c + 1) * TC], start=True, stop=True)
                mm.then_inc(tile_done, 1)

            def gate_tile(layer, t):
                return t, psum_tile(t, HB), lambda k: (GWH[:, layer, k], GWL[:, layer, k]), (gw_lo, 1)

            def unit_tile(u, t):
                return t, psum_tile(t), lambda k: (WHI[:, u % SLOTS, k * P:(k + 1) * P],
                                                   WLO[:, u % SLOTS, k * P:(k + 1) * P]), (w_lo, u + 1)

            def first_tiles(n, tiles):
                for t, _, _, ready in tiles:
                    pe.wait_ge(*ready)
                    pe.wait_ge(tile_free[t % 2], t // 2)
                for k in range(ND):
                    pe.wait_ge((h_lo_dve, h_lo_pool)[k % 2], n * (ND // 2) + k // 2 + 1)
                    for t, out, weights, _ in tiles:
                        mm = passes(out, *weights(k), HHI[:, k], HLO[:, k], k == 0, k == ND - 1)
                        if k == ND - 1:
                            mm.then_inc(tile_done, 1)

            def values_turned(j, layer):
                t = (T_IE if layer == 0 else T_IO) + 8 + j
                pe.wait_ge(tile_free[t % 2], freed(t))
                for r in range(2):
                    n = (layer * NW + j) * 2 + r
                    wait(pe, vt_sbuf, n)
                    for q in range(4):
                        mm = pe.transpose(M0[:, q * P:(q + 1) * P], TMP[j % 2][:, (r * 4 + q) * P:(r * 4 + q + 1) * P],
                                          ident)
                    mm.then_inc(vt_psum, 1)

            def forgets_turned(r):
                half, hq = r // 2, r % 2
                if r == 0:
                    pe.wait_ge(logf_in, 32)
                wait(pe, lt_sbuf, r)
                for q in range(4):
                    mm = pe.transpose(M0[:, q * P:(q + 1) * P], LG[:, half, :, hq * 4 + q], ident)
                mm.then_inc(lt_psum, 1)

            def forgets_summed(r):
                half, hq = r // 2, r % 2
                pe.wait_ge(tot_ready, 1)
                pe.wait_ge(lt_sbuf, r + 1)
                wait(pe, bias_sbuf, r)
                for q in range(4):
                    h = hq * 4 + q
                    dst = M1[:, q * P:(q + 1) * P]
                    pe.matmul(dst, CON[:, C_LATER], LT[:, half, h], start=True, stop=False)
                    mm = pe.matmul(dst, TOT[:, half, h:h + 1].to_broadcast([P, P]), CON[:, C_PLATER],
                                   start=False, stop=True)
                mm.then_inc(bias_psum, 1)

            pe.wait_ge(par_in, 16 * PAR_LOADS)
            norm(0)
            first_tiles(0, [gate_tile(0, T_GE), unit_tile(U_IE, T_IE)])
            for u in range(24):
                if u:
                    plain_unit(U_IE + u, T_IE + u)
                if u < 4:
                    forgets_turned(u)
                if 1 <= u < 5:
                    forgets_summed(u - 1)
                if u == 4:
                    pe.wait_ge(lt_sbuf, 4)
                    for s in range(2):
                        pe.wait_ge(tile_free[s], freed(T_IE + 2 + s))
                    for j in range(NW):
                        mm = pe.transpose(M0[0:B, j * P:(j + 1) * P], QT[:, j, TP:T], ident)
                    mm.then_inc(qrow_psum, 1)
                    pe.wait_ge(qrow_sbuf, 1)
                if 9 <= u <= 12:
                    values_turned(u - 9, 0)

            def value_sum(b):
                pe.wait_ge(v_used_dve, 8 * (b + 1))
                pe.wait_ge(v_used_pool, 8 * (b + 1))
                if b == 0:
                    pe.wait_ge(bias_sbuf, 4)
                for c in range(NW):
                    for n, acc in enumerate(VACC[b % 2]):
                        mm = pe.matmul(M1[:, b * NW + c:b * NW + c + 1], acc[:, c * P:(c + 1) * P], ones[:, 0:1],
                                       start=n == 0, stop=n == 1)
                mm.then_inc(v_summed, 1)

            def scores(x, h, qb):
                rows = slice(HD * (h % 2), HD * (h % 2) + HD)
                n = (qb + 1) * P
                for c0 in range(0, n, 512):
                    c1 = min(n, c0 + 512)
                    pe.matmul(GF[x % 2][:, c0:c1], QT[rows, h // 2, qb * P:(qb + 1) * P], KT[rows, h // 2, c0:c1],
                              start=True, stop=c1 < n)
                pe.matmul(GF[x % 2][:, n - P:n], ident, CON[:, C_MASK], start=False, stop=True).then_inc(s_done, 1)

            rounds = [0]

            def turns(h, qb, k):
                pe.wait_ge(p_ready, k + 1)
                for r in range(qb // 4 + 1):
                    n = rounds[0]
                    wait(pe, pt_sbuf, n - 1)
                    for q in range(r * 4, min(r * 4 + 4, qb + 1)):
                        mm = pe.transpose(G[n % 2][:, 2, (q % 4) * P:(q % 4 + 1) * P], SC[k % 2][:, q * P:(q + 1) * P],
                                          ident)
                    mm.then_inc(pt_psum, 1)
                    rounds[0] = n + 1

            def results(h, qb, k):
                pe.wait_ge(pt_sbuf, ROUNDS[k])
                wait(pe, o_sbuf, k)
                for q in range(qb + 1):
                    mm = pe.matmul(M0[:, 0:HD], PTS[k % 2][:, q * P:(q + 1) * P], VTOK[:, q, h * HD:(h + 1) * HD],
                                   start=q == 0, stop=q == qb)
                mm.then_inc(o_done, 1)

            pe.wait_ge(vt_sbuf, 2 * NW)
            pe.wait_ge(fcum_ready, 1)
            for s in range(2):
                pe.wait_ge(tile_free[s], (T_OE + 1 - s) // 2)
            late = []
            for x, item in enumerate(ORDER):
                if item[0] == "s" and item[2] == 1 and item[1]:
                    value_sum(item[1] - 1)
                wait(pe, s_free[x % 2], x // 2)
                if item[0] == "n":
                    for c0 in (0, 512):
                        mm = pe.matmul(GF[x % 2][:, c0:c0 + 512], ident[0:HB, item[1]:item[1] + 1].to_broadcast([HB, P]),
                                       GB[:, c0:c0 + 512], start=True, stop=True)
                    mm.then_inc(s_done, 1)
                    continue
                elif item[0] == "s":
                    scores(x, item[1], item[2])
                else:
                    j = item[1]
                    if x == len(ORDER) - 1:
                        turns(*late[1])
                        results(*late[0])
                        results(*late[1])
                    pe.wait_ge(o_sbuf, (2 * j + 2) * NB)
                    for qb in range(NB):
                        mm = pe.transpose(GF[x % 2][:, qb * P:(qb + 1) * P], OT[:, qb], ident)
                    mm.then_inc(s_done, 1)
                    continue
                if late:
                    turns(*late[-1])
                if len(late) == 2:
                    results(*late.pop(0))
                late.append((item[1], item[2], item[1] * NB + item[2]))

            value_sum(B - 1)

            pe.wait_ge(ssum, 1)
            pe.wait_ge(qk_new, 1)
            pe.matmul(M0[:, 0:B * HB], ones, RSS[:].rearrange("p b h -> p (b h)"), start=True, stop=True)
            pe.matmul(M0[:, 64:96], CON[:, C_BLK], SM[:, 0], start=True, stop=True)
            for c in range(NW):
                mm = pe.matmul(M0[:, 96 + c * B:96 + (c + 1) * B], SELC[:, c], GA[:, TP:T], start=True, stop=True)
            mm.then_inc(fin_psum, 1)

            pe.wait_ge(back_lo, NW + 1)
            pe.wait_ge(sfeat, 1)
            for s in range(2):
                pe.wait_ge(s_free[s], (len(ORDER) + 1 - s) // 2)
            for m in range(ND):
                plain_unit(U_OE + m, T_OE + m)

            def mlp(layer):
                tb, ub = T_F[layer], U_F[layer]
                norm(2 * layer + 1)

                def down(t, u, plus, hid):
                    pe.wait_ge(hid_lo, hid)
                    for m in range(ND):
                        tt = t + m
                        pe.wait_ge(tile_free[tt % 2], plus(tt // 2))
                        for jj in range(2):
                            slot = (u + jj) % SLOTS
                            mm = passes(psum_tile(tt), WHI[:, slot, m * P:(m + 1) * P], WLO[:, slot, m * P:(m + 1) * P],
                                        HIDH[:, jj], HIDL[:, jj], jj == 0, jj == 1)
                        mm.then_inc(tile_done, 1)

                first_tiles(2 * layer + 1, [unit_tile(ub + r, tb + r) for r in range(2)])
                for r in range(2, 4):
                    plain_unit(ub + r, tb + r)
                with pe.Fori(0, FI - 1) as i:
                    for r in range(4):
                        t = tb + 4 + r
                        unit(ub + 4 + r, t, i * 6 + t // 2, i * 6 + (ub + 4 + r + 1))
                    pe.wait_ge(w_lo, i * 6 + (ub + 10))
                    down(tb + 8, ub + 8, lambda v: i * 6 + v, i * 2 + (layer * NF + 2))
                pe.wait_ge(w_lo, ub + 6 * FI)
                down(tb + 12 * FI - 8, ub + 6 * FI - 2, lambda v: v, (layer + 1) * NF)

            mlp(0)

            norm(2)
            first_tiles(2, [gate_tile(1, T_GO), unit_tile(U_IO, T_IO)])
            for u in range(20):
                t = T_IO + u if u < 16 else T_P[u - 16]
                if u:
                    plain_unit(U_IO + u, t)
                if u == 4:
                    pe.wait_ge(arow_ready, 1)
                    pe.wait_ge(sfeat, 1)
                    for ch in range(NB):
                        mm = pe.transpose(M0[:, ch * HC:(ch + 1) * HC], AROW[:, ch * P:(ch + 1) * P], ident[0:HC, 0:HC])
                    mm.then_inc(acol_psum, 1)
                    pe.wait_ge(acol_ready, 1)
                if 9 <= u <= 12:
                    values_turned(u - 9, 1)
                if u == 13:
                    pe.wait_ge(vt_sbuf, 4 * NW)
                    pe.wait_ge(vts_ready, 2 * NW)
                    for j in range(NW):
                        mm = pe.transpose(M0[0:B, j * P:(j + 1) * P], VTS[:, j], ident)
                    mm.then_inc(vrow_psum, 1)
                if u >= 17:
                    for g in ([u - 17] if u < 19 else [2, 3]):
                        t = T_PM[g]
                        pe.wait_ge(pz_ready, g + 1)
                        pe.wait_ge(tile_free[t % 2], t // 2)
                        for c in range(BANKS):
                            mm = pe.matmul(psum_tile(t)[:, c], PW[:, g], PZ[g % 2][:, c * TC:(c + 1) * TC],
                                           start=True, stop=True)
                        mm.then_inc(tile_done, 1)

            pe.wait_ge(vrow_sbuf, 1)
            pe.wait_ge(srows_ready, 1)
            for h in range(HC):
                mm = pe.matmul(M0[:, h * 3 * B:(h + 1) * 3 * B], ident[0:HC, h:h + 1].to_broadcast([HC, P]),
                               SROWS[:].rearrange("p k b -> p (k b)")[:, 0:3 * B], start=True, stop=True)
            mm.then_inc(srows_psum, 1)
            pe.wait_ge(sbc_ready, 1)
            pe.wait_ge(c_new, HC * B)
            pe.wait_ge(qn_ready, 1)
            pe.matmul(M0[:, 128:128 + HC * B], ones, SM[:, 2], start=True, stop=True)
            for s in range(HC * B):
                b, h = s // HC, s % HC
                mm = pe.matmul(M0[:, 192 + h * B + b:193 + h * B + b], C0[:, s], QT[:, h, TP + b:TP + b + 1],
                               start=True, stop=True)
            mm.then_inc(snum_psum, 1)

            for s in range(2):
                pe.wait_ge(tile_free[s], (T_OO + 1 - s) // 2)
            pe.wait_ge(mrow_ready, 1)

            def chunk_in(i):
                ch, h = divmod(i, HC)
                cols = slice(ch * P, (ch + 1) * P)
                wait(pe, xa_sbuf, i - 1)
                x = G[i % 2][:, 0]
                sel = ident[0:HC, h:h + 1].to_broadcast([HC, P])
                pe.matmul(x[:, 0:P], sel, MAXROW[:, cols], start=True, stop=True)
                pe.matmul(x[:, P:2 * P], sel, MROW[:, cols], start=True, stop=True)
                pe.matmul(x[:, 2 * P:3 * P], KT[:, h, cols], QT[:, h, cols], start=True, stop=True)
                pe.transpose(x[:, 3 * P:4 * P], KT[:, h, cols], ident).then_inc(xa_psum, 1)

            def chunk_out(i):
                ch, h = divmod(i, HC)
                y = G[i % 2][:, 1]
                v = VTOK[:, ch, h * DK:(h + 1) * DK]
                w = XW[i % 2]
                wait(pe, cst_ready, i - 3)
                wait(pe, hc_ready, i - 1)
                wait(pe, cst_ready, i - 1)
                pe.wait_ge(kw_ready, i + 1)
                pe.matmul(y[:, 0:P], v, w[:, P:2 * P], start=True, stop=False)
                pe.matmul(y[:, 0:P], CST[:, h, 0:DK], w[:, 2 * P:3 * P], start=False, stop=True)
                pe.matmul(y[:, P:2 * P], ones, w[:, P:2 * P], start=True, stop=False)
                pe.matmul(y[:, P:2 * P], CST[:, h, DK:DK + 1].to_broadcast([P, P]), w[:, 2 * P:3 * P],
                          start=False, stop=True)
                pe.matmul(y[:, 2 * P:3 * P], w[:, 3 * P:4 * P], v, start=True, stop=True)
                pe.matmul(y[:, 3 * P:3 * P + 1], w[:, 3 * P:4 * P], ones[:, 0:1], start=True, stop=True
                          ).then_inc(y_psum, 1)

            chunk_in(0)
            for i in range(HC * NB):
                if i + 1 < HC * NB:
                    chunk_in(i + 1)
                chunk_out(i)

            pe.wait_ge(hc_lo, NW)
            pe.wait_ge(back_lo, 2 * NW + 1)
            pe.wait_ge(hc_ready, HC * NB)
            pe.wait_ge(cst_ready, HC * NB)
            for m in range(ND):
                plain_unit(U_OO + m, T_OO + m)

            mlp(1)
            norm(4)

        @block.scalar
        def _(act):
            own = Own(act, own_act)
            A = nc.scalar.activation

            def load(u):
                if u < U_END:
                    wait(act, w_lo, u - SLOTS + 1)
                    act.dma_start(WRAW[:, u % SLOTS], a["w"][u]).then_inc(w_loaded[u % SLOTS], 16)

            def load_at(u, i):
                act.wait_ge(w_lo, i * 6 + (u - SLOTS + 1))
                act.dma_start(WRAW[:, u % SLOTS], a["w"][bass.ds(i * 6 + u, 1)].rearrange("a p f -> (a p) f")
                              ).then_inc(w_loaded[u % SLOTS], 16)

            def high(u):
                if u < U_END:
                    act.wait_ge(w_loaded[u % SLOTS], 16 * (u // SLOTS + 1))
                    if u >= SLOTS:
                        act.wait_ge(tile_done, last_tile(u - SLOTS) + 1)
                    A(WHI[:, u % SLOTS], WRAW[:, u % SLOTS], ACT.Copy).then_inc(w_hi, 1)

            def unit_used(u, deferred=()):
                high(u + SLOTS)
                if u + 5 not in deferred:
                    load(u + 5)

            def evacuate(out, t, func=ACT.Copy, rows=P, **kw):
                act.wait_ge(tile_done, t + 1)
                A(by3(out), psum_tile(t, rows), func, **kw).then_inc(tile_free[t % 2], 1)
                act.wait_ge(tile_free[t % 2], freed(t))

            def square(n, c):
                if n == 0:
                    act.wait_ge(x_in, 32)
                else:
                    act.wait_ge(tile_free[(T_X[n] + c) % 2], freed(T_X[n] + c))
                if c >= 3:
                    act.wait_ge(sq_summed, n * (ND - 1) + c - 2)
                A(ACC if c == 0 else SQ[c % 2], XT[:, c], ACT.Square).then_inc(sq_ready, 1)

            def norm(n, halves=True):
                t = T_N[n]
                for c in range(0 if n == 0 else ND - 1, ND):
                    square(n, c)
                act.wait_ge(tile_done, t + 1)
                A(by3(RSTD), psum_tile(t), ACT.Sqrt, bias=PRM[:, O_EPS:O_EPS + 1], scale=1.0 / D).then_inc(tile_free[t % 2], 1)
                if halves:
                    for c in range(ND):
                        act.wait_ge(h_raw, n * ND + c + 1)
                        A(HHI[:, c], HN[c % 4], ACT.Copy).then_inc(h_hi, 1)

            def values_turned(j, layer):
                for r in range(2):
                    n = (layer * NW + j) * 2 + r
                    act.wait_ge(vt_psum, n + 1)
                    A(VTOK[:, r * 4:r * 4 + 4, j * P:(j + 1) * P], M0[:].rearrange("p (q f) -> p q f", f=P),
                      ACT.Copy).then_inc(vt_sbuf, 1)

            for u in range(SLOTS):
                load(u)
            act.wait_ge(par_in, 16 * PAR_LOADS)
            A(GWH[:], GWR[:], ACT.Copy).then_inc(gw_hi, 1)
            for u in range(SLOTS):
                high(u)
            for u in range(SLOTS, 5):
                load(u)

            def forgets_turned(r):
                half, hq = r // 2, r % 2
                act.wait_ge(lt_psum, r + 1)
                A(LT[:, half, hq * 4:hq * 4 + 4], M0[:].rearrange("p (h g) -> p h g", g=P), ACT.Copy).then_inc(lt_sbuf, 1)

            def forgets_summed(r):
                half, hq = r // 2, r % 2
                act.wait_ge(bias_psum, r + 1)
                A(SCR[:, half * 4:half * 4 + 4, :, hq * 4:hq * 4 + 4].rearrange("p b g h -> p h (b g)"),
                  M1[:].rearrange("p (h g) -> p h g", g=P), ACT.Copy).then_inc(bias_sbuf, 1)

            norm(0)
            t = T_GE
            act.wait_ge(tile_done, t + 1)
            A(by3(GA[:]), psum_tile(t, HB), ACT.Identity, bias=PRM[0:HB, O_GB:O_GB + 1]).then_inc(tile_free[t % 2], 1)
            act.wait_ge(tile_free[t % 2], freed(t))

            def log_sigmoid(z, out):
                own.link(A(out, z, ACT.Abs))
                own.link(A(out, out, ACT.Exp, scale=-1.0))
                A(out, out, ACT.Ln, bias=ones[0:z.shape[0], 0:1]).then_inc(logsig_in, 1)

            log_sigmoid(GA[:], GB[:])

            def store_tmp(s, dst, done):
                act.dma_start(dst, TMP[s]).then_inc(done, 16)

            for u in range(24):
                t, j = T_IE + u, u % 4
                if u < 4:
                    evacuate(QT[:, j], t, scale=HD ** -0.5)
                elif u < 8:
                    evacuate(KT[:, j], t)
                    act.dma_start(o["k"][j], KT[:, j]).then_inc(act_outs, 16)
                elif u < 12:
                    if j >= 2:
                        act.wait_ge(tmp_out[j % 2], 16)
                    evacuate(TMP[j % 2], t)
                    A(VTS[:, j], TMP[j % 2][:, TP:T], ACT.Copy).then_inc(vts_ready, 1)
                    act.dma_start(o["v"][j], TMP[j % 2]).then_inc(tmp_out[j % 2], 16)
                elif (u - 12) % 3 == 0:
                    jc = (u - 12) // 3
                    if jc == 0:
                        act.wait_ge(tmp_out[0], 32)
                    else:
                        act.wait_ge(tile_free[(t - 2) % 2], freed(t - 2))
                    evacuate(TMP[0], t)
                elif (u - 12) % 3 == 2:
                    jc = (u - 12) // 3
                    act.wait_ge(tile_free[t % 2], freed(t))
                    act.dma_start(o["a_scr"][jc], TMP[1]).then_inc(a_saved, 16)
                if u == 4:
                    act.wait_ge(qrow_psum, 1)
                    A(SROW[:], M0[0:B], ACT.Copy).then_inc(qrow_sbuf, 1)
                unit_used(U_IE + u, deferred=(U_OE + 3, U_OE + 4))
                if u < 4:
                    forgets_turned(u)
                if 1 <= u < 5:
                    forgets_summed(u - 1)
                if 9 <= u <= 12:
                    values_turned(u - 9, 0)
                if u == 5:
                    act.wait_ge(logf_ready, 1)
                    act.dma_start(o["logf"], GA[:]).then_inc(act_outs, 16)
            act.wait_ge(fout_conv, NW)
            act.dma_start(o["conv_a"], FOUT[:, 0:NW]).then_inc(fconv_out, 16)

            act.wait_ge(sshift, 1)
            flat = SCR[:].rearrange("p b g h -> p (b g h)")
            A(flat, flat, ACT.Exp).then_inc(sprob, 1)

            rounds = [0]
            act.wait_ge(w_lo, U_OE + SLOTS)

            def turned(h, qb, k):
                for r in range(qb // 4 + 1):
                    n = rounds[0]
                    w = min(4, qb + 1 - 4 * r) * P
                    act.wait_ge(pt_psum, n + 1)
                    wait(act, o_done, k - 1)
                    A(PTS[k % 2][:, r * 512:r * 512 + w], G[n % 2][:, 2, 0:w], ACT.Copy).then_inc(pt_sbuf, 1)
                    rounds[0] = n + 1

            def result(h, qb, k):
                act.wait_ge(rsum_ready, k + 1)
                act.wait_ge(o_done, k + 1)
                if h >= 2 and h % 2 == 0:
                    act.wait_ge(s_done, ORDER.index(("t", h // 2 - 1)) + 1)
                A(OT[:, qb, (h % 2) * HD:(h % 2 + 1) * HD], M0[:, 0:HD], ACT.Copy, scale=FMX[:, 3, k % 4:k % 4 + 1]
                  ).then_inc(o_sbuf, 1)

            late = []
            for x, item in enumerate(ORDER):
                if item[0] == "n":
                    h = item[1]
                    wait(act, sc_ready, NB * (h - 1))
                    act.wait_ge(s_done, x + 1)
                    A(NEGF[h % 2], GF[x % 2][:, 0:TP], ACT.Copy).then_inc(s_free[x % 2], 1)
                    continue
                if item[0] == "s":
                    k = item[1] * NB + item[2]
                    n = (item[2] + 1) * P
                    act.wait_ge(sc_ready, k + 1)
                    wait(act, rsum_ready, k - 3)
                    A(SC[k % 2][:, 0:n], SC[k % 2][:, 0:n], ACT.Exp, bias=FMX[:, 1, k % 4:k % 4 + 1],
                      accum_out=FMX[:, 2, k % 4:k % 4 + 1]).then_inc(p_ready, 1)
                    if late:
                        turned(*late[-1])
                    if len(late) == 2:
                        result(*late.pop(0))
                    late.append((item[1], item[2], k))
                    continue
                j = item[1]
                if x == len(ORDER) - 1:
                    turned(*late[1])
                    result(*late[0])
                    result(*late[1])
                act.wait_ge(s_done, x + 1)
                A(HHI[:, NW + j, 0:TP], GF[x % 2][:, 0:TP], ACT.Copy).then_inc(att_hi, 1)
                act.wait_ge(a_saved, 16 * NW)
                act.dma_start(QT[:, j, 0:TP], o["a_scr"][j][:, 0:TP]).then_inc(back_in[j], 16)
                act.dma_start(AS[:, j], o["a_scr"][j][:, TP:T]).then_inc(back_in[j], 16)
                if j > 1:
                    act.wait_ge(back_in[j - 1], 32)
                    A(HHI[:, j - 1, 0:TP], QT[:, j - 1, 0:TP], ACT.Copy).then_inc(back_hi, 1)
            act.wait_ge(v_summed, B)
            for j in (0, NW - 1):
                act.wait_ge(back_in[j], 32)
                A(HHI[:, j, 0:TP], QT[:, j, 0:TP], ACT.Copy).then_inc(back_hi, 1)
            A(HHI[:, 0:NW, TP:T], AS[:], ACT.Copy).then_inc(back_hi, 1)
            act.wait_ge(o_done, HB * NB)
            act.wait_ge(att_hi, NW)
            load(U_OE + 3)
            load(U_OE + 4)

            act.wait_ge(fin_args, 1)
            A(SM[:, 6:8].rearrange("p k f -> p (k f)"), SM[:, 4:6].rearrange("p k f -> p (k f)"), ACT.Exp
              ).then_inc(fin_exp, 1)
            act.wait_ge(fin_att, 1)
            A(HHI[:, NW:ND, TP:T], SM[:, 10].rearrange("p (c b) -> p c b", c=NW), ACT.Copy).then_inc(fin_hi, 1)

            def project(u, t, n):
                for m in range(ND):
                    act.wait_ge(tile_done, t + m + 1)
                    unit_used(u + m)
                    if m:
                        square(n, m - 1)

            project(U_OE, T_OE, 1)

            def mlp(layer):
                tb, ub = T_F[layer], U_F[layer]
                norm(2 * layer + 1)

                def gate(jj, t, done, free, conv):
                    act.wait_ge(tile_done, done)
                    wait(act, conv_done, conv)
                    wait(act, fout_ready, conv)
                    A(by3(CV[jj][:, 2:2 + T]), psum_tile(t), ACT.Copy).then_inc(tile_free[t % 2], 1)

                def silu(jj, conv):
                    act.wait_ge(conv_done, conv)
                    A(CC[jj], CC[jj], ACT.Silu, bias=FPB[:, jj, 3:4]).then_inc(silu_done, 1)

                def hidden(jj, t, free, hid):
                    act.wait_ge(tile_free[t % 2], free)
                    A(HIDH[:, jj], HR[jj], ACT.Copy).then_inc(hid_hi, 1)

                c0 = layer * NF
                for jj in range(2):
                    t = tb + 2 * jj
                    gate(jj, t, t + 1, None, c0)
                    unit_used(ub + 2 * jj)
                    silu(jj, c0 + jj + 1)
                    act.wait_ge(tile_done, t + 2)
                    unit_used(ub + 2 * jj + 1)
                for jj in range(2):
                    t = tb + 2 * jj + 1
                    hidden(jj, t, freed(t), None)
                def step(i):
                    def used_at(u, done):
                        if isinstance(i, int):
                            act.wait_ge(tile_done, done)
                            return unit_used(u + 6 * i)
                        v = u + SLOTS
                        act.wait_ge(w_loaded[v % SLOTS], i * 32 + 16 * (v // SLOTS + 1))
                        act.wait_ge(tile_done, done)
                        A(WHI[:, v % SLOTS], WRAW[:, v % SLOTS], ACT.Copy).then_inc(w_hi, 1)
                        load_at(u + 5, i)

                    for jj in range(2):
                        t = tb + 4 + 2 * jj
                        gate(jj, t, i * 12 + (t + 1), None, i * 2 + (c0 + jj + 1))
                        used_at(ub + 4 + 2 * jj, i * 12 + (t + 1))
                        silu(jj, i * 2 + (c0 + 2 + jj + 1))
                        used_at(ub + 5 + 2 * jj, i * 12 + (t + 2))
                    for r in range(2):
                        used_at(ub + 8 + r, i * 12 + (tb + 16))
                    for jj in range(2):
                        t = tb + 5 + 2 * jj
                        hidden(jj, t, i * 6 + freed(t), None)

                with act.Fori(0, FI - 2) as i:
                    step(i)
                step(FI - 2)
                act.wait_ge(fout_ready, (layer + 1) * NF)
                for c in range(ND - 1):
                    square(2 * layer + 2, c)
                act.wait_ge(tile_done, tb + 12 * FI)
                for r in range(2):
                    unit_used(ub + 6 * FI - 2 + r)

            mlp(0)

            norm(2)
            t = T_GO
            act.wait_ge(tile_done, t + 1)
            A(by3(GA[:]), psum_tile(t, HB), ACT.Identity, bias=PRM[0:HB, O_GB + 1:O_GB + 2]).then_inc(tile_free[t % 2], 1)
            act.wait_ge(gmoved, 16)
            log_sigmoid(GB[0:HC, :], TROW)
            for u in range(20):
                t, j = (T_IO + u if u < 16 else T_P[u - 16]), u % 4
                if u < 4:
                    evacuate(QT[:, j], t)
                elif u < 8:
                    evacuate(KT[:, j], t, scale=DK ** -0.5)
                elif u < 12:
                    if u == 8:
                        act.wait_ge(x_saved, 16)
                    act.wait_ge(vt_psum, 2 * (NW + j - 1))
                    evacuate(TMP[j % 2], t)
                    A(VTS[:, j], TMP[j % 2][:, TP:T], ACT.Copy).then_inc(vts_ready, 1)
                elif u < 16:
                    if j < 2:
                        act.wait_ge(vt_psum, 2 * (NW + 3 + (j > 0)))
                    else:
                        act.wait_ge(tmp_out[j % 2], 48)
                    evacuate(TMP[j % 2], t, ACT.Sigmoid)
                    act.dma_start(o["o_scr"][j], TMP[j % 2]).then_inc(tmp_out[j % 2], 16)
                else:
                    if j == 0:
                        act.wait_ge(px_zero, 1)
                    else:
                        act.wait_ge(pz_ready, j)
                        act.wait_ge(pool_out, 32 * j)
                    evacuate(PX[:, PREV:PREV + T], t)
                    A(SX[:, :, PREV], PX[:, PREV + TP:PREV + T], ACT.Copy).then_inc(px_ready, 1)
                    act.wait_ge(px_ready, j + 1)
                    act.wait_ge(sx_ready, j + 1)
                    act.dma_start(o["pool_p"][j], PX[:, TP:TP + PREV]).then_inc(pool_out, 16)
                    act.dma_start(o["pool_s"][j], SX[:, :, 1:16]).then_inc(pool_out, 16)
                if u == 4:
                    act.wait_ge(acol_psum, 1)
                    A(ACOL[:].rearrange("p c h -> p (c h)"), M0[:, 0:NB * HC], ACT.Copy).then_inc(acol_ready, 1)
                unit_used(U_IO + u, deferred=(U_OO + 3, U_OO + 4))
                if 9 <= u <= 12:
                    values_turned(u - 9, 1)
                if u == 13:
                    act.wait_ge(vrow_psum, 1)
                    A(SROW[:], M0[0:B], ACT.Copy).then_inc(vrow_sbuf, 1)
                if u >= 17:
                    for g in ([u - 17] if u < 19 else [2, 3]):
                        t = T_PM[g]
                        act.wait_ge(tmp_out[g % 2], 64 if g < 2 else 80)
                        evacuate(TMP[g % 2], t, ACT.Identity, scale=PRM[:, O_PSCALE + g:O_PSCALE + g + 1])
                        act.dma_start(o["p_scr"][g], TMP[g % 2]).then_inc(tmp_out[g % 2], 16)

            act.wait_ge(sgate_args, 1)
            A(SROWS[:, 0:3].rearrange("p k b -> p (k b)"), SROWS[:, 4:7].rearrange("p k b -> p (k b)"), ACT.Exp
              ).then_inc(srows_ready, 1)
            act.wait_ge(srows_psum, 1)
            A(SBC[:].rearrange("p h k b -> p (h k b)"), M0[:, 0:HC * 3 * B], ACT.Copy).then_inc(sbc_ready, 1)

            def chunk_in(i):
                ch, h = divmod(i, HC)
                x, w, e = XA[i % 2], XW[i % 2], XE[i % 2]
                act.wait_ge(xa_psum, i + 1)
                wait(act, kw_ready, i - 1)
                wait(act, hc_ready, i - 1)
                A(x, G[i % 2][:, 0], ACT.Copy).then_inc(xa_sbuf, 1)
                act.wait_ge(xa_sbuf, i + 1)
                A(e[:, 0:P], x[:, 0:P], ACT.Exp, scale=-1.0, bias=APV[:, h:h + 1])
                A(e[:, P:2 * P], x[:, P:2 * P], ACT.Exp, scale=-1.0)
                A(WG[:, i % 2:i % 2 + 1], x[:, P - 1:P], ACT.Exp, scale=-1.0, bias=ACOL[:, ch, h:h + 1])
                act.wait_ge(wm_ready, i + 1)
                A(w[:, 0:P], w[:, 0:P], ACT.Exp, bias=ACOL[:, ch, h:h + 1]).then_inc(w_exp, 1)

            def chunk_out(i):
                act.wait_ge(y_psum, i + 1)
                A(XE[i % 2][:, 2 * P:3 * P], G[i % 2][:, 1, P:2 * P], ACT.Abs).then_inc(den_abs, 1)

            act.wait_ge(w_lo, U_OO + SLOTS)
            act.wait_ge(mrow_ready, 1)
            for i in range(HC * NB):
                if i >= 1:
                    wait(act, apv_ready, i - HC + 1)
                chunk_in(i)
                if i:
                    chunk_out(i - 1)
            chunk_out(HC * NB - 1)
            act.wait_ge(hc_ready, HC * NB)
            load(U_OO + 3)
            load(U_OO + 4)
            for c in range(NW):
                act.wait_ge(hc_gated, c + 1)
                A(HHI[:, c], HCT[:, c], ACT.Copy).then_inc(hc_hi, 1)
            act.wait_ge(pool_back, 16)
            for c in range(NW):
                A(HHI[:, NW + c], QT[:, c], ACT.Copy).then_inc(back_hi, 1)
            act.dma_start(o["m_p"], GB[0:HC, TP - 1:TP]).then_inc(act_outs, 16)
            act.dma_start(o["m_s"], SROWS[:, 3]).then_inc(act_outs, 16)
            act.wait_ge(qn_ready, 1)
            act.dma_start(o["n_s"], SM[:, 1]).then_inc(act_outs, 16)

            project(U_OO, T_OO, 3)
            mlp(1)
            norm(4, halves=False)

        @block.vector
        def _(dve):
            own = Own(dve, own_dve)
            TT, TS, STT = nc.vector.tensor_tensor, nc.vector.tensor_scalar, nc.vector.scalar_tensor_tensor

            def free(ins, t):
                ins.then_inc(tile_free[t % 2], 1)

            def add_square(n, c):
                dve.wait_ge(sq_ready, n * ND + c + 1)
                if c > 1:
                    dve.wait_ge(sq_summed, n * (ND - 1) + c - 1)
                TT(ACC, ACC, SQ[c % 2], ALU.add).then_inc(sq_summed, 1)

            def norm(n):
                t = T_N[n]
                for c in range(1 if n == 0 else ND - 1, ND):
                    add_square(n, c)
                dve.wait_ge(tile_free[t % 2], freed(t))
                own.link(nc.vector.reciprocal(RSTD, RSTD))

                def low(c):
                    dve.wait_ge(h_hi, n * ND + c + 1)
                    TT(HLO[:, c], HN[c % 4], HHI[:, c].bitcast(F32), ALU.subtract).then_inc(h_lo_dve, 1)

                for c in range(ND):
                    gain = PRM[:, GAINS[n] + c:GAINS[n] + c + 1]
                    if n == 4:
                        STT(out=XT[:, c], in0=XT[:, c], scalar=gain, in1=RSTD, op0=ALU.mult, op1=ALU.mult
                            ).then_inc(y_ready, 1)
                        continue
                    if c >= 4:
                        dve.wait_ge((h_lo_dve, h_lo_pool)[c % 2], n * (ND // 2) + (c - 4) // 2 + 1)
                    STT(out=HN[c % 4], in0=XT[:, c], scalar=gain, in1=RSTD, op0=ALU.mult, op1=ALU.mult
                        ).then_inc(h_raw, 1)
                    if c % 2:
                        low(c - 1)

            def key_group(g):
                b, slot = g // 8, g % 2
                if g < GROUPS:
                    if g == 0:
                        dve.wait_ge(bias_sbuf, 4)
                    dve.wait_ge(qb_loaded, 16 * (b + 1))
                    dve.wait_ge(kd_loaded[slot], 16 * KD * (g // 2 + 1))
                    ring = RING[:, slot, 0:KD]
                    TT(ring, ring, QB[:, b % 2:b % 2 + 1, :].to_broadcast([P, KD, NW * P]), ALU.mult
                       ).then_inc(kd_mul, 1)
                if g:
                    key_sums(g - 1, KD, PG, k_mul, kp_red)
                    dve.wait_ge(kp_red, g)
                    dve.wait_ge(kd_red, g)
                    q = g - 1
                    dst = SCR[:, q // 8, (q % 8) * PG:(q % 8 + 1) * PG]
                    TT(dst, dst, KTMP[:, q % 2], ALU.add).then_inc(k_added, 1)
                if g < GROUPS:
                    wait(dve, k_added, g - 1)
                    key_sums(g, 0, KD, kd_mul, kd_red)

            def key_sums(g, p0, p1, multiplied, summed):
                dve.wait_ge(multiplied, g + 1)
                nc.vector.tensor_reduce(KTMP[:, g % 2, p0:p1].rearrange("p g h -> p (g h)"),
                                        RING[:, g % 2, p0:p1].rearrange("p g (h d) -> p (g h) d", d=HD),
                                        AX.X, ALU.add).then_inc(summed, 1)

            dve.wait_ge(logf_in, 32)
            nc.vector.tensor_reduce(TOT[:], LG.rearrange("p s q h -> p s h q"), AX.X, ALU.add).then_inc(tot_ready, 1)

            dve.wait_ge(par_in, 16 * PAR_LOADS)
            norm(0)
            dve.wait_ge(logsig_in, 1)
            STT(out=GA[:], in0=GA[:], scalar=0.0, in1=GB[:], op0=ALU.min, op1=ALU.subtract).then_inc(logf_ready, 1)
            dve.wait_ge(logf_ready, 1)
            nc.vector.tensor_tensor_scan(GB[:, 0:TP], ones[0:HB, 0:1].to_broadcast([HB, TP]), GA[:, 0:TP], 0.0,
                                         ALU.mult, ALU.subtract).then_inc(fcum_ready, 1)

            def conv(cv, out, taps, state, step):
                s0, s1 = state[:, :, 0], state[:, :, 1]
                own.link(TS(out[:, 0:TP], cv[:, 0:TP], taps[0], None, ALU.mult))
                own.link(TS(out[:, TP:T], s0, taps[0], None, ALU.mult))
                own.link(STT(out=out[:, 0:TP], in0=cv[:, 1:TP + 1], scalar=taps[1], in1=out[:, 0:TP],
                             op0=ALU.mult, op1=ALU.add))
                own.link(STT(out=out[:, TP:T], in0=s1, scalar=taps[1], in1=out[:, TP:T], op0=ALU.mult, op1=ALU.add))
                ins = STT(out=out, in0=cv[:, 2:T + 2], scalar=taps[2], in1=out, op0=ALU.mult, op1=ALU.add)
                step(ins)

            key = [0]
            for u in range(24):
                t, jc, kind = T_IE + u, (u - 12) // 3, (u - 12) % 3
                for _ in range(K_PLAN.get(u, 0)):
                    key_group(key[0])
                    key[0] += 1
                if u >= 12 and kind == 1:
                    if jc == 0:
                        dve.wait_ge(tmp_out[1], 32)
                        dve.wait_ge(vt_psum, 2 * NW)
                        dve.wait_ge(cvx_zero, 1)
                    else:
                        dve.wait_ge(a_saved, 16 * jc)
                    dve.wait_ge(tile_free[(t - 1) % 2], freed(t - 1))
                    dve.wait_ge(tile_done, t + 1)
                    free(TT(by3(CVX[:, 2:2 + T]), psum_tile(t), by3(TMP[0]), ALU.mult), t)
                    dve.wait_ge(tile_free[t % 2], freed(t))
                    state = PRM[:, O_SCONVA + jc * 2 * B:O_SCONVA + (jc + 1) * 2 * B].rearrange("p (b r) -> p b r", r=2)
                    conv(CVX, TMP[1], [PRM[:, O_CONVA + jc * 3 + x:O_CONVA + jc * 3 + x + 1] for x in range(3)],
                         state, own.link)
                    nc.vector.tensor_copy(FOUT[:, jc, 0:2], CVX[:, TP:TP + 2])
                    FO = FOUT[:, jc, 2:].rearrange("p (b r) -> p b r", r=2)
                    nc.vector.tensor_copy(FO[:, :, 0], state[:, :, 1])
                    nc.vector.tensor_copy(FO[:, :, 1], CVX[:, TP + 2:T + 2]).then_inc(fout_conv, 1)
                if u >= 12 and kind == 2:
                    dve.wait_ge(tile_done, t + 1)
                    free(TT(by3(TMP[1]), psum_tile(t), by3(TMP[1]), ALU.mult), t)

            key_group(GROUPS)
            dve.wait_ge(k_added, GROUPS)

            nc.vector.tensor_reduce(MX[:], SCR[:].rearrange("p b g h -> p b h g"), AX.X, ALU.max).then_inc(smax_ready, 1)
            dve.wait_ge(smax_all, 1)
            TT(SCR[:], SCR[:], MXA[:].rearrange("p b (a h) -> p b a h", a=1).to_broadcast([P, B, PAGES, HB]),
               ALU.subtract).then_inc(sshift, 1)
            dve.wait_ge(sprob, 1)
            nc.vector.tensor_reduce(RSS[:], SCR[:].rearrange("p b g h -> p b h g"), AX.X, ALU.add).then_inc(ssum, 1)
            c4 = lambda k: SM[:, k].rearrange("p (c b) -> p c b", c=NW)
            TT(c4(0), QT[:, :, TP:T], KT[:, :, TP:T], ALU.mult).then_inc(qk_new, 1)

            def inverse(k):
                dve.wait_ge(p_ready, k + 1)
                wait(dve, o_sbuf, k - 3)
                nc.vector.reciprocal(FMX[:, 3, k % 4:k % 4 + 1], FMX[:, 2, k % 4:k % 4 + 1]).then_inc(rsum_ready, 1)

            values = values_of(dve, TT, slice_of_dve, 0, v_used_dve, own)
            dve.wait_ge(w_lo, U_OE + SLOTS)
            dve.wait_ge(a_saved, 16 * NW)
            for x, item in enumerate(ORDER):
                if item[0] == "n":
                    continue
                if item[0] == "s":
                    h, qb = item[1:]
                    k, n = h * NB + qb, (qb + 1) * P
                    if qb == 0:
                        xn = ORDER.index(("n", h))
                        dve.wait_ge(s_free[xn % 2], xn // 2 + 1)
                    if k >= 2:
                        dve.wait_ge(pt_psum, ROUNDS[k - 2])
                    dve.wait_ge(s_done, x + 1)
                    nc.vector.tensor_tensor_reduce(SC[k % 2][:, 0:n], GF[x % 2][:, 0:n], NEGF[h % 2][:, 0:n], 1.0,
                                                   -3.0e38, ALU.add, ALU.max, FMX[:, 0, k % 4:k % 4 + 1]
                                                   ).then_inc(s_free[x % 2], 1)
                    dve.wait_ge(s_free[x % 2], x // 2 + 1)
                    TS(FMX[:, 1, k % 4:k % 4 + 1], FMX[:, 0, k % 4:k % 4 + 1], -1.0, None, ALU.mult).then_inc(sc_ready, 1)
                    if k:
                        inverse(k - 1)
                    values(k)
                    continue
                j = item[1]
                if x == len(ORDER) - 1:
                    inverse(HB * NB - 1)
                dve.wait_ge(att_hi, j + 1)
                TT(HLO[:, NW + j, 0:TP], GF[x % 2][:, 0:TP], HHI[:, NW + j, 0:TP].bitcast(F32), ALU.subtract
                   ).then_inc(s_free[x % 2], 1)

            dve.wait_ge(vts_ready, NW)
            dve.wait_ge(fin_psum, 1)
            dve.wait_ge(v_summed, B)
            for par in range(2):
                r = slice(64 * par, 64 * par + 64)
                by_b = lambda v: v.rearrange("p b (c two) -> p c b two", two=2)[:, :, :, par]
                own.link(nc.vector.tensor_copy(c4(2)[r], by_b(MXA[r])))
                own.link(nc.vector.tensor_copy(c4(3)[r], by_b(M0[r, 0:64].rearrange("p (b h) -> p b h", b=B))))
            own.link(nc.vector.tensor_copy(c4(8), M1[:, 0:NW * B].rearrange("p (b c) -> p c b", b=B)))
            own.link(nc.vector.tensor_copy(SM[:, 9], M0[:, 96:128]))
            own.link(TT(SM[:, 1], M0[:, 64:96], SM[:, 9], ALU.subtract))
            own.link(TT(SM[:, 9], SM[:, 1], SM[:, 2], ALU.max))
            own.link(TT(SM[:, 4], SM[:, 2], SM[:, 9], ALU.subtract))
            TT(SM[:, 5], SM[:, 1], SM[:, 9], ALU.subtract).then_inc(fin_args, 1)
            dve.wait_ge(fin_exp, 1)
            own.link(TT(SM[:, 9], SM[:, 6], SM[:, 3], ALU.mult))
            own.link(TT(SM[:, 9], SM[:, 9], SM[:, 7], ALU.add))
            own.link(nc.vector.reciprocal(SM[:, 9], SM[:, 9]))
            own.link(TT(SM[:, 8], SM[:, 8], SM[:, 6], ALU.mult))
            own.link(TT(SM[:, 10], VTS[:].rearrange("p c b -> p (c b)"), SM[:, 7], ALU.mult))
            own.link(TT(SM[:, 8], SM[:, 8], SM[:, 10], ALU.add))
            TT(SM[:, 10], SM[:, 8], SM[:, 9], ALU.mult).then_inc(fin_att, 1)
            dve.wait_ge(fin_att, 1)
            dve.wait_ge(fin_hi, 1)
            TT(HLO[:, NW:ND, TP:T], c4(10), HHI[:, NW:ND, TP:T].bitcast(F32), ALU.subtract).then_inc(sfeat, 1)

            def add_tile(t, m, n):
                free(TT(by3(XT[:, m]), by3(XT[:, m]), psum_tile(t + m), ALU.add), t + m)
                if n and m >= 2:
                    add_square(n, m - 1)

            def residual(t, loads, n):
                dve.wait_ge(x_in, loads)
                for m in range(ND):
                    dve.wait_ge(tile_done, t + m + 1)
                    add_tile(t, m, n)

            residual(T_OE, 64, 1)

            def mlp(layer):
                tb, n0 = T_F[layer], layer * NF
                norm(2 * layer + 1)

                def up(jj, t, gate_free, fpb, up_done, silu, hid):
                    dve.wait_ge(cv_zero, layer + 1)
                    dve.wait_ge(fpb_ready, fpb)
                    dve.wait_ge(tile_free[t % 2], gate_free)
                    state = FPB[:, jj, 4:].rearrange("p (b r) -> p b r", r=2)
                    conv(CV[jj], CC[jj], [FPB[:, jj, x:x + 1] for x in range(3)], state,
                         lambda ins: ins.then_inc(conv_done, 1))
                    dve.wait_ge(silu_done, silu)
                    dve.wait_ge(tile_done, up_done)
                    wait(dve, hid_lo, hid)
                    free(TT(by3(HR[jj]), psum_tile(t + 1), by3(CC[jj]), ALU.mult), t + 1)

                def down(t, done, n=None):
                    for m in range(ND):
                        dve.wait_ge(tile_done, done(m))
                        add_tile(t, m, n)

                for jj in range(2):
                    t = tb + 2 * jj
                    up(jj, t, freed(t), layer * FI + 1, t + 2, n0 + jj + 1, n0)
                with dve.Fori(0, FI - 1) as i:
                    own.enter(i, 8)
                    for jj in range(2):
                        t = tb + 4 + 2 * jj
                        up(jj, t, i * 6 + freed(t), i + (layer * FI + 2), i * 12 + (t + 2), i * 2 + (n0 + jj + 3),
                           i * 2 + (n0 + jj + 1))
                    down(tb + 8, lambda m: i * 12 + (tb + 9 + m))
                own.leave(FI - 1)
                t = tb + 12 * FI - 8
                down(t, lambda m: t + m + 1, 2 * layer + 2)

            mlp(0)

            norm(2)
            dve.wait_ge(logsig_in, 2)
            own.link(STT(out=GB[0:HC, :], in0=GB[0:HC, :], scalar=0.0, in1=TROW, op0=ALU.min, op1=ALU.subtract))
            one_row = ones[0:HC, 0:1].to_broadcast([HC, TP])
            own.link(nc.vector.tensor_tensor_scan(BROW, one_row, GB[0:HC, 0:TP], 0.0, ALU.mult, ALU.add))
            TT(AROW, AROW, BROW, ALU.subtract).then_inc(arow_ready, 1)
            dve.wait_ge(arow_ready, 1)
            own.link(nc.vector.tensor_tensor_scan(MAXROW, one_row, AROW, 0.0, ALU.mult, ALU.max))
            own.link(TT(MROW, BROW, MAXROW, ALU.add))
            m0 = PRM[0:HC, O_M0:O_M0 + B]
            li, lf = GA[0:HC, TP:T], GB[0:HC, TP:T]
            own.link(TT(SROWS[:, 4], lf, m0, ALU.add))
            own.link(TT(SROWS[:, 3], SROWS[:, 4], li, ALU.max))
            own.link(TT(SROWS[:, 4], SROWS[:, 4], SROWS[:, 3], ALU.subtract))
            own.link(TT(SROWS[:, 5], li, SROWS[:, 3], ALU.subtract))
            TS(SROWS[:, 6], SROWS[:, 3], -1.0, None, ALU.mult).then_inc(sgate_args, 1)
            nc.vector.memset(APV[:], 0.0)
            nc.vector.memset(CST[:], 0.0).then_inc(mrow_ready, 1)
            dve.wait_ge(mrow_ready, 1)

            for g, win in enumerate(WINS):
                t = T_P[g]
                if g >= 2:
                    dve.wait_ge(tile_done, T_PM[g - 2] + 1)
                dve.wait_ge(px_ready, g + 1)
                dve.wait_ge(sx_ready, g + 1)
                src, lo = PX, 0
                for lev in range(g + 1):
                    s = 1 << lev
                    lo += s
                    dst = PD[lev % 2]
                    own.link(TT(dst[:, lo:PREV + TP], src[:, lo:PREV + TP], src[:, lo - s:PREV + TP - s], ALU.add))
                    src = dst
                z = PZ[g % 2]
                own.link(STT(out=z[:, 0:TP], in0=src[:, PREV:PREV + TP], scalar=1.0 / win, in1=PX[:, PREV:PREV + TP],
                             op0=ALU.mult, op1=ALU.subtract))
                own.link(TT(z[:, 0:PREV], src[:, PREV:2 * PREV], PRM[:, O_RCP + g * PREV:O_RCP + (g + 1) * PREV], ALU.mult))
                own.link(TT(z[:, 0:PREV], z[:, 0:PREV], PX[:, PREV:2 * PREV], ALU.subtract))
                own.link(nc.vector.tensor_reduce(SXS[:], SX[:, :, 16 - win:16], AX.X, ALU.add))
                STT(out=z[:, TP:T], in0=SXS[:], scalar=1.0 / win, in1=SX[:, :, PREV], op0=ALU.mult, op1=ALU.subtract
                    ).then_inc(pz_ready, 1)

            dve.wait_ge(sbc_ready, 1)
            hb = lambda k: SM[:, k].rearrange("p (h b) -> p h b", h=HC)
            n0v = PRM[:, O_N0:O_N0 + HC * B].rearrange("p (h b) -> p h b", h=HC)
            own.link(TT(hb(0), KT[:, :, TP:T], SBC[:, :, 1], ALU.mult))
            own.link(TT(hb(1), n0v, SBC[:, :, 0], ALU.mult))
            own.link(TT(hb(1), hb(1), hb(0), ALU.add))
            TT(hb(2), hb(1), QT[:, :, TP:T], ALU.mult).then_inc(qn_ready, 1)
            dve.wait_ge(c0_in, 16)
            dve.wait_ge(vb_in, 16 * B)
            for s in range(HC * B):
                b, h = divmod(s, HC)
                own.link(TS(C0[:, s], C0[:, s], SBC[:, h, 0, b:b + 1], None, ALU.mult))
                STT(out=C0[:, s], in0=VB[:, b, h * DK:(h + 1) * DK], scalar=SM[:, 0, h * B + b:h * B + b + 1],
                    in1=C0[:, s], op0=ALU.mult, op1=ALU.add).then_inc(c_new, 1)
            dve.wait_ge(snum_psum, 1)
            own.link(nc.vector.tensor_copy(SM[:, 3], M0[:, 192:224]))
            own.link(nc.vector.tensor_copy(SM[:, 4], M0[:, 128:160]))
            own.link(STT(out=SM[:, 5], in0=SM[:, 4], scalar=-1.0, in1=SM[:, 4], op0=ALU.mult, op1=ALU.max))
            own.link(TT(hb(4), hb(5), SBC[:, :, 2], ALU.max))
            own.link(nc.vector.reciprocal(SM[:, 4], SM[:, 4]))
            dve.wait_ge(c_new, HC * B)
            TT(HCT[:, :, TP:T], hb(3), hb(4), ALU.mult).then_inc(hcs_ready, 1)

            def chunk_in(i):
                ch, h = divmod(i, HC)
                x, w, e = XA[i % 2], XW[i % 2], XE[i % 2]
                wait(dve, y_psum, i - 1)
                dve.wait_ge(xa_sbuf, i + 1)
                STT(out=w[:, 0:P], in0=x[:, 0:P], scalar=-1.0, in1=CON[:, C_MASKT], op0=ALU.mult, op1=ALU.add
                    ).then_inc(wm_ready, 1)
                dve.wait_ge(w_exp, i + 1)
                nc.vector.tensor_copy(APV[:, h:h + 1], x[:, P - 1:P]).then_inc(apv_ready, 1)
                TT(w[:, P:2 * P], x[:, 2 * P:3 * P], w[:, 0:P], ALU.mult)
                TT(w[:, 2 * P:3 * P], QT[:, h, ch * P:(ch + 1) * P], e[:, 0:P], ALU.mult)
                TS(w[:, 3 * P:4 * P], x[:, 3 * P:4 * P], WG[:, i % 2:i % 2 + 1], None, ALU.mult).then_inc(kw_ready, 1)

            def chunk_out(i):
                ch, h = divmod(i, HC)
                y, e = G[i % 2][:, 1], XE[i % 2]
                dve.wait_ge(den_abs, i + 1)
                STT(out=CST[:, h], in0=CST[:, h], scalar=e[:, P - 1:P], in1=y[:, 2 * P:3 * P + 1], op0=ALU.mult,
                    op1=ALU.add).then_inc(cst_ready, 1)
                own.link(TT(e[:, 2 * P:3 * P], e[:, 2 * P:3 * P], e[:, P:2 * P], ALU.max))
                own.link(nc.vector.reciprocal(e[:, 2 * P:3 * P], e[:, 2 * P:3 * P]))
                TT(HCT[:, h, ch * P:(ch + 1) * P], y[:, 0:P], e[:, 2 * P:3 * P], ALU.mult).then_inc(hc_ready, 1)

            for i in range(HC * NB):
                chunk_in(i)
                if i:
                    chunk_out(i - 1)
            chunk_out(HC * NB - 1)
            dve.wait_ge(og_in, 16)
            dve.wait_ge(hcs_ready, 1)
            dve.wait_ge(hc_ready, HC * NB)
            for c in range(NW):
                TT(HCT[:, c], HCT[:, c], XT[:, c], ALU.mult).then_inc(hc_gated, 1)
            for c in range(NW):
                dve.wait_ge(hc_gated, c + 1)
                dve.wait_ge(hc_hi, c + 1)
                TT(HLO[:, c], HCT[:, c], HHI[:, c].bitcast(F32), ALU.subtract).then_inc(hc_lo, 1)

            residual(T_OO, 80, 3)
            mlp(1)
            norm(4)

        @block.gpsimd
        def _(pool):
            TT = nc.gpsimd.tensor_tensor

            def low(u, value=None):
                if u < U_END or value is not None:
                    pool.wait_ge(w_hi, u + 1 if value is None else value)
                    s = u % SLOTS
                    TT(WLO[:, s], WRAW[:, s], WHI[:, s].bitcast(F32), ALU.subtract).then_inc(w_lo, 1)

            def norm(n):
                for c in range(1, ND, 2):
                    pool.wait_ge(h_hi, n * ND + c + 1)
                    TT(HLO[:, c], HN[c % 4], HHI[:, c].bitcast(F32), ALU.subtract).then_inc(h_lo_pool, 1)

            pool.dma_start(PTI[:], a["pti"]).then_inc(pages_in_pool, 16)
            pool.wait_ge(pages_in_pool, 16)
            for s in range(2):
                pool.indirect_dma_start(out=VF[:, s * 1024:(s + 1) * 1024], out_offset=None, in_=a["clf"],
                                        in_offset=bass.IndirectOffsetOnAxis(ap=PTI[:, s:s + 1], axis=0),
                                        ).then_inc(logf_in, 16)
            pool.wait_ge(gw_hi, 1)
            TT(GWL[:], GWR[:], GWH[:].bitcast(F32), ALU.subtract).then_inc(gw_lo, 1)
            for u in range(SLOTS):
                low(u)
            norm(0)
            pool.wait_ge(h_raw, ND)
            nc.gpsimd.memset(CVX[:, 0:2], 0.0).then_inc(cvx_zero, 1)

            key = [0]
            for u in range(24):
                for _ in range(K_PLAN.get(u, 0)):
                    g = key[0]
                    b, slot = g // 8, g % 2
                    pool.wait_ge(qb_loaded, 16 * (b + 1))
                    pool.wait_ge(kp_loaded[slot], 16 * (PG - KD) * (g // 2 + 1))
                    ring = RING[:, slot, KD:PG]
                    TT(ring, ring, QB[:, b % 2:b % 2 + 1, :].to_broadcast([P, PG - KD, NW * P]), ALU.mult).then_inc(k_mul, 1)
                    key[0] += 1
                low(U_IE + u + SLOTS)

            pool.wait_ge(smax_ready, 1)
            nc.gpsimd.partition_all_reduce(MXA[:].rearrange("p b h -> p (b h)"), MX[:].rearrange("p b h -> p (b h)"),
                                           P, RMAX).then_inc(smax_all, 1)

            own = Own(pool, own_pool)
            values = values_of(pool, TT, slice_of_pool, 1, v_used_pool, own)
            for g in range(GROUPS):
                values(g)
            pool.wait_ge(v_used_dve, GROUPS)
            if True:
                for n, j in enumerate((1, 2, 0, 3)):
                    pool.wait_ge(back_hi, n + 1)
                    TT(HLO[:, j, 0:TP], QT[:, j, 0:TP], HHI[:, j, 0:TP].bitcast(F32), ALU.subtract
                       ).then_inc(back_lo, 1)
            pool.wait_ge(back_hi, NW + 1)
            TT(HLO[:, 0:NW, TP:T], AS[:], HHI[:, 0:NW, TP:T].bitcast(F32), ALU.subtract).then_inc(back_lo, 1)

            for m in range(ND):
                low(U_OE + m + SLOTS)

            def mlp(layer):
                ub, n0 = U_F[layer], layer * NF
                norm(2 * layer + 1)
                pool.wait_ge(sq_summed, (2 * layer + 2) * (ND - 1))
                pool.wait_ge(tile_done, T_N[2 * layer + 1] + 1)
                nc.gpsimd.memset(CV[0][:, 0:2], 0.0)
                nc.gpsimd.memset(CV[1][:, 0:2], 0.0).then_inc(cv_zero, 1)
                pool.wait_ge(fpar_in, 16 * (layer + 1))
                if layer == 0:
                    pool.wait_ge(fconv_out, 16)
                else:
                    pool.wait_ge(outs, 16)

                def params(i, silu):
                    wait(pool, silu_done, silu)
                    wait(pool, fout_ready, silu)
                    src = FPRM[:, bass.ds(i * 2, 2)]
                    nc.gpsimd.tensor_copy(FPB[:], src).then_inc(fpb_ready, 1)

                def states(i, jj, free, fpb):
                    t = T_F[layer] + 2 * jj
                    pool.wait_ge(tile_free[t % 2], free)
                    pool.wait_ge(fpb_ready, fpb)
                    dst = FOUT[:, bass.ds(i * 2 + jj, 1)].rearrange("p a f -> p (a f)")
                    nc.gpsimd.tensor_copy(dst[:, 0:2], CV[jj][:, TP:TP + 2])
                    pairs = dst[:, 2:].rearrange("p (b r) -> p b r", r=2)
                    nc.gpsimd.tensor_copy(pairs[:, :, 0], FPB[:, jj, 4:].rearrange("p (b r) -> p b r", r=2)[:, :, 1])
                    nc.gpsimd.tensor_copy(pairs[:, :, 1], CV[jj][:, TP + 2:T + 2]).then_inc(fout_ready, 1)

                def hidden(jj, hi):
                    pool.wait_ge(hid_hi, hi)
                    TT(HIDL[:, jj], HR[jj], HIDH[:, jj].bitcast(F32), ALU.subtract).then_inc(hid_lo, 1)

                params(0, n0)
                for jj in range(2):
                    t = T_F[layer] + 2 * jj
                    low(ub + 2 * jj + SLOTS)
                    states(0, jj, freed(t), layer * FI + 1)
                    low(ub + 2 * jj + 1 + SLOTS)
                for jj in range(2):
                    hidden(jj, n0 + jj + 1)
                def step(i):
                    def low_at(u):
                        low(u + 6 * i) if isinstance(i, int) else low(u, i * 6 + (u + 1))

                    params(i + 1, i * 2 + (n0 + 2))
                    for jj in range(2):
                        t = T_F[layer] + 4 + 2 * jj
                        u = ub + 4 + 2 * jj + SLOTS
                        low_at(u)
                        states(i + 1, jj, i * 6 + freed(t), i + (layer * FI + 2))
                        low_at(u + 1)
                    for r in range(2):
                        low_at(ub + 8 + r + SLOTS)
                    for jj in range(2):
                        hidden(jj, i * 2 + (n0 + jj + 3))

                with pool.Fori(0, FI - 2) as i:
                    step(i)
                step(FI - 2)
                for r in range(2):
                    low(ub + 6 * FI - 2 + r + SLOTS)

            mlp(0)
            norm(2)

            for u in range(20):
                if u >= 16:
                    j = u - 16
                    if j == 0:
                        pool.wait_ge(x_saved, 16)
                        pool.wait_ge(spool_in, 16)
                        nc.gpsimd.memset(PX[:, 0:PREV], 0.0).then_inc(px_zero, 1)
                    else:
                        pool.wait_ge(pz_ready, j)
                        pool.wait_ge(pool_out, 32 * j)
                    nc.gpsimd.tensor_copy(SX[:, :, 0:PREV], SPOOL[:, j]).then_inc(sx_ready, 1)
                low(U_IO + u + SLOTS)
            for c in range(NW):
                pool.wait_ge(back_hi, NW + 1 + c + 1)
                TT(HLO[:, NW + c], QT[:, c], HHI[:, NW + c].bitcast(F32), ALU.subtract).then_inc(back_lo, 1)
            for m in range(ND):
                low(U_OO + m + SLOTS)
            mlp(1)
            assert key[0] == GROUPS


_SCRATCH = {"q_scr": (B, NW * P), "v_scr": (B, NW * P), "a_scr": (NW, P, T), "o_scr": (NW, P, T),
            "p_scr": (NW, P, T), "x_scr": (P, ND, T)}
_OUTS = {"y": (ND, P, T), "k": (NW, P, T), "v": (NW, P, T), "logf": (HB, T), "conv_a": (P, NW, 2 + 2 * B),
         "c_p": (P, HC, DK + 1), "c_s": (P, HC * B, DK), "n_s": (P, HC * B), "m_p": (HC, 1), "m_s": (HC, B),
         "pool_p": (NW, P, PREV), "pool_s": (NW, P, B, PREV), "ffn": (2, P, NF, 2 + 2 * B)}


def _chunks(x):
    return np.ascontiguousarray(np.moveaxis(x.reshape((-1, P) + x.shape[1:]), 0, 1))


def _units(w):
    n = w.shape[1] // P
    return w.reshape(ND, P, n, P).transpose(2, 1, 0, 3).reshape(n, P, UNIT)


def _mlp_units(w_up, w_down):
    up, down = _units(w_up), w_down.reshape(NF, P, UNIT)
    out = []
    for i in range(FI + 1):
        if i < FI:
            for j in (2 * i, 2 * i + 1):
                out += [up[j], up[NF + j]]
        if i:
            out += [down[2 * i - 2], down[2 * i - 1]]
    return np.stack(out)


def _weights(x):
    we, wo = x["w_in_even"][0], x["w_in_odd"][0]
    a, w, k = 512, _units(we[:, 0:6 * 512]), 4
    conv = [w[g * k + j] for j in range(k) for g in (0, 2, 1)]
    odd = np.concatenate([wo[:, 0:4 * a], wo[:, 4 * a + 2 * HC:]], axis=1)
    return np.concatenate([w[3 * k:], np.stack(conv), _units(x["w_out_even"][0]), _mlp_units(x["w_up"][0], x["w_down"][0]),
                           _units(odd), _units(x["w_out_odd"][0]), _mlp_units(x["w_up"][1], x["w_down"][1])])


def _params(x):
    p = np.zeros((P, O_END), np.float32)
    for n in range(2):
        p[:, O_GMIX + n * ND:O_GMIX + (n + 1) * ND] = _chunks(x["norm_mix"][n])
        p[:, O_GFFN + n * ND:O_GFFN + (n + 1) * ND] = _chunks(x["norm_ffn"][n])
    p[:, O_GFIN:O_GFIN + ND] = _chunks(x["norm_final"])
    p[:, O_CONVA:O_CONVA + NW * 3] = _chunks(x["conv_a"][0].T).reshape(P, -1)
    p[:, O_PSCALE:O_PSCALE + NW] = _chunks(x["pool_scale_odd"][0])
    p[0:HB, O_GB] = x["b_forget_even"][0]
    p[0:HC, O_GB + 1] = x["b_igate_odd"][0]
    p[HC:2 * HC, O_GB + 1] = x["b_fgate_odd"][0]
    p[:, O_SCONVA:O_SCONVA + NW * B * 2] = _chunks(x["state_conv_a"][0].transpose(2, 0, 1)).reshape(P, -1)
    for g, win in enumerate(WINS):
        for t in range(PREV):
            p[:, O_RCP + g * PREV + t] = 1.0 / min(win, t + 1)
    p[:, O_N0:O_N0 + HC * B] = x["state_mlstm_n"][0].transpose(2, 1, 0).reshape(P, -1)
    p[0:HC, O_M0:O_M0 + B] = x["state_mlstm_m"][0].T
    p[:, O_EPS] = EPS
    return p


def _mlp_params(x):
    taps = x["ffn_conv_w"].transpose(0, 2, 1)
    bias = x["ffn_conv_b"][:, :, None]
    state = x["state_ffn_conv"].transpose(0, 3, 1, 2).reshape(2, FF, 2 * B)
    return np.stack([_chunks(np.concatenate([taps[n], bias[n], state[n]], axis=1)) for n in range(2)])


def _constants():
    i = np.arange(P)
    c = np.zeros((P, NCON, P), np.float32)
    c[:, C_ID] = np.eye(P)
    c[:, C_ONE] = 1.0
    c[:, C_MASK] = np.where(i[None, :] > i[:, None], NEG, 0.0)
    c[:, C_MASKT] = np.where(i[:, None] > i[None, :], NEG, 0.0)
    c[:, C_LATER] = i[:, None] > i[None, :]
    same = i[:, None] // PAGES == i[None, :] // PAGES
    c[:, C_PLATER] = same & (i[:, None] > i[None, :])
    c[:, C_BLK] = i[:, None] // HD == i[None, :] // HD
    s = np.zeros((HB, NW, P), np.float32)
    for h in range(HB):
        s[h, h // 2, (h % 2) * HD:(h % 2 + 1) * HD] = 1.0
    return c, s


def kernel(**inputs):
    import concourse.bacc as bacc
    from concourse.bass_utils import run_bass_kernel_spmd

    x = {k: np.asarray(v) for k, v in inputs.items()}
    con, selc = _constants()
    gw = np.stack([_chunks(x["w_in_even"][0][:, 3072:3080]), _chunks(x["w_in_odd"][0][:, 2048:2056])], axis=1)
    phys = x["cache_k"].shape[1]
    arrays = {
        "xp": _chunks(x["x_prompt"][0].T), "xs": _chunks(x["x_sample"][:, 0].T),
        "ck": x["cache_k"].reshape(phys, P, 512), "cv": x["cache_v"].reshape(phys, P, 512),
        "clf": x["cache_logf"].reshape(phys, P * HB), "pt": x["page_table"].reshape(1, -1),
        "pti": x["page_table"].reshape(2, P).T, "w": _weights(x), "gw": gw, "prm": _params(x),
        "fprm": _mlp_params(x), "con": con, "selc": selc, "pw": x["w_pool_odd"][0].transpose(1, 0, 2),
        "c0": x["state_mlstm_c"][0].transpose(2, 0, 1, 3).reshape(P, HC * B, DK),
        "spool": _chunks(x["state_pool"][0].transpose(2, 0, 1)),
    }
    arrays = {k: np.ascontiguousarray(v) for k, v in arrays.items()}
    nc = bacc.Bacc("TRN2", target_bir_lowering=False, num_devices=1, dynamic_dma_scratch_size=2048)
    ins = {k: nc.dram_tensor(f"in_{k}", v.shape, mybir.dt.from_np(v.dtype), kind="ExternalInput").ap()
           for k, v in arrays.items()}
    outs = {k: nc.dram_tensor(f"out_{k}", s, F32, kind="ExternalOutput").ap() for k, s in _OUTS.items()}
    outs |= {k: nc.dram_tensor(k, s, F32, kind="Internal").ap() for k, s in _SCRATCH.items()}
    trunk(nc, ins, outs)
    r = run_bass_kernel_spmd(nc, [{f"in_{k}": v for k, v in arrays.items()}], core_ids=[0]).results[0]
    g = {k: np.asarray(r[f"out_{k}"]).reshape(s) for k, s in _OUTS.items()}

    def tokens(v):
        v = v.reshape(-1, T).T
        return v[:TP], v[TP:]

    yp, ys = tokens(g["y"])
    kp, ks = tokens(g["k"])
    vp, vs = tokens(g["v"])
    lp, ls = tokens(g["logf"])

    def states(v):
        v = v.transpose(2, 1, 0).reshape(2 + 2 * B, -1)
        return v[None, 0:2], v[2:].reshape(B, 2, -1)

    cp, cs = states(g["conv_a"])
    fp, fs = zip(*(states(g["ffn"][n]) for n in range(2)))
    c_p = g["c_p"].transpose(1, 0, 2)
    pool_p = g["pool_p"].reshape(512, PREV).T
    pool_s = g["pool_s"].reshape(512, B, PREV).transpose(1, 2, 0)
    out = (yp[None], ys[:, None],
           kp.reshape(1, 1, TP, HB, HD), ks.reshape(1, B, 1, HB, HD),
           vp.reshape(1, 1, TP, HB, HD), vs.reshape(1, B, 1, HB, HD),
           lp.reshape(1, 1, TP, HB), ls.reshape(1, B, 1, HB), cp[None], cs[None],
           c_p[None, None, :, :, 0:DK], g["c_s"].reshape(P, B, HC, DK).transpose(1, 2, 0, 3)[None],
           c_p[None, None, :, :, DK], g["n_s"].reshape(P, HC, B).transpose(2, 1, 0)[None],
           g["m_p"].reshape(1, 1, HC), g["m_s"].T[None],
           pool_p[None, None], pool_s[None], np.stack(fp), np.stack(fs))
    return tuple(np.ascontiguousarray(v) for v in out)
```

```python
from contextlib import ExitStack

import numpy as np

import concourse.bass as bass
from concourse import mybir

F32 = mybir.dt.float32
F32R = mybir.dt.float32r
I32 = mybir.dt.int32
ALU = mybir.AluOpType
ACT = mybir.ActivationFunctionType
AX = mybir.AxisListType
RMAX = bass.bass_isa.ReduceOp.max

P = 128
D = 1024
ND = D // P
TP = 1024
NB = TP // P
B = 8
T = TP + B
BANKS = 3
TC = T // BANKS
PAGES = 32
PG = 4
GROUPS = B * PAGES // PG
HB, HD = 8, 64
HC, DK = 4, 128
NW = 4
FF = 2816
NF = FF // P
FI = NF // 2
SLOTS = 3
UNIT = 1024
WINS = (2, 4, 8, 16)
PREV = 15
EPS = 1e-6
NEG = -1.0e30

O_GMIX, O_GFFN, O_GFIN = 0, 2 * ND, 4 * ND
O_CONVA = 5 * ND
O_PSCALE = O_CONVA + NW * 3
O_GB = O_PSCALE + NW
O_SCONVA = O_GB + 2
O_RCP = O_SCONVA + NW * B * 2
O_N0 = O_RCP + NW * PREV
O_M0 = O_N0 + HC * B
O_EPS = O_M0 + B
O_END = O_EPS + 1
FCH = 4 + 2 * B
C_ID, C_ONE, C_MASK, C_MASKT, C_LATER, C_PLATER, C_BLK = range(7)
NCON = 7
CVW = 2 + T + 6
PXW = PREV + T + 1

U_IE = 0
U_OE = U_IE + 24
U_F = (U_OE + 8, 0)
U_IO = U_F[0] + 6 * FI
U_OO = U_IO + 20
U_F = (U_F[0], U_OO + 8)
U_END = U_F[1] + 6 * FI
T_N0, T_GE, T_IE = 0, 1, 2
T_OE = T_IE + 24
T_N1 = T_OE + 8
T_F0 = T_N1 + 1
T_N2 = T_F0 + 12 * FI
T_GO = T_N2 + 1
T_IO = T_GO + 1
T_P = [T_IO + 16 + x for x in (0, 1, 3, 5)]
T_PM = [T_IO + 16 + x for x in (2, 4, 6, 7)]
T_OO = T_IO + 24
T_N3 = T_OO + 8
T_F1 = T_N3 + 1
T_N4 = T_F1 + 12 * FI
T_F = (T_F0, T_F1)
T_N = (T_N0, T_N1, T_N2, T_N3, T_N4)
GAINS = (O_GMIX, O_GFFN, O_GMIX + ND, O_GFFN + ND, O_GFIN)
T_X = (None, T_OE, T_N2 - 8, T_OO, T_N4 - 8)


def after_unit(n_in, u0, t0):
    return {u0 + j: t0 + j for j in range(n_in)}


LAST_TILE = {**after_unit(24, U_IE, T_IE), **after_unit(8, U_OE, T_OE), **after_unit(20, U_IO, T_IO),
             **after_unit(8, U_OO, T_OO)}
for _j in range(4):
    LAST_TILE[U_IO + 16 + _j] = T_P[_j]


def last_tile(u):
    if u in LAST_TILE:
        return LAST_TILE[u]
    layer = int(u >= U_F[1])
    v, t = u - U_F[layer], T_F[layer]
    if v < 4:
        return t + v
    i, r = divmod(v - 4, 6)
    if i == FI - 1:
        return t + 12 * FI - 1
    return t + 4 + 12 * i + (r if r < 4 else 11)


BLOCKS = (7, 0, 6, 1, 5, 2, 4, 3)
def attention_order():
    order = [("n", 0)]
    for h in range(HB):
        for step in range(NB):
            order.append(("s", h, step))
            if step == 5 and h + 1 < HB:
                order.append(("n", h + 1))
            if step == 1 and h % 2 == 0 and h:
                order.append(("t", h // 2 - 1))
    order.append(("t", HB // 2 - 1))
    return order


ORDER = attention_order()
ROUNDS = []
for _k in range(HB * NB):
    ROUNDS.append((ROUNDS[-1] if ROUNDS else 0) + BLOCKS[_k % NB] // 4 + 1)
PT_ROUNDS = ROUNDS[-1]
PAR_LOADS = 5
ACT_OUTS = 8
KD = 2
V_POOL = (2, 2)
K_PLAN = {u: (4 if u < 9 else 3) for u in range(5, 24)}
K_LATE = GROUPS - sum(K_PLAN.values())
EARLY = K_LATE + 1
VALUES = [max(0, -(-(_k + 1 - EARLY) * GROUPS // (HB * NB - EARLY))) for _k in range(HB * NB)]


def wait(eng, sem, value):
    if not isinstance(value, int) or value > 0:
        eng.wait_ge(sem, value)


class Own:

    def __init__(self, eng, sem):
        self.eng, self.sem, self.n = eng, sem, 0

    def link(self, ins):
        ins.then_inc(self.sem, 1)
        self.n = self.n + 1
        self.eng.wait_ge(self.sem, self.n)

    def enter(self, i, per):
        self.base, self.per, self.n = self.n, per, i * per + self.n
        self.start, self.made = self.n, 0

    def leave(self, times):
        self.n = self.base + self.per * times


def trunk(nc, a, o):
    with ExitStack() as ctx:
        E = ctx.enter_context

        def sb(name, shape, dt=F32):
            return E(nc.sbuf_tensor(name, shape, dt))

        def sem(name):
            return E(nc.semaphore(name))

        XT = sb("XT", [P, ND, T])
        with nc.sbuf_tensor("HF", [P, 2, ND * T], F32) as HF:
            pass
        HHI = sb("HHI", [P, ND, T], F32R)
        HLO = sb("HLO", [P, ND, T], F32R)
        WHI = sb("WHI", [P, SLOTS, UNIT], F32R)
        WLO = sb("WLO", [P, SLOTS, UNIT], F32R)
        WRAW = sb("WRAW", [P, SLOTS, UNIT])
        VTOK = sb("VTOK", [P, NB, NW * P])
        with nc.sbuf_tensor("KT", [P, NW, T], F32) as KT:
            pass
        KLO = sb("KLO", [P, NW, T], F32R)
        with nc.sbuf_tensor("QT", [P, NW, T], F32) as QT:
            pass
        with nc.sbuf_tensor("QLO", [P, NW, T], F32R) as QLO:
            pass
        HIDH = sb("HIDH", [P, 2, T], F32R)
        HIDL = sb("HIDL", [P, 2, T], F32R)
        SCR = sb("SCR", [P, B, PAGES, HB])
        QB = sb("QB", [P, 2, NW * P])
        with nc.sbuf_tensor("GA", [HB, T], F32) as GA:
            pass
        FHI = sb("FHI", [HB, T], F32R)
        with nc.sbuf_tensor("GB", [HB, T], F32) as GB:
            pass
        FLO = sb("FLO", [HB, T], F32R)
        PRM = sb("PRM", [P, O_END])
        FPRM = sb("FPRM", [P, NF, FCH])
        FPB = sb("FPB", [P, 2, FCH])
        FOUT = sb("FOUT", [P, NF, 2 + 2 * B])
        CON = sb("CON", [P, NCON, P])
        SELC = sb("SELC", [HB, NW, P])
        GWR = sb("GWR", [P, 2, ND, HB])
        GWH = sb("GWH", [P, 2, ND, HB], F32R)
        GWL = sb("GWL", [P, 2, ND, HB], F32R)
        PT = sb("PT", [1, B * PAGES], I32)
        PTI = sb("PTI", [P, 2], I32)
        TOT = sb("TOT", [P, 2, HB])
        KTMP = sb("KTMP", [P, 2, PG, HB])
        MX = sb("MX", [P, B, HB])
        MXA = sb("MXA", [P, B, HB])
        RSS = MX
        IMR = sb("IMR", [P, 2, P], F32R)
        SM = sb("SM", [P, 11, NW * B])
        VTS = sb("VTS", [P, NW, B])
        SROW = sb("SROW", [HB, NW * P])
        FMX = sb("FMX", [P, 4, 4])
        ACOL = sb("ACOL", [P, NB, HC])
        APV = sb("APV", [P, HC])
        WG = sb("WG", [P, 2])
        SROWS = sb("SROWS", [HC, 7, B])
        AS = sb("AS", [P, NW, B])
        SXS = sb("SXS", [P, B])
        PW = sb("PW", [P, NW, P])
        SBC = sb("SBC", [P, HC, 3, B])

        G = [E(nc.psum_tensor(f"G{s}", [P, BANKS, 512], F32)) for s in range(2)]
        M0 = E(nc.psum_tensor("M0", [P, 512], F32))
        M1 = E(nc.psum_tensor("M1", [P, 512], F32))

        XF = XT[:].rearrange("p c t -> p (c t)")
        KF = KT[:].rearrange("p c t -> p (c t)")
        VF = VTOK[:].rearrange("p c t -> p (c t)")
        GF = [g[:].rearrange("p a b -> p (a b)") for g in G]
        ident = CON[:, C_ID]
        ones = CON[:, C_ONE]
        RING = XF[:, 0:2 * PG * 512].rearrange("p (s g f) -> p s g f", s=2, g=PG)
        KDS = [RING[:, s, 0:KD] for s in range(2)]
        KPS = [RING[:, s, KD:PG] for s in range(2)] + [
            XF[:, 6 * T + CVW:6 * T + CVW + (PG - KD) * 512].rearrange("p (g f) -> p g f", f=512)]
        SQ = [KT[:, 0], KT[:, 1]]
        ACC, RSTD = KT[:, 2], KT[:, 3]
        HN = [QT[:, c] for c in range(4)]
        LG = VF[:, 0:2048].rearrange("p (s q h) -> p s q h", s=2, h=HB)
        LT = VF[:, 2048:4096].rearrange("p (s h g) -> p s h g", s=2, h=HB)
        TMP = [XT[:, 4], XT[:, 5]]
        CVX = XF[:, 6 * T:6 * T + CVW]
        NEGF = [XT[:, 4, 0:TP], XT[:, 7, 0:TP]]
        SC = [XT[:, 5], XT[:, 6]]
        PTS = [WRAW[:, 0], WRAW[:, 1]]
        OT = WRAW[:, 2].rearrange("p (q f) -> p q f", f=P)
        KHI = [HHI[:, NW + j] for j in range(NW)]
        QHI = [HLO[:, NW + j] for j in range(NW)]
        VSLOT = [RING[:, 0], RING[:, 1]] + [
            HF[:, 1, s * PG * 512:(s + 1) * PG * 512].rearrange("p (g f) -> p g f", g=PG) for s in range(2)]
        VACC = [[QB[:, 0], QB[:, 1]],
                [HF[:, 0, s * 512:(s + 1) * 512] for s in range(2)]]
        CV = [KF[:, 0:CVW], KF[:, CVW:2 * CVW]]
        CC = [KF[:, 2 * CVW:2 * CVW + T], VF[:, 2 * T:3 * T]]
        HR = [VF[:, 0:T], VF[:, T:2 * T]]
        PX = XF[:, 0:PXW]
        PD = [XF[:, PXW:2 * PXW], XF[:, 2 * PXW:3 * PXW]]
        SX = XF[:, 3 * PXW:3 * PXW + B * 16].rearrange("p (b r) -> p b r", r=16)
        PZ = [XT[:, 6], XT[:, 7]]
        C0 = HF[:, 0, 0:HC * B * DK].rearrange("p (s e) -> p s e", e=DK)
        VB = HF[:, 1, 0:B * 512].rearrange("p (b f) -> p b f", b=B)
        AROW, MROW = GA[0:HC, 0:TP], GB[0:HC, 0:TP]
        TROW = SCR[:].rearrange("p b g h -> p (b g h)")[0:HC, 0:T]
        MAXROW = TROW[:, 0:TP]
        SPOOL = SCR[:].rearrange("p b g h -> p (b g h)")[:, 1548:1548 + NW * B * PREV].rearrange(
            "p (c b r) -> p c b r", c=NW, b=B)
        CST = SCR[:].rearrange("p b g h -> p (b g h)")[:, T:T + HC * (DK + 1)].rearrange(
            "p (h e) -> p h e", h=HC)
        BROW = QB[:].rearrange("p s f -> p (s f)")[0:HC, 0:TP]
        XA = [WRAW[:, 0, 0:512], WRAW[:, 0, 512:1024]]
        XW = [WRAW[:, 1, 0:512], WRAW[:, 1, 512:1024]]
        XE = [WRAW[:, 2, 0:512], WRAW[:, 2, 512:1024], QB[:, 0], QB[:, 1]]
        HCT = XT[:, 4:8]

        def psum_tile(t, rows=P):
            return G[t % 2][0:rows, :, 0:TC]

        def third(x, b):
            return x[:, b * TC:(b + 1) * TC]

        def by3(x):
            return x.rearrange("p (b t) -> p b t", b=BANKS)

        def freed(t):
            return t // 2 + 1

        x_in = sem("x_in")
        par_in = sem("par_in")
        pages_in = sem("pages_in")
        fpar_in = sem("fpar_in")
        loaded = sem("loaded")
        qrow_sbuf = sem("qrow_sbuf")
        row_dram = sem("row_dram")
        qb_loaded = sem("qb_loaded")
        h_raw = sem("h_raw")
        kd_loaded = [sem(f"kd_loaded{s}") for s in range(2)]
        kd_red = sem("kd_red")
        kp_loaded = [sem(f"kp_loaded{s}") for s in range(3)]
        kp_red = sem("kp_red")
        v_loaded = [sem(f"v_loaded{s}") for s in range(4)]
        tile_done = sem("tile_done")
        v_used_dve = sem("v_used_dve")
        v_used_pool = sem("v_used_pool")
        p_ready = sem("p_ready")
        pt_psum = sem("pt_psum")
        fout_ready = sem("fout_ready")
        outs = sem("outs")
        fpb_ready = sem("fpb_ready")
        x_saved = sem("x_saved")
        spool_in = sem("spool_in")
        tile_free = [sem(f"tile_free{s}") for s in range(2)]
        gmoved = sem("gmoved")
        vrow_sbuf = sem("vrow_sbuf")
        c0_in = sem("c0_in")
        vb_in = sem("vb_in")
        tmp_out = [sem(f"tmp_out{s}") for s in range(2)]
        pool_back = sem("pool_back")
        pz_ready = sem("pz_ready")
        pool_out = sem("pool_out")
        og_in = sem("og_in")
        c_new = sem("c_new")
        c_out = sem("c_out")
        cst_ready = sem("cst_ready")
        hc_lo = sem("hc_lo")
        hc_lo_pool = sem("hc_lo_pool")
        y_ready = sem("y_ready")
        act_outs = sem("act_outs")
        fconv_out = sem("fconv_out")
        w_lo = sem("w_lo")
        sq_summed = sem("sq_summed")
        sq_psum = sem("sq_psum")
        gw_lo = sem("gw_lo")
        h_lo_dve = sem("h_lo_dve")
        h_lo_pool = sem("h_lo_pool")
        vt_sbuf = sem("vt_sbuf")
        vt_psum = sem("vt_psum")
        logf_in = sem("logf_in")
        lt_sbuf = sem("lt_sbuf")
        lt_psum = sem("lt_psum")
        tot_ready = sem("tot_ready")
        bias_sbuf = sem("bias_sbuf")
        bias_psum = sem("bias_psum")
        qrow_psum = sem("qrow_psum")
        summed = sem("summed")
        v_summed = sem("v_summed")
        att_in_lo = sem("att_in_lo")
        s_done = sem("s_done")
        ssum = sem("ssum")
        qk_new = sem("qk_new")
        fin_psum = sem("fin_psum")
        pt_sbuf = sem("pt_sbuf")
        o_sbuf = sem("o_sbuf")
        o_done = sem("o_done")
        fcum_ready = sem("fcum_ready")
        s_free = [sem(f"s_free{s}") for s in range(2)]
        sfeat = sem("sfeat")
        back_lo = sem("back_lo")
        back_lo_dve = sem("back_lo_dve")
        hid_lo = sem("hid_lo")
        arow_ready = sem("arow_ready")
        acol_psum = sem("acol_psum")
        acol_ready = sem("acol_ready")
        vts_ready = sem("vts_ready")
        vrow_psum = sem("vrow_psum")
        srows_ready = sem("srows_ready")
        srows_psum = sem("srows_psum")
        sbc_ready = sem("sbc_ready")
        qn_ready = sem("qn_ready")
        snum_psum = sem("snum_psum")
        mrow_ready = sem("mrow_ready")
        xa_sbuf = sem("xa_sbuf")
        xa_psum = sem("xa_psum")
        hc_ready = sem("hc_ready")
        kw_ready = sem("kw_ready")
        y_psum = sem("y_psum")
        own_act = sem("own_act")
        w_loaded = [sem(f"w_loaded{s}") for s in range(SLOTS)]
        w_hi = sem("w_hi")
        sq_ready = sem("sq_ready")
        std_ready = sem("std_ready")
        h_hi = sem("h_hi")
        gw_hi = sem("gw_hi")
        logsig_in = sem("logsig_in")
        a_saved = sem("a_saved")
        logf_ready = sem("logf_ready")
        fout_conv = sem("fout_conv")
        att_in_hi = sem("att_in_hi")
        rsum_ready = sem("rsum_ready")
        back_in = [sem(f"back_in{s}") for s in range(NW)]
        back_hi = sem("back_hi")
        sc_ready = sem("sc_ready")
        fin_args = sem("fin_args")
        fin_exp = sem("fin_exp")
        att_hi = sem("att_hi")
        sshift = sem("sshift")
        sprob = sem("sprob")
        fin_att = sem("fin_att")
        fin_hi = sem("fin_hi")
        conv_done = sem("conv_done")
        silu_done = sem("silu_done")
        hid_hi = sem("hid_hi")
        px_zero = sem("px_zero")
        px_ready = sem("px_ready")
        sx_ready = sem("sx_ready")
        sgate_args = sem("sgate_args")
        wm_ready = sem("wm_ready")
        w_exp = sem("w_exp")
        den_abs = sem("den_abs")
        apv_ready = sem("apv_ready")
        hc_gated = sem("hc_gated")
        hc_hi = sem("hc_hi")
        own_dve = sem("own_dve")
        kd_mul = sem("kd_mul")
        k_mul = sem("k_mul")
        k_added = sem("k_added")
        cvx_zero = sem("cvx_zero")
        smax_ready = sem("smax_ready")
        smax_all = sem("smax_all")
        cv_zero = sem("cv_zero")
        hcs_ready = sem("hcs_ready")
        pages_in_pool = sem("pages_in_pool")
        own_pool = sem("own_pool")

        block = E(nc.Block())

        def slice_of_dve(g):
            return slice(V_POOL[g % 2], PG)

        def slice_of_pool(g):
            return slice(0, V_POOL[g % 2])

        def values_of(eng, multiply_add, pages_of, which, used, own):
            def group(g):
                b, slot, pages = g // 8, VSLOT[g % 4], pages_of(g)
                acc = VACC[b % 2][which]
                n = pages.stop - pages.start
                if g == 0:
                    eng.wait_ge(sprob, 1)
                eng.wait_ge(v_loaded[g % 4], 16 * PG * (g // 4 + 1))
                v = slot[:, pages].rearrange("p g (h d) -> p (g h) d", d=HD)
                p0 = (g % 8) * PG
                prob = SCR[:, b, p0 + pages.start:p0 + pages.stop].rearrange("p g (h a) -> p (g h) a", a=1)
                own.link(multiply_add(v, v, prob.to_broadcast([P, n * HB, HD]), ALU.mult))
                page = [slot[:, pages.start + j] for j in range(n)]
                if g % 8 == 0:
                    wait(eng, v_summed, b - 1)
                    if n == 1:
                        (nc.vector if eng is nc.vector else nc.gpsimd).tensor_copy(acc, page[0]).then_inc(used, 1)
                        eng.wait_ge(used, g + 1)
                        return
                    own_or_used = page[1:]
                    first = multiply_add(acc, page[0], page[1], ALU.add)
                    rest = page[2:]
                else:
                    first = multiply_add(acc, acc, page[0], ALU.add)
                    rest = page[1:]
                for x in rest:
                    own.link(first)
                    first = multiply_add(acc, acc, x, ALU.add)
                first.then_inc(used, 1)
                eng.wait_ge(used, g + 1)
            return group

        @block.sync
        def _(sp):
            sp.dma_start(XT[:, :, 0:TP], a["xp"]).then_inc(x_in, 16)
            sp.dma_start(XT[:, :, TP:T], a["xs"]).then_inc(x_in, 16)
            sp.dma_start(CON[:], a["con"]).then_inc(par_in, 16)
            sp.dma_start(PT[:], a["pt"]).then_inc(pages_in, 16)
            sp.dma_start(GWR[:], a["gw"]).then_inc(par_in, 16)
            sp.dma_start(PRM[:], a["prm"]).then_inc(par_in, 16)
            sp.dma_start(SELC[:], a["selc"]).then_inc(par_in, 16)
            sp.dma_start(PW[:], a["pw"]).then_inc(par_in, 16)
            sp.dma_start(FPRM[:], a["fprm"][0]).then_inc(fpar_in, 16)

            def bcast_row(t, row):
                return t[bass.ds(row, 1), :].to_broadcast([P, NW * P])

            def kv_load(cache, g, dst, pg, loaded, *used):
                pages = [sp.value_load(PT[0:1, bass.ds(g * PG + j, 1)], min_val=0, max_val=cache.shape[0] - 1)
                         for j in pg]
                for done, value in used:
                    wait(sp, done, value)
                for j, page in zip(pg, pages):
                    sp.dma_start(dst[:, j - pg[0]], cache[bass.ds(page, 1)].rearrange("a p f -> (a p) f")
                                 ).then_inc(loaded, 16)

            sp.wait_ge(qrow_sbuf, 1)
            sp.dma_start(o["q_scr"], SROW[:]).then_inc(row_dram, 16)
            sp.wait_ge(row_dram, 16)
            sp.dma_start(QB[:, 0], bcast_row(o["q_scr"], 0)).then_inc(qb_loaded, 16)
            sp.wait_ge(h_raw, BANKS * ND)
            sp.wait_ge(pages_in, 16)

            for g in range(GROUPS):
                if g % 8 == 3 and g // 8 + 1 < B:
                    b = g // 8 + 1
                    sp.wait_ge(qb_loaded, b * 16)
                    sp.dma_start(QB[:, b % 2], bcast_row(o["q_scr"], b)).then_inc(qb_loaded, 16)
                kv_load(a["ck"], g, KDS[g % 2], range(KD), kd_loaded[g % 2], (kd_red, g - 1))
                kv_load(a["ck"], g, KPS[g % 3], range(KD, PG), kp_loaded[g % 3], (kp_red, g - 2))

            for g in range(8):
                kv_load(a["cv"], g, VSLOT[g % 4], range(PG), v_loaded[g % 4],
                        *([(kd_red, GROUPS - 1 + g), (kp_red, GROUPS)] if g < 2 else [(tile_done, T_IE + 24)] if g < 4 else
                          [(v_used_dve, g - 3), (v_used_pool, g - 3)]))
            with sp.Fori(1, B) as b:
                for g in range(8):
                    kv_load(a["cv"], b * 8 + g, VSLOT[g % 4], range(PG), v_loaded[g % 4], (v_used_dve, b * 8 + (g - 3)),
                            (v_used_pool, b * 8 + (g - 3)))

            sp.wait_ge(v_used_dve, GROUPS)
            sp.wait_ge(v_used_pool, GROUPS)
            sp.wait_ge(p_ready, HB * NB)
            sp.wait_ge(pt_psum, PT_ROUNDS)
            sp.dma_start(XT[:, :, 0:TP], a["xp"]).then_inc(x_in, 16)
            sp.dma_start(XT[:, :, TP:T], a["xs"]).then_inc(x_in, 16)

            sp.wait_ge(fout_ready, NF)
            sp.dma_start(o["ffn"][0], FOUT[:]).then_inc(outs, 16)
            sp.wait_ge(fpb_ready, FI)
            sp.dma_start(FPRM[:], a["fprm"][1]).then_inc(fpar_in, 16)

            sp.wait_ge(h_raw, 3 * BANKS * ND)
            sp.dma_start(o["x_scr"], XT[:]).then_inc(x_saved, 16)
            sp.dma_start(SPOOL, a["spool"]).then_inc(spool_in, 16)
            sp.wait_ge(tile_free[T_GO % 2], freed(T_GO))
            sp.dma_start(GB[0:HC, :], GA[HC:2 * HC, :]).then_inc(gmoved, 16)
            sp.wait_ge(vrow_sbuf, 1)
            sp.dma_start(o["v_scr"], SROW[:]).then_inc(row_dram, 16)
            sp.wait_ge(row_dram, 32)
            sp.wait_ge(tile_done, T_P[3] + 1)
            sp.dma_start(C0, a["c0"]).then_inc(c0_in, 16)
            for b in range(B):
                sp.dma_start(VB[:, b], bcast_row(o["v_scr"], b)).then_inc(vb_in, 16)
            for s in range(2):
                sp.wait_ge(tmp_out[s], 96)
            sp.dma_start(HF[:, 1, NW * T:ND * T].rearrange("p (c t) -> p c t", t=T), o["p_scr"].rearrange("c p t -> p c t")
                         ).then_inc(pool_back, 16)
            sp.wait_ge(pz_ready, NW)
            sp.wait_ge(pool_out, 32 * NW)
            sp.dma_start(XT[:, 0:NW], o["o_scr"].rearrange("c p t -> p c t")).then_inc(og_in, 16)
            sp.wait_ge(c_new, B)
            sp.dma_start(o["c_s"], C0).then_inc(c_out, 16)
            sp.wait_ge(cst_ready, HC * NB)
            sp.dma_start(o["c_p"], CST).then_inc(outs, 16)
            sp.wait_ge(hc_lo, NW // 2)
            sp.wait_ge(hc_lo_pool, NW // 2)
            sp.wait_ge(x_saved, 16)
            sp.dma_start(XT[:], o["x_scr"]).then_inc(x_in, 16)

            sp.wait_ge(fout_ready, 2 * NF)
            sp.dma_start(o["ffn"][1], FOUT[:]).then_inc(outs, 16)
            for c in range(ND):
                sp.wait_ge(y_ready, c + 1)
                sp.dma_start(o["y"][c], XT[:, c]).then_inc(outs, 16)
            sp.wait_ge(outs, 16 * (3 + ND))
            sp.wait_ge(act_outs, 16 * ACT_OUTS)
            sp.wait_ge(fconv_out, 16)
            sp.wait_ge(pool_out, 32 * NW)

        @block.tensor
        def _(pe):
            def passes(out, whi, wlo, xhi, xlo, first, last):
                for n, (w, x) in enumerate(((whi, xhi), (whi, xlo), (wlo, xhi))):
                    for c in range(BANKS):
                        mm = pe.matmul(out[:, c], w, x[:, c * TC:(c + 1) * TC], start=first and n == 0,
                                       stop=last and n == 2)
                return mm

            def unit(u, t, free, lo):
                slot = u % SLOTS
                pe.wait_ge(w_lo, lo)
                wait(pe, tile_free[t % 2], free)
                for k in range(ND):
                    mm = passes(psum_tile(t), WHI[:, slot, k * P:(k + 1) * P], WLO[:, slot, k * P:(k + 1) * P],
                                HHI[:, k], HLO[:, k], k == 0, k == ND - 1)
                mm.then_inc(tile_done, 1)

            def plain_unit(u, t):
                unit(u, t, t // 2, u + 1)

            def norm(n):
                t = T_N[n]
                pe.wait_ge(sq_summed, (n + 1) * (ND - 1))
                wait(pe, tile_free[t % 2], t // 2)
                for b in range(BANKS):
                    pe.matmul(psum_tile(t)[:, b], ones, third(ACC, b), start=True, stop=True
                              ).then_inc(tile_done if b == BANKS - 1 else sq_psum, 1)

            def gate_tile(layer, t):
                return t, psum_tile(t, HB), lambda k: (GWH[:, layer, k], GWL[:, layer, k]), (gw_lo, 1)

            def unit_tile(u, t):
                return t, psum_tile(t), lambda k: (WHI[:, u % SLOTS, k * P:(k + 1) * P],
                                                   WLO[:, u % SLOTS, k * P:(k + 1) * P]), (w_lo, u + 1)

            def normed_tiles(n, tiles):
                for t, _, _, ready in tiles:
                    pe.wait_ge(*ready)
                    pe.wait_ge(tile_free[t % 2], t // 2)
                for b in range(BANKS):
                    for k in range(ND):
                        pe.wait_ge((h_lo_dve, h_lo_pool)[k % 2], (n * BANKS + b) * (ND // 2) + k // 2 + 1)
                        for t, out, weights, _ in tiles:
                            whi, wlo = weights(k)
                            for r, (w, x) in enumerate(((whi, HHI), (whi, HLO), (wlo, HHI))):
                                mm = pe.matmul(out[:, b], w, third(x[:, k], b), start=k == 0 and r == 0,
                                               stop=k == ND - 1 and r == 2)
                            if b == BANKS - 1 and k == ND - 1:
                                mm.then_inc(tile_done, 1)

            def first_tiles(order, tiles):
                for t, _, _, ready in tiles:
                    pe.wait_ge(*ready)
                    pe.wait_ge(tile_free[t % 2], t // 2)
                for n, (k, waits) in enumerate(order):
                    for done, value in waits:
                        pe.wait_ge(done, value)
                    for t, out, weights, _ in tiles:
                        mm = passes(out, *weights(k), HHI[:, k], HLO[:, k], n == 0, n == ND - 1)
                        if n == ND - 1:
                            mm.then_inc(tile_done, 1)

            def values_turned(j, layer):
                t = (T_IE if layer == 0 else T_IO) + 8 + j
                pe.wait_ge(tile_free[t % 2], freed(t))
                for r in range(2):
                    n = (layer * NW + j) * 2 + r
                    wait(pe, vt_sbuf, n)
                    for q in range(4):
                        mm = pe.transpose(M0[:, q * P:(q + 1) * P], TMP[j % 2][:, (r * 4 + q) * P:(r * 4 + q + 1) * P],
                                          ident)
                    mm.then_inc(vt_psum, 1)

            def forgets_turned(r):
                half, hq = r // 2, r % 2
                if r == 0:
                    pe.wait_ge(logf_in, 32)
                wait(pe, lt_sbuf, r)
                for q in range(4):
                    mm = pe.transpose(M0[:, q * P:(q + 1) * P], LG[:, half, :, hq * 4 + q], ident)
                mm.then_inc(lt_psum, 1)

            def forgets_summed(r):
                half, hq = r // 2, r % 2
                pe.wait_ge(tot_ready, 1)
                pe.wait_ge(lt_sbuf, r + 1)
                wait(pe, bias_sbuf, r)
                for q in range(4):
                    h = hq * 4 + q
                    dst = M1[:, q * P:(q + 1) * P]
                    pe.matmul(dst, CON[:, C_LATER], LT[:, half, h], start=True, stop=False)
                    mm = pe.matmul(dst, TOT[:, half, h:h + 1].to_broadcast([P, P]), CON[:, C_PLATER],
                                   start=False, stop=True)
                mm.then_inc(bias_psum, 1)

            pe.wait_ge(par_in, 16 * PAR_LOADS)
            norm(0)
            normed_tiles(0, [gate_tile(0, T_GE), unit_tile(U_IE, T_IE)])
            for u in range(24):
                if u:
                    plain_unit(U_IE + u, T_IE + u)
                if u < 4:
                    forgets_turned(u)
                if 1 <= u < 5:
                    forgets_summed(u - 1)
                if u == 4:
                    pe.wait_ge(lt_sbuf, 4)
                    for s in range(2):
                        pe.wait_ge(tile_free[s], freed(T_IE + 2 + s))
                    for j in range(NW):
                        mm = pe.transpose(M0[0:B, j * P:(j + 1) * P], QT[:, j, TP:T], ident)
                    mm.then_inc(qrow_psum, 1)
                    pe.wait_ge(qrow_sbuf, 1)
                if 9 <= u <= 12:
                    values_turned(u - 9, 0)

            def value_sum(b):
                pe.wait_ge(v_used_dve, 8 * (b + 1))
                pe.wait_ge(v_used_pool, 8 * (b + 1))
                if b == 0:
                    pe.wait_ge(bias_sbuf, 4)
                for c in range(NW):
                    for n, acc in enumerate(VACC[b % 2]):
                        mm = pe.matmul(M1[:, b * NW + c:b * NW + c + 1], acc[:, c * P:(c + 1) * P], ones[:, 0:1],
                                       start=n == 0, stop=n == 1)
                mm.then_inc(v_summed, 1)

            def scores(x, h, step):
                qb = BLOCKS[step]
                rows = slice(HD * (h % 2), HD * (h % 2) + HD)
                n = (qb + 1) * P
                block = slice(qb * P, (qb + 1) * P)
                if step == 0 and h % 2 == 0:
                    pe.wait_ge(att_in_lo, h + 3)
                kh, kl, qh, ql = KHI[h // 2], KLO[:, h // 2], QHI[h // 2], QLO[:, h // 2]
                for r, (q, kk) in enumerate(((qh, kh), (qh, kl), (ql, kh))):
                    for c0 in range(0, n, 512):
                        c1 = min(n, c0 + 512)
                        pe.matmul(GF[x % 2][:, c0:c1], q[rows, block], kk[rows, c0:c1], start=r == 0,
                                  stop=r == 2 and c1 < n)
                pe.matmul(GF[x % 2][:, n - P:n], IMR[:, 0], IMR[:, 1], start=False, stop=True).then_inc(s_done, 1)

            def sample_sums():
                pe.wait_ge(ssum, 1)
                pe.wait_ge(qk_new, 1)
                pe.matmul(M1[:, 64:128], ones, RSS[:].rearrange("p b h -> p (b h)"), start=True, stop=True)
                pe.matmul(M1[:, 128:160], CON[:, C_BLK], SM[:, 0], start=True, stop=True)
                for c in range(NW):
                    mm = pe.matmul(M1[:, 160 + c * B:160 + (c + 1) * B], SELC[:, c], GA[:, TP:T], start=True, stop=True)
                mm.then_inc(fin_psum, 1)

            rounds = [0]

            def turns(h, qb, k):
                pe.wait_ge(p_ready, k + 1)
                for r in range(qb // 4 + 1):
                    n = rounds[0]
                    wait(pe, pt_sbuf, n - 1)
                    for q in range(r * 4, min(r * 4 + 4, qb + 1)):
                        mm = pe.transpose(G[n % 2][:, 2, (q % 4) * P:(q % 4 + 1) * P], SC[k % 2][:, q * P:(q + 1) * P],
                                          ident)
                    mm.then_inc(pt_psum, 1)
                    rounds[0] = n + 1

            def results(h, qb, k):
                pe.wait_ge(pt_sbuf, ROUNDS[k])
                wait(pe, o_sbuf, k)
                for q in range(qb + 1):
                    mm = pe.matmul(M0[:, 0:HD], PTS[k % 2][:, q * P:(q + 1) * P], VTOK[:, q, h * HD:(h + 1) * HD],
                                   start=q == 0, stop=q == qb)
                mm.then_inc(o_done, 1)

            pe.wait_ge(vt_sbuf, 2 * NW)
            pe.wait_ge(fcum_ready, 1)
            for s in range(2):
                pe.wait_ge(tile_free[s], (T_OE + 1 - s) // 2)
            late = []
            for x, item in enumerate(ORDER):
                if item[0] == "s":
                    k = item[1] * NB + item[2]
                    for b in range(B - 1):
                        if k and VALUES[k - 1] >= 8 * (b + 1) > (VALUES[k - 2] if k > 1 else 0):
                            value_sum(b)
                wait(pe, s_free[x % 2], x // 2)
                if item[0] == "n":
                    pe.wait_ge(att_in_lo, 1)
                    for c0 in (0, 512):
                        for r, part in enumerate((FHI, FLO)):
                            mm = pe.matmul(GF[x % 2][:, c0:c0 + 512],
                                           IMR[0:HB, 0, item[1]:item[1] + 1].to_broadcast([HB, P]),
                                           part[:, c0:c0 + 512], start=r == 0, stop=r == 1)
                    mm.then_inc(s_done, 1)
                    continue
                elif item[0] == "s":
                    scores(x, item[1], item[2])
                else:
                    j = item[1]
                    if x == len(ORDER) - 1:
                        turns(*late[1])
                        value_sum(B - 1)
                        sample_sums()
                        results(*late[0])
                        results(*late[1])
                    pe.wait_ge(o_sbuf, (2 * j + 2) * NB)
                    for qb in range(NB):
                        mm = pe.transpose(GF[x % 2][:, qb * P:(qb + 1) * P], OT[:, qb], ident)
                    mm.then_inc(s_done, 1)
                    continue
                if late:
                    turns(*late[-1])
                if len(late) == 2:
                    results(*late.pop(0))
                late.append((item[1], BLOCKS[item[2]], item[1] * NB + item[2]))

            pe.wait_ge(sfeat, 1)
            for s in range(2):
                pe.wait_ge(s_free[s], (len(ORDER) + 1 - s) // 2)
            first_tiles([(4, []), (5, []), (6, []), (7, []), (1, [(back_lo, NW // 2 + 1), (back_lo_dve, 1)]),
                         (2, [(back_lo_dve, 2)]), (0, []), (3, [])],
                        [unit_tile(U_OE + m, T_OE + m) for m in range(2)])
            for m in range(2, ND):
                plain_unit(U_OE + m, T_OE + m)

            def mlp(layer):
                tb, ub = T_F[layer], U_F[layer]
                norm(2 * layer + 1)

                def down(t, u, plus, hid):
                    pe.wait_ge(hid_lo, hid)
                    for m in range(ND):
                        tt = t + m
                        pe.wait_ge(tile_free[tt % 2], plus(tt // 2))
                        for jj in range(2):
                            slot = (u + jj) % SLOTS
                            mm = passes(psum_tile(tt), WHI[:, slot, m * P:(m + 1) * P], WLO[:, slot, m * P:(m + 1) * P],
                                        HIDH[:, jj], HIDL[:, jj], jj == 0, jj == 1)
                        mm.then_inc(tile_done, 1)

                normed_tiles(2 * layer + 1, [unit_tile(ub + r, tb + r) for r in range(2)])
                for r in range(2, 4):
                    plain_unit(ub + r, tb + r)
                with pe.Fori(0, FI - 1) as i:
                    for r in range(4):
                        t = tb + 4 + r
                        unit(ub + 4 + r, t, i * 6 + t // 2, i * 6 + (ub + 4 + r + 1))
                    pe.wait_ge(w_lo, i * 6 + (ub + 10))
                    down(tb + 8, ub + 8, lambda v: i * 6 + v, i * 2 + (layer * NF + 2))
                pe.wait_ge(w_lo, ub + 6 * FI)
                down(tb + 12 * FI - 8, ub + 6 * FI - 2, lambda v: v, (layer + 1) * NF)

            mlp(0)

            norm(2)
            normed_tiles(2, [gate_tile(1, T_GO), unit_tile(U_IO, T_IO)])
            for u in range(20):
                t = T_IO + u if u < 16 else T_P[u - 16]
                if u:
                    plain_unit(U_IO + u, t)
                if u == 4:
                    pe.wait_ge(arow_ready, 1)
                    for ch in range(NB):
                        mm = pe.transpose(M0[:, ch * HC:(ch + 1) * HC], AROW[:, ch * P:(ch + 1) * P], ident[0:HC, 0:HC])
                    mm.then_inc(acol_psum, 1)
                    pe.wait_ge(acol_ready, 1)
                if 9 <= u <= 12:
                    values_turned(u - 9, 1)
                if u == 13:
                    pe.wait_ge(vt_sbuf, 4 * NW)
                    pe.wait_ge(vts_ready, 2 * NW)
                    for j in range(NW):
                        mm = pe.transpose(M0[0:B, j * P:(j + 1) * P], VTS[:, j], ident)
                    mm.then_inc(vrow_psum, 1)
                if u == 15:
                    pe.wait_ge(vrow_sbuf, 1)
                    pe.wait_ge(srows_ready, 1)
                    for h in range(HC):
                        mm = pe.matmul(M0[:, h * 3 * B:(h + 1) * 3 * B], ident[0:HC, h:h + 1].to_broadcast([HC, P]),
                                       SROWS[:].rearrange("p k b -> p (k b)")[:, 0:3 * B], start=True, stop=True)
                    mm.then_inc(srows_psum, 1)
                if u >= 17:
                    for g in ([u - 17] if u < 19 else [2, 3]):
                        t = T_PM[g]
                        pe.wait_ge(pz_ready, g + 1)
                        pe.wait_ge(tile_free[t % 2], t // 2)
                        for c in range(BANKS):
                            mm = pe.matmul(psum_tile(t)[:, c], PW[:, g], PZ[g % 2][:, c * TC:(c + 1) * TC],
                                           start=True, stop=True)
                        mm.then_inc(tile_done, 1)

            def sample_results(b):
                if b == 0:
                    pe.wait_ge(sbc_ready, 1)
                    pe.wait_ge(qn_ready, 1)
                    pe.matmul(M0[:, 128:128 + HC * B], ones, SM[:, 2], start=True, stop=True)
                pe.wait_ge(c_new, b + 1)
                for h in range(HC):
                    mm = pe.matmul(M0[:, 192 + h * B + b:193 + h * B + b], C0[:, b * HC + h], QT[:, h, TP + b:TP + b + 1],
                                   start=True, stop=True)
                mm.then_inc(snum_psum, 1)

            for s in range(2):
                pe.wait_ge(tile_free[s], (T_OO + 1 - s) // 2)
            pe.wait_ge(mrow_ready, 1)

            def chunk_in(i):
                ch, h = divmod(i, HC)
                cols = slice(ch * P, (ch + 1) * P)
                wait(pe, xa_sbuf, i - 1)
                x = G[i % 2][:, 0]
                sel = ident[0:HC, h:h + 1].to_broadcast([HC, P])
                pe.matmul(x[:, 0:P], sel, MAXROW[:, cols], start=True, stop=True)
                pe.matmul(x[:, P:2 * P], sel, MROW[:, cols], start=True, stop=True)
                pe.matmul(x[:, 2 * P:3 * P], KT[:, h, cols], QT[:, h, cols], start=True, stop=True)
                pe.transpose(x[:, 3 * P:4 * P], KT[:, h, cols], ident).then_inc(xa_psum, 1)

            def chunk_out(i):
                ch, h = divmod(i, HC)
                y = G[i % 2][:, 1]
                v = VTOK[:, ch, h * DK:(h + 1) * DK]
                w = XW[i % 2]
                wait(pe, cst_ready, i - 3)
                wait(pe, hc_ready, i - 1)
                wait(pe, cst_ready, i - 1)
                pe.wait_ge(kw_ready, i + 1)
                pe.matmul(y[:, 0:P], v, w[:, P:2 * P], start=True, stop=False)
                pe.matmul(y[:, 0:P], CST[:, h, 0:DK], w[:, 2 * P:3 * P], start=False, stop=True)
                pe.matmul(y[:, P:2 * P], ones, w[:, P:2 * P], start=True, stop=False)
                pe.matmul(y[:, P:2 * P], CST[:, h, DK:DK + 1].to_broadcast([P, P]), w[:, 2 * P:3 * P],
                          start=False, stop=True)
                pe.matmul(y[:, 2 * P:3 * P], w[:, 3 * P:4 * P], v, start=True, stop=True)
                pe.matmul(y[:, 3 * P:3 * P + 1], w[:, 3 * P:4 * P], ones[:, 0:1], start=True, stop=True
                          ).then_inc(y_psum, 1)

            chunk_in(0)
            for i in range(HC * NB):
                if i + 1 < HC * NB:
                    chunk_in(i + 1)
                chunk_out(i)
                if i % 3 == 1 and 7 <= i < 7 + 3 * B:
                    sample_results((i - 7) // 3)

            pe.wait_ge(hc_ready, HC * NB)
            pe.wait_ge(cst_ready, HC * NB)
            first_tiles([(NW + c, [(back_lo, NW // 2 + 1 + c + 1)]) for c in range(NW)] +
                        [(c, [((hc_lo, hc_lo_pool)[c % 2], c // 2 + 1)]) for c in range(NW)],
                        [unit_tile(U_OO + m, T_OO + m) for m in range(2)])
            for m in range(2, ND):
                plain_unit(U_OO + m, T_OO + m)

            mlp(1)
            norm(4)

        @block.scalar
        def _(act):
            own = Own(act, own_act)
            A = nc.scalar.activation

            def load(u):
                if u < U_END:
                    wait(act, w_lo, u - SLOTS + 1)
                    act.dma_start(WRAW[:, u % SLOTS], a["w"][u]).then_inc(w_loaded[u % SLOTS], 16)

            def load_at(u, i):
                act.wait_ge(w_lo, i * 6 + (u - SLOTS + 1))
                act.dma_start(WRAW[:, u % SLOTS], a["w"][bass.ds(i * 6 + u, 1)].rearrange("a p f -> (a p) f")
                              ).then_inc(w_loaded[u % SLOTS], 16)

            def high(u):
                if u < U_END:
                    act.wait_ge(w_loaded[u % SLOTS], 16 * (u // SLOTS + 1))
                    if u >= SLOTS:
                        act.wait_ge(tile_done, last_tile(u - SLOTS) + 1)
                    A(WHI[:, u % SLOTS], WRAW[:, u % SLOTS], ACT.Copy).then_inc(w_hi, 1)

            def unit_used(u, deferred=()):
                high(u + SLOTS)
                if u + 5 not in deferred:
                    load(u + 5)

            def evacuate(out, t, func=ACT.Copy, rows=P, **kw):
                act.wait_ge(tile_done, t + 1)
                A(by3(out), psum_tile(t, rows), func, **kw).then_inc(tile_free[t % 2], 1)
                act.wait_ge(tile_free[t % 2], freed(t))

            def square(n, c):
                if n == 0:
                    act.wait_ge(x_in, 32)
                else:
                    act.wait_ge(tile_free[(T_X[n] + c) % 2], freed(T_X[n] + c))
                if c >= 3:
                    act.wait_ge(sq_summed, n * (ND - 1) + c - 2)
                A(ACC if c == 0 else SQ[c % 2], XT[:, c], ACT.Square).then_inc(sq_ready, 1)

            def norm(n, halves=True):
                t = T_N[n]
                if n:
                    square(n, ND - 1)
                for b in range(BANKS):
                    if b < BANKS - 1:
                        act.wait_ge(sq_psum, n * (BANKS - 1) + b + 1)
                    else:
                        act.wait_ge(tile_done, t + 1)
                    A(third(RSTD, b), psum_tile(t)[:, b], ACT.Sqrt, bias=PRM[:, O_EPS:O_EPS + 1], scale=1.0 / D
                      ).then_inc(tile_free[t % 2] if b == BANKS - 1 else std_ready, 1)
                if halves:
                    for b in range(BANKS):
                        for c in range(ND):
                            act.wait_ge(h_raw, (n * BANKS + b) * ND + c + 1)
                            A(third(HHI[:, c], b), third(HN[c % 4], b), ACT.Copy).then_inc(h_hi, 1)

            def values_turned(j, layer):
                for r in range(2):
                    n = (layer * NW + j) * 2 + r
                    act.wait_ge(vt_psum, n + 1)
                    A(VTOK[:, r * 4:r * 4 + 4, j * P:(j + 1) * P], M0[:].rearrange("p (q f) -> p q f", f=P),
                      ACT.Copy).then_inc(vt_sbuf, 1)

            for u in range(SLOTS):
                load(u)
            for c in range(ND):
                square(0, c)
            act.wait_ge(par_in, 16 * PAR_LOADS)
            A(GWH[:], GWR[:], ACT.Copy).then_inc(gw_hi, 1)
            for u in range(SLOTS):
                high(u)
            for u in range(SLOTS, 5):
                load(u)

            def forgets_turned(r):
                half, hq = r // 2, r % 2
                act.wait_ge(lt_psum, r + 1)
                A(LT[:, half, hq * 4:hq * 4 + 4], M0[:].rearrange("p (h g) -> p h g", g=P), ACT.Copy).then_inc(lt_sbuf, 1)

            def forgets_summed(r):
                half, hq = r // 2, r % 2
                act.wait_ge(bias_psum, r + 1)
                A(SCR[:, half * 4:half * 4 + 4, :, hq * 4:hq * 4 + 4].rearrange("p b g h -> p h (b g)"),
                  M1[:].rearrange("p (h g) -> p h g", g=P), ACT.Copy).then_inc(bias_sbuf, 1)

            norm(0)
            t = T_GE
            act.wait_ge(tile_done, t + 1)
            A(by3(GA[:]), psum_tile(t, HB), ACT.Identity, bias=PRM[0:HB, O_GB:O_GB + 1]).then_inc(tile_free[t % 2], 1)
            act.wait_ge(tile_free[t % 2], freed(t))

            def log_sigmoid(z, out):
                own.link(A(out, z, ACT.Abs))
                own.link(A(out, out, ACT.Exp, scale=-1.0))
                A(out, out, ACT.Ln, bias=ones[0:z.shape[0], 0:1]).then_inc(logsig_in, 1)

            log_sigmoid(GA[:], GB[:])

            def store_tmp(s, dst, done):
                act.dma_start(dst, TMP[s]).then_inc(done, 16)

            for u in range(24):
                t, j = T_IE + u, u % 4
                if u < 4:
                    evacuate(QT[:, j], t, scale=HD ** -0.5)
                elif u < 8:
                    evacuate(KT[:, j], t)
                    act.dma_start(o["k"][j], KT[:, j]).then_inc(act_outs, 16)
                elif u < 12:
                    if j >= 2:
                        act.wait_ge(tmp_out[j % 2], 16)
                    evacuate(TMP[j % 2], t)
                    A(VTS[:, j], TMP[j % 2][:, TP:T], ACT.Copy).then_inc(vts_ready, 1)
                    act.dma_start(o["v"][j], TMP[j % 2]).then_inc(tmp_out[j % 2], 16)
                elif (u - 12) % 3 == 0:
                    jc = (u - 12) // 3
                    if jc == 0:
                        act.wait_ge(tmp_out[0], 32)
                    else:
                        act.wait_ge(tile_free[(t - 2) % 2], freed(t - 2))
                    evacuate(TMP[0], t)
                elif (u - 12) % 3 == 2:
                    jc = (u - 12) // 3
                    act.wait_ge(tile_free[t % 2], freed(t))
                    act.dma_start(o["a_scr"][jc], TMP[1]).then_inc(a_saved, 16)
                if u == 4:
                    act.wait_ge(qrow_psum, 1)
                    A(SROW[:], M0[0:B], ACT.Copy).then_inc(qrow_sbuf, 1)
                unit_used(U_IE + u, deferred=(U_OE + 3, U_OE + 4))
                if u < 4:
                    forgets_turned(u)
                if 1 <= u < 5:
                    forgets_summed(u - 1)
                if 9 <= u <= 12:
                    values_turned(u - 9, 0)
                if u == 5:
                    act.wait_ge(logf_ready, 1)
                    act.dma_start(o["logf"], GA[:]).then_inc(act_outs, 16)
            act.wait_ge(fout_conv, NW)
            act.dma_start(o["conv_a"], FOUT[:, 0:NW]).then_inc(fconv_out, 16)

            def pair_high(j):
                A(KHI[j][:, 0:TP], KT[:, j, 0:TP], ACT.Copy).then_inc(att_in_hi, 1)
                A(QHI[j][:, 0:TP], QT[:, j, 0:TP], ACT.Copy).then_inc(att_in_hi, 1)

            A(IMR[:, 0], ident, ACT.Copy)
            A(IMR[:, 1], CON[:, C_MASK], ACT.Copy)
            act.wait_ge(act_outs, 16 * (NW + 1))
            act.wait_ge(fcum_ready, 1)
            A(FHI[:, 0:TP], GB[:, 0:TP], ACT.Copy).then_inc(att_in_hi, 1)
            pair_high(0)

            rounds = [0]
            act.wait_ge(w_lo, U_OE + SLOTS)

            def turned(h, qb, k):
                for r in range(qb // 4 + 1):
                    n = rounds[0]
                    w = min(4, qb + 1 - 4 * r) * P
                    act.wait_ge(pt_psum, n + 1)
                    wait(act, o_done, k - 1)
                    A(PTS[k % 2][:, r * 512:r * 512 + w], G[n % 2][:, 2, 0:w], ACT.Copy).then_inc(pt_sbuf, 1)
                    rounds[0] = n + 1

            def result(h, qb, k):
                act.wait_ge(rsum_ready, k + 1)
                act.wait_ge(o_done, k + 1)
                if h >= 2 and h % 2 == 0:
                    act.wait_ge(s_done, ORDER.index(("t", h // 2 - 1)) + 1)
                A(OT[:, qb, (h % 2) * HD:(h % 2 + 1) * HD], M0[:, 0:HD], ACT.Copy, scale=FMX[:, 3, k % 4:k % 4 + 1]
                  ).then_inc(o_sbuf, 1)

            def conv_back(j):
                act.wait_ge(a_saved, 16 * NW)
                act.dma_start(QT[:, j, 0:TP], o["a_scr"][j][:, 0:TP]).then_inc(back_in[j], 16)
                act.dma_start(AS[:, j], o["a_scr"][j][:, TP:T]).then_inc(back_in[j], 16)

            def conv_high(j):
                act.wait_ge(back_in[j], 32)
                A(HHI[:, j, 0:TP], QT[:, j, 0:TP], ACT.Copy).then_inc(back_hi, 1)

            late = []

            def attend(x):
                item = ORDER[x]
                if item == ("s", HB - 1, 4):
                    conv_high(2)
                if item[0] == "n":
                    h = item[1]
                    wait(act, sc_ready, NB * (h - 1))
                    act.wait_ge(s_done, x + 1)
                    A(NEGF[h % 2], GF[x % 2][:, 0:TP], ACT.Copy).then_inc(s_free[x % 2], 1)
                    return
                if item[0] == "s":
                    k = item[1] * NB + item[2]
                    n = (BLOCKS[item[2]] + 1) * P
                    act.wait_ge(sc_ready, k + 1)
                    wait(act, rsum_ready, k - 3)
                    A(SC[k % 2][:, 0:n], SC[k % 2][:, 0:n], ACT.Exp, bias=FMX[:, 1, k % 4:k % 4 + 1],
                      accum_out=FMX[:, 2, k % 4:k % 4 + 1]).then_inc(p_ready, 1)
                    if late:
                        turned(*late[-1])
                    if len(late) == 2:
                        result(*late.pop(0))
                    late.append((item[1], BLOCKS[item[2]], k))
                    return
                j = item[1]
                if x == len(ORDER) - 1:
                    turned(*late[1])
                    conv_back(j)
                    result(*late[0])
                    result(*late[1])
                    act.wait_ge(v_summed, B)
                    conv_high(0)
                    act.wait_ge(fin_args, 1)
                    A(SM[:, 6:8].rearrange("p k f -> p (k f)"), SM[:, 4:6].rearrange("p k f -> p (k f)"), ACT.Exp
                      ).then_inc(fin_exp, 1)
                act.wait_ge(s_done, x + 1)
                A(HHI[:, NW + j, 0:TP], GF[x % 2][:, 0:TP], ACT.Copy).then_inc(att_hi, 1)
                if x < len(ORDER) - 1:
                    conv_back(j)
                if j == 2:
                    conv_high(1)

            act.wait_ge(a_saved, 16 * NW)
            for x in range(1 + EARLY):
                attend(x)
            act.wait_ge(sshift, 1)
            flat = SCR[:].rearrange("p b g h -> p (b g h)")
            A(flat, flat, ACT.Exp).then_inc(sprob, 1)
            for j in range(1, NW):
                pair_high(j)
            for x in range(1 + EARLY, len(ORDER)):
                attend(x)
            act.wait_ge(fin_att, 1)
            A(HHI[:, NW:ND, TP:T], SM[:, 10].rearrange("p (c b) -> p c b", c=NW), ACT.Copy).then_inc(fin_hi, 1)
            conv_high(NW - 1)
            A(HHI[:, 0:NW, TP:T], AS[:], ACT.Copy).then_inc(back_hi, 1)
            act.wait_ge(o_done, HB * NB)
            act.wait_ge(att_hi, NW)
            load(U_OE + 3)
            load(U_OE + 4)

            def project(u, t, n):
                for m in range(ND):
                    act.wait_ge(tile_done, t + m + 1)
                    unit_used(u + m)
                    if m:
                        square(n, m - 1)

            project(U_OE, T_OE, 1)

            def mlp(layer):
                tb, ub = T_F[layer], U_F[layer]
                norm(2 * layer + 1)

                def gate(jj, t, done, free, conv):
                    act.wait_ge(tile_done, done)
                    wait(act, conv_done, conv)
                    wait(act, fout_ready, conv)
                    A(by3(CV[jj][:, 2:2 + T]), psum_tile(t), ACT.Copy).then_inc(tile_free[t % 2], 1)

                def silu(jj, conv):
                    act.wait_ge(conv_done, conv)
                    A(CC[jj], CC[jj], ACT.Silu, bias=FPB[:, jj, 3:4]).then_inc(silu_done, 1)

                def hidden(jj, t, free, hid):
                    act.wait_ge(tile_free[t % 2], free)
                    A(HIDH[:, jj], HR[jj], ACT.Copy).then_inc(hid_hi, 1)

                c0 = layer * NF
                for jj in range(2):
                    t = tb + 2 * jj
                    gate(jj, t, t + 1, None, c0)
                    unit_used(ub + 2 * jj)
                    silu(jj, c0 + jj + 1)
                    act.wait_ge(tile_done, t + 2)
                    unit_used(ub + 2 * jj + 1)
                for jj in range(2):
                    t = tb + 2 * jj + 1
                    hidden(jj, t, freed(t), None)
                def step(i):
                    def used_at(u, done):
                        if isinstance(i, int):
                            act.wait_ge(tile_done, done)
                            return unit_used(u + 6 * i)
                        v = u + SLOTS
                        act.wait_ge(w_loaded[v % SLOTS], i * 32 + 16 * (v // SLOTS + 1))
                        act.wait_ge(tile_done, done)
                        A(WHI[:, v % SLOTS], WRAW[:, v % SLOTS], ACT.Copy).then_inc(w_hi, 1)
                        load_at(u + 5, i)

                    for jj in range(2):
                        t = tb + 4 + 2 * jj
                        gate(jj, t, i * 12 + (t + 1), None, i * 2 + (c0 + jj + 1))
                        used_at(ub + 4 + 2 * jj, i * 12 + (t + 1))
                        silu(jj, i * 2 + (c0 + 2 + jj + 1))
                        used_at(ub + 5 + 2 * jj, i * 12 + (t + 2))
                    used_at(ub + 8, i * 12 + (tb + 16))
                    if not isinstance(i, int):
                        used_at(ub + 9, i * 12 + (tb + 16))
                    for jj in range(2):
                        t = tb + 5 + 2 * jj
                        hidden(jj, t, i * 6 + freed(t), None)
                    if isinstance(i, int):
                        used_at(ub + 9, i * 12 + (tb + 16))

                with act.Fori(0, FI - 2) as i:
                    step(i)
                step(FI - 2)
                act.wait_ge(fout_ready, (layer + 1) * NF)
                for c in range(ND - 1):
                    square(2 * layer + 2, c)
                act.wait_ge(tile_done, tb + 12 * FI)
                for r in range(2):
                    unit_used(ub + 6 * FI - 2 + r)

            mlp(0)

            norm(2)
            t = T_GO
            act.wait_ge(tile_done, t + 1)
            A(by3(GA[:]), psum_tile(t, HB), ACT.Identity, bias=PRM[0:HB, O_GB + 1:O_GB + 2]).then_inc(tile_free[t % 2], 1)
            act.wait_ge(gmoved, 16)
            log_sigmoid(GB[0:HC, :], TROW)
            for u in range(20):
                t, j = (T_IO + u if u < 16 else T_P[u - 16]), u % 4
                if u < 4:
                    evacuate(QT[:, j], t)
                elif u < 8:
                    evacuate(KT[:, j], t, scale=DK ** -0.5)
                elif u < 12:
                    if u == 8:
                        act.wait_ge(x_saved, 16)
                    act.wait_ge(vt_psum, 2 * (NW + j - 1))
                    evacuate(TMP[j % 2], t)
                    A(VTS[:, j], TMP[j % 2][:, TP:T], ACT.Copy).then_inc(vts_ready, 1)
                elif u < 16:
                    if j < 2:
                        act.wait_ge(vt_psum, 2 * (NW + 3 + (j > 0)))
                    else:
                        act.wait_ge(tmp_out[j % 2], 48)
                    evacuate(TMP[j % 2], t, ACT.Sigmoid)
                    act.dma_start(o["o_scr"][j], TMP[j % 2]).then_inc(tmp_out[j % 2], 16)
                else:
                    if j == 0:
                        act.wait_ge(px_zero, 1)
                    else:
                        act.wait_ge(pz_ready, j)
                        act.wait_ge(pool_out, 32 * j)
                    evacuate(PX[:, PREV:PREV + T], t)
                    A(SX[:, :, PREV], PX[:, PREV + TP:PREV + T], ACT.Copy).then_inc(px_ready, 1)
                    act.wait_ge(px_ready, j + 1)
                    act.wait_ge(sx_ready, j + 1)
                    act.dma_start(o["pool_p"][j], PX[:, TP:TP + PREV]).then_inc(pool_out, 16)
                    act.dma_start(o["pool_s"][j], SX[:, :, 1:16]).then_inc(pool_out, 16)
                if u == 4:
                    act.wait_ge(acol_psum, 1)
                    A(ACOL[:].rearrange("p c h -> p (c h)"), M0[:, 0:NB * HC], ACT.Copy).then_inc(acol_ready, 1)
                unit_used(U_IO + u, deferred=(U_OO + 3, U_OO + 4))
                if 9 <= u <= 12:
                    values_turned(u - 9, 1)
                if u == 5:
                    act.wait_ge(sgate_args, 1)
                    A(SROWS[:, 0:3].rearrange("p k b -> p (k b)"), SROWS[:, 4:7].rearrange("p k b -> p (k b)"),
                      ACT.Exp).then_inc(srows_ready, 1)
                if u == 15:
                    act.wait_ge(srows_psum, 1)
                    A(SBC[:].rearrange("p h k b -> p (h k b)"), M0[:, 0:HC * 3 * B], ACT.Copy).then_inc(sbc_ready, 1)
                if u == 13:
                    act.wait_ge(vrow_psum, 1)
                    A(SROW[:], M0[0:B], ACT.Copy).then_inc(vrow_sbuf, 1)
                if u >= 17:
                    for g in ([u - 17] if u < 19 else [2, 3]):
                        t = T_PM[g]
                        act.wait_ge(tmp_out[g % 2], 64 if g < 2 else 80)
                        evacuate(TMP[g % 2], t, ACT.Identity, scale=PRM[:, O_PSCALE + g:O_PSCALE + g + 1])
                        act.dma_start(o["p_scr"][g], TMP[g % 2]).then_inc(tmp_out[g % 2], 16)

            def chunk_in(i):
                ch, h = divmod(i, HC)
                x, w, e = XA[i % 2], XW[i % 2], XE[i % 4]
                act.wait_ge(xa_psum, i + 1)
                wait(act, kw_ready, i - 1)
                wait(act, hc_ready, i - 3)
                A(x, G[i % 2][:, 0], ACT.Copy).then_inc(xa_sbuf, 1)
                act.wait_ge(xa_sbuf, i + 1)
                A(e[:, 0:P], x[:, 0:P], ACT.Exp, scale=-1.0, bias=APV[:, h:h + 1])
                A(e[:, P:2 * P], x[:, P:2 * P], ACT.Exp, scale=-1.0)
                A(WG[:, i % 2:i % 2 + 1], x[:, P - 1:P], ACT.Exp, scale=-1.0, bias=ACOL[:, ch, h:h + 1])
                act.wait_ge(wm_ready, i + 1)
                A(w[:, 0:P], w[:, 0:P], ACT.Exp, bias=ACOL[:, ch, h:h + 1]).then_inc(w_exp, 1)

            def chunk_out(i):
                act.wait_ge(y_psum, i + 1)
                A(XE[i % 4][:, 2 * P:3 * P], G[i % 2][:, 1, P:2 * P], ACT.Abs).then_inc(den_abs, 1)

            act.wait_ge(w_lo, U_OO + SLOTS)
            act.wait_ge(mrow_ready, 1)
            for i in range(HC * NB):
                if i >= 1:
                    wait(act, apv_ready, i - HC + 1)
                chunk_in(i)
                if i:
                    chunk_out(i - 1)
                if i in (8, 10, 12, 14):
                    c = i // 2 - 4
                    act.wait_ge(pool_back, 16)
                    A(HHI[:, NW + c], HF[:, 1, (NW + c) * T:(NW + c + 1) * T], ACT.Copy).then_inc(back_hi, 1)
            chunk_out(HC * NB - 1)
            act.wait_ge(hc_ready, HC * NB)
            load(U_OO + 3)
            load(U_OO + 4)
            act.wait_ge(c_out, 16)
            for c in range(NW):
                act.wait_ge(hc_gated, c + 1)
                A(HHI[:, c], HCT[:, c], ACT.Copy).then_inc(hc_hi, 1)
            act.dma_start(o["m_p"], GB[0:HC, TP - 1:TP]).then_inc(act_outs, 16)
            act.dma_start(o["m_s"], SROWS[:, 3]).then_inc(act_outs, 16)
            act.wait_ge(qn_ready, 1)
            act.dma_start(o["n_s"], SM[:, 1]).then_inc(act_outs, 16)

            project(U_OO, T_OO, 3)
            mlp(1)
            norm(4, halves=False)

        @block.vector
        def _(dve):
            own = Own(dve, own_dve)
            TT, TS, STT = nc.vector.tensor_tensor, nc.vector.tensor_scalar, nc.vector.scalar_tensor_tensor

            def free(ins, t):
                ins.then_inc(tile_free[t % 2], 1)

            def add_square(n, c):
                dve.wait_ge(sq_ready, n * ND + c + 1)
                if c > 1:
                    dve.wait_ge(sq_summed, n * (ND - 1) + c - 1)
                TT(ACC, ACC, SQ[c % 2], ALU.add).then_inc(sq_summed, 1)

            def norm(n):
                t = T_N[n]
                for c in range(1 if n == 0 else ND - 1, ND):
                    add_square(n, c)
                if n == 0:
                    dve.wait_ge(par_in, 16 * PAR_LOADS)
                def inverse(b):
                    if b < BANKS - 1:
                        dve.wait_ge(std_ready, n * (BANKS - 1) + b + 1)
                    else:
                        dve.wait_ge(tile_free[t % 2], freed(t))
                    own.link(nc.vector.reciprocal(third(RSTD, b), third(RSTD, b)))

                def low(b, c):
                    dve.wait_ge(h_hi, (n * BANKS + b) * ND + c + 1)
                    TT(third(HLO[:, c], b), third(HN[c % 4], b), third(HHI[:, c], b).bitcast(F32), ALU.subtract
                       ).then_inc(h_lo_dve, 1)

                def gain(c):
                    return PRM[:, GAINS[n] + c:GAINS[n] + c + 1]

                if n == 4:
                    for b in range(BANKS):
                        inverse(b)
                    for c in range(ND):
                        STT(out=XT[:, c], in0=XT[:, c], scalar=gain(c), in1=RSTD, op0=ALU.mult, op1=ALU.mult
                            ).then_inc(y_ready, 1)
                    return
                for b in range(BANKS):
                    inverse(b)
                    for c in range(ND):
                        if c >= 4:
                            dve.wait_ge((h_lo_dve, h_lo_pool)[c % 2], (n * BANKS + b) * (ND // 2) + (c - 4) // 2 + 1)
                        STT(out=third(HN[c % 4], b), in0=third(XT[:, c], b), scalar=gain(c), in1=third(RSTD, b),
                            op0=ALU.mult, op1=ALU.mult).then_inc(h_raw, 1)
                        if c % 2:
                            low(b, c - 1)

            def key_group(g):
                b, slot = g // 8, g % 2
                if g < GROUPS:
                    if g == 0:
                        dve.wait_ge(bias_sbuf, 4)
                    dve.wait_ge(qb_loaded, 16 * (b + 1))
                    dve.wait_ge(kd_loaded[slot], 16 * KD * (g // 2 + 1))
                    ring = KDS[slot]
                    TT(ring, ring, QB[:, b % 2:b % 2 + 1, :].to_broadcast([P, KD, NW * P]), ALU.mult
                       ).then_inc(kd_mul, 1)
                if g:
                    key_sums(g - 1, KPS[(g - 1) % 3], KD, k_mul, kp_red)
                    dve.wait_ge(kp_red, g)
                    dve.wait_ge(kd_red, g)
                    q = g - 1
                    dst = SCR[:, q // 8, (q % 8) * PG:(q % 8 + 1) * PG]
                    TT(dst, dst, KTMP[:, q % 2], ALU.add).then_inc(k_added, 1)
                if g < GROUPS:
                    wait(dve, k_added, g - 1)
                    key_sums(g, KDS[slot], 0, kd_mul, kd_red)

            def key_sums(g, pages, p0, multiplied, summed):
                dve.wait_ge(multiplied, g + 1)
                nc.vector.tensor_reduce(KTMP[:, g % 2, p0:p0 + 2].rearrange("p g h -> p (g h)"),
                                        pages.rearrange("p g (h d) -> p (g h) d", d=HD),
                                        AX.X, ALU.add).then_inc(summed, 1)

            norm(0)
            dve.wait_ge(logf_in, 32)
            nc.vector.tensor_reduce(TOT[:], LG.rearrange("p s q h -> p s h q"), AX.X, ALU.add).then_inc(tot_ready, 1)
            dve.wait_ge(logsig_in, 1)
            STT(out=GA[:], in0=GA[:], scalar=0.0, in1=GB[:], op0=ALU.min, op1=ALU.subtract).then_inc(logf_ready, 1)
            dve.wait_ge(logf_ready, 1)
            nc.vector.tensor_tensor_scan(GB[:, 0:TP], ones[0:HB, 0:1].to_broadcast([HB, TP]), GA[:, 0:TP], 0.0,
                                         ALU.mult, ALU.subtract).then_inc(fcum_ready, 1)

            def conv(cv, out, taps, state, step):
                s0, s1 = state[:, :, 0], state[:, :, 1]
                own.link(TS(out[:, 0:TP], cv[:, 0:TP], taps[0], None, ALU.mult))
                own.link(TS(out[:, TP:T], s0, taps[0], None, ALU.mult))
                own.link(STT(out=out[:, 0:TP], in0=cv[:, 1:TP + 1], scalar=taps[1], in1=out[:, 0:TP],
                             op0=ALU.mult, op1=ALU.add))
                own.link(STT(out=out[:, TP:T], in0=s1, scalar=taps[1], in1=out[:, TP:T], op0=ALU.mult, op1=ALU.add))
                ins = STT(out=out, in0=cv[:, 2:T + 2], scalar=taps[2], in1=out, op0=ALU.mult, op1=ALU.add)
                step(ins)

            key = [0]
            for u in range(24):
                t, jc, kind = T_IE + u, (u - 12) // 3, (u - 12) % 3
                for _ in range(K_PLAN.get(u, 0)):
                    key_group(key[0])
                    key[0] += 1
                if u >= 12 and kind == 1:
                    if jc == 0:
                        dve.wait_ge(tmp_out[1], 32)
                        dve.wait_ge(vt_psum, 2 * NW)
                        dve.wait_ge(cvx_zero, 1)
                    else:
                        dve.wait_ge(a_saved, 16 * jc)
                    dve.wait_ge(tile_free[(t - 1) % 2], freed(t - 1))
                    dve.wait_ge(tile_done, t + 1)
                    free(TT(by3(CVX[:, 2:2 + T]), psum_tile(t), by3(TMP[0]), ALU.mult), t)
                    dve.wait_ge(tile_free[t % 2], freed(t))
                    state = PRM[:, O_SCONVA + jc * 2 * B:O_SCONVA + (jc + 1) * 2 * B].rearrange("p (b r) -> p b r", r=2)
                    conv(CVX, TMP[1], [PRM[:, O_CONVA + jc * 3 + x:O_CONVA + jc * 3 + x + 1] for x in range(3)],
                         state, own.link)
                    nc.vector.tensor_copy(FOUT[:, jc, 0:2], CVX[:, TP:TP + 2])
                    FO = FOUT[:, jc, 2:].rearrange("p (b r) -> p b r", r=2)
                    nc.vector.tensor_copy(FO[:, :, 0], state[:, :, 1])
                    nc.vector.tensor_copy(FO[:, :, 1], CVX[:, TP + 2:T + 2]).then_inc(fout_conv, 1)
                if u >= 12 and kind == 2:
                    dve.wait_ge(tile_done, t + 1)
                    free(TT(by3(TMP[1]), psum_tile(t), by3(TMP[1]), ALU.mult), t)

            def pair_low(j):
                for n, (full, high, low) in enumerate(((KT, KHI, KLO), (QT, QHI, QLO))):
                    dve.wait_ge(att_in_hi, 2 * j + n + 2)
                    TT(low[:, j, 0:TP], full[:, j, 0:TP], high[j][:, 0:TP].bitcast(F32), ALU.subtract
                       ).then_inc(att_in_lo, 1)

            def inverse(k):
                dve.wait_ge(p_ready, k + 1)
                wait(dve, o_sbuf, k - 3)
                nc.vector.reciprocal(FMX[:, 3, k % 4:k % 4 + 1], FMX[:, 2, k % 4:k % 4 + 1]).then_inc(rsum_ready, 1)

            def attend(x):
                h, step = ORDER[x][1:]
                k, n = h * NB + step, (BLOCKS[step] + 1) * P
                if step == 0:
                    xn = ORDER.index(("n", h))
                    dve.wait_ge(s_free[xn % 2], xn // 2 + 1)
                if k >= 2:
                    dve.wait_ge(pt_psum, ROUNDS[k - 2])
                dve.wait_ge(s_done, x + 1)
                nc.vector.tensor_tensor_reduce(SC[k % 2][:, 0:n], GF[x % 2][:, 0:n], NEGF[h % 2][:, 0:n], 1.0,
                                               -3.0e38, ALU.add, ALU.max, FMX[:, 0, k % 4:k % 4 + 1]
                                               ).then_inc(s_free[x % 2], 1)
                dve.wait_ge(s_free[x % 2], x // 2 + 1)
                TS(FMX[:, 1, k % 4:k % 4 + 1], FMX[:, 0, k % 4:k % 4 + 1], -1.0, None, ALU.mult).then_inc(sc_ready, 1)
                if k:
                    inverse(k - 1)
                return h, step, k

            dve.wait_ge(act_outs, 16 * (NW + 1))
            dve.wait_ge(att_in_hi, 1)
            TT(FLO[:, 0:TP], GB[:, 0:TP], FHI[:, 0:TP].bitcast(F32), ALU.subtract).then_inc(att_in_lo, 1)
            pair_low(0)
            dve.wait_ge(w_lo, U_OE + SLOTS)
            dve.wait_ge(a_saved, 16 * NW)
            for s in range(EARLY):
                attend(1 + s)
                if s < K_LATE:
                    key_group(GROUPS - K_LATE + s)
            key_group(GROUPS)
            dve.wait_ge(k_added, GROUPS)

            nc.vector.tensor_reduce(MX[:], SCR[:].rearrange("p b g h -> p b h g"), AX.X, ALU.max).then_inc(smax_ready, 1)
            dve.wait_ge(smax_all, 1)
            TT(SCR[:], SCR[:], MXA[:].rearrange("p b (a h) -> p b a h", a=1).to_broadcast([P, B, PAGES, HB]),
               ALU.subtract).then_inc(sshift, 1)
            c4 = lambda k: SM[:, k].rearrange("p (c b) -> p c b", c=NW)
            TT(c4(0), QT[:, :, TP:T], KT[:, :, TP:T], ALU.mult).then_inc(qk_new, 1)
            dve.wait_ge(sprob, 1)
            nc.vector.tensor_reduce(RSS[:], SCR[:].rearrange("p b g h -> p b h g"), AX.X, ALU.add).then_inc(ssum, 1)

            def sample_weights():
                dve.wait_ge(smax_all, 1)
                dve.wait_ge(vts_ready, NW)
                dve.wait_ge(fin_psum, 1)
                dve.wait_ge(v_summed, B)
                for par in range(2):
                    r = slice(64 * par, 64 * par + 64)
                    by_b = lambda v: v.rearrange("p b (c two) -> p c b two", two=2)[:, :, :, par]
                    own.link(nc.vector.tensor_copy(c4(2)[r], by_b(MXA[r])))
                    own.link(nc.vector.tensor_copy(c4(3)[r], by_b(M1[r, 64:128].rearrange("p (b h) -> p b h", b=B))))
                own.link(nc.vector.tensor_copy(c4(8), M1[:, 0:NW * B].rearrange("p (b c) -> p c b", b=B)))
                own.link(nc.vector.tensor_copy(SM[:, 9], M1[:, 160:192]))
                own.link(TT(SM[:, 1], M1[:, 128:160], SM[:, 9], ALU.subtract))
                own.link(TT(SM[:, 9], SM[:, 1], SM[:, 2], ALU.max))
                own.link(TT(SM[:, 4], SM[:, 2], SM[:, 9], ALU.subtract))
                TT(SM[:, 5], SM[:, 1], SM[:, 9], ALU.subtract).then_inc(fin_args, 1)

            def sample_attention():
                dve.wait_ge(fin_exp, 1)
                own.link(TT(SM[:, 9], SM[:, 6], SM[:, 3], ALU.mult))
                own.link(TT(SM[:, 9], SM[:, 9], SM[:, 7], ALU.add))
                own.link(nc.vector.reciprocal(SM[:, 9], SM[:, 9]))
                own.link(TT(SM[:, 8], SM[:, 8], SM[:, 6], ALU.mult))
                own.link(TT(SM[:, 10], VTS[:].rearrange("p c b -> p (c b)"), SM[:, 7], ALU.mult))
                own.link(TT(SM[:, 8], SM[:, 8], SM[:, 10], ALU.add))
                TT(SM[:, 10], SM[:, 8], SM[:, 9], ALU.mult).then_inc(fin_att, 1)
                dve.wait_ge(fin_att, 1)
                dve.wait_ge(fin_hi, 1)
                TT(HLO[:, NW:ND, TP:T], c4(10), HHI[:, NW:ND, TP:T].bitcast(F32), ALU.subtract).then_inc(sfeat, 1)

            values = values_of(dve, TT, slice_of_dve, 0, v_used_dve, own)
            for x, item in enumerate(ORDER):
                if item[0] == "n" or x <= EARLY:
                    continue
                if item[0] == "s":
                    h, step, k = attend(x)
                    for g in range(VALUES[k - 1], VALUES[k]):
                        values(g)
                    if h % 2 and step == 2 and h + 1 < HB:
                        pair_low((h + 1) // 2)
                    continue
                j = item[1]
                if x == len(ORDER) - 1:
                    inverse(HB * NB - 1)
                    sample_weights()
                    dve.wait_ge(v_used_pool, GROUPS)
                    for n, c in enumerate((1, 2)):
                        dve.wait_ge(back_hi, n + 1)
                        TT(HLO[:, c, 0:TP], QT[:, c, 0:TP], HHI[:, c, 0:TP].bitcast(F32), ALU.subtract
                           ).then_inc(back_lo_dve, 1)
                    sample_attention()
                dve.wait_ge(att_hi, j + 1)
                TT(HLO[:, NW + j, 0:TP], GF[x % 2][:, 0:TP], HHI[:, NW + j, 0:TP].bitcast(F32), ALU.subtract
                   ).then_inc(s_free[x % 2], 1)

            def add_tile(t, m, n):
                free(TT(by3(XT[:, m]), by3(XT[:, m]), psum_tile(t + m), ALU.add), t + m)
                if n and m >= 2:
                    add_square(n, m - 1)

            def residual(t, loads, n):
                dve.wait_ge(x_in, loads)
                for m in range(ND):
                    dve.wait_ge(tile_done, t + m + 1)
                    add_tile(t, m, n)

            residual(T_OE, 64, 1)

            def mlp(layer):
                tb, n0 = T_F[layer], layer * NF
                norm(2 * layer + 1)

                def up(jj, t, gate_free, fpb, up_done, silu, hid):
                    dve.wait_ge(cv_zero, layer + 1)
                    dve.wait_ge(fpb_ready, fpb)
                    dve.wait_ge(tile_free[t % 2], gate_free)
                    state = FPB[:, jj, 4:].rearrange("p (b r) -> p b r", r=2)
                    conv(CV[jj], CC[jj], [FPB[:, jj, x:x + 1] for x in range(3)], state,
                         lambda ins: ins.then_inc(conv_done, 1))
                    dve.wait_ge(silu_done, silu)
                    dve.wait_ge(tile_done, up_done)
                    wait(dve, hid_lo, hid)
                    free(TT(by3(HR[jj]), psum_tile(t + 1), by3(CC[jj]), ALU.mult), t + 1)

                def down(t, done, n=None):
                    for m in range(ND):
                        dve.wait_ge(tile_done, done(m))
                        add_tile(t, m, n)

                for jj in range(2):
                    t = tb + 2 * jj
                    up(jj, t, freed(t), layer * FI + 1, t + 2, n0 + jj + 1, n0)
                with dve.Fori(0, FI - 1) as i:
                    own.enter(i, 8)
                    for jj in range(2):
                        t = tb + 4 + 2 * jj
                        up(jj, t, i * 6 + freed(t), i + (layer * FI + 2), i * 12 + (t + 2), i * 2 + (n0 + jj + 3),
                           i * 2 + (n0 + jj + 1))
                    down(tb + 8, lambda m: i * 12 + (tb + 9 + m))
                own.leave(FI - 1)
                for jj in range(2):
                    dve.wait_ge(hid_hi, n0 + NF - 1 + jj)
                    TT(HIDL[:, jj], HR[jj], HIDH[:, jj].bitcast(F32), ALU.subtract).then_inc(hid_lo, 1)
                t = tb + 12 * FI - 8
                down(t, lambda m: t + m + 1, 2 * layer + 2)

            mlp(0)

            norm(2)
            dve.wait_ge(logsig_in, 2)
            own.link(STT(out=GB[0:HC, :], in0=GB[0:HC, :], scalar=0.0, in1=TROW, op0=ALU.min, op1=ALU.subtract))
            one_row = ones[0:HC, 0:1].to_broadcast([HC, TP])
            own.link(nc.vector.tensor_tensor_scan(BROW, one_row, GB[0:HC, 0:TP], 0.0, ALU.mult, ALU.add))
            TT(AROW, AROW, BROW, ALU.subtract).then_inc(arow_ready, 1)
            dve.wait_ge(arow_ready, 1)
            own.link(nc.vector.tensor_tensor_scan(MAXROW, one_row, AROW, 0.0, ALU.mult, ALU.max))
            own.link(TT(MROW, BROW, MAXROW, ALU.add))
            m0 = PRM[0:HC, O_M0:O_M0 + B]
            li, lf = GA[0:HC, TP:T], GB[0:HC, TP:T]
            own.link(TT(SROWS[:, 4], lf, m0, ALU.add))
            own.link(TT(SROWS[:, 3], SROWS[:, 4], li, ALU.max))
            own.link(TT(SROWS[:, 4], SROWS[:, 4], SROWS[:, 3], ALU.subtract))
            own.link(TT(SROWS[:, 5], li, SROWS[:, 3], ALU.subtract))
            TS(SROWS[:, 6], SROWS[:, 3], -1.0, None, ALU.mult).then_inc(sgate_args, 1)
            nc.vector.memset(APV[:], 0.0)
            nc.vector.memset(CST[:], 0.0).then_inc(mrow_ready, 1)
            dve.wait_ge(mrow_ready, 1)

            dve.wait_ge(sbc_ready, 1)
            hb = lambda k: SM[:, k].rearrange("p (h b) -> p h b", h=HC)
            n0v = PRM[:, O_N0:O_N0 + HC * B].rearrange("p (h b) -> p h b", h=HC)
            own.link(TT(hb(0), KT[:, :, TP:T], SBC[:, :, 1], ALU.mult))
            own.link(TT(hb(1), n0v, SBC[:, :, 0], ALU.mult))
            own.link(TT(hb(1), hb(1), hb(0), ALU.add))
            TT(hb(2), hb(1), QT[:, :, TP:T], ALU.mult).then_inc(qn_ready, 1)

            for g, win in enumerate(WINS):
                t = T_P[g]
                if g >= 2:
                    dve.wait_ge(tile_done, T_PM[g - 2] + 1)
                dve.wait_ge(px_ready, g + 1)
                dve.wait_ge(sx_ready, g + 1)
                src, lo = PX, 0
                for lev in range(g + 1):
                    s = 1 << lev
                    lo += s
                    dst = PD[lev % 2]
                    own.link(TT(dst[:, lo:PREV + TP], src[:, lo:PREV + TP], src[:, lo - s:PREV + TP - s], ALU.add))
                    src = dst
                z = PZ[g % 2]
                own.link(STT(out=z[:, 0:TP], in0=src[:, PREV:PREV + TP], scalar=1.0 / win, in1=PX[:, PREV:PREV + TP],
                             op0=ALU.mult, op1=ALU.subtract))
                own.link(TT(z[:, 0:PREV], src[:, PREV:2 * PREV], PRM[:, O_RCP + g * PREV:O_RCP + (g + 1) * PREV], ALU.mult))
                own.link(TT(z[:, 0:PREV], z[:, 0:PREV], PX[:, PREV:2 * PREV], ALU.subtract))
                own.link(nc.vector.tensor_reduce(SXS[:], SX[:, :, 16 - win:16], AX.X, ALU.add))
                STT(out=z[:, TP:T], in0=SXS[:], scalar=1.0 / win, in1=SX[:, :, PREV], op0=ALU.mult, op1=ALU.subtract
                    ).then_inc(pz_ready, 1)

            def chunk_in(i):
                ch, h = divmod(i, HC)
                x, w, e = XA[i % 2], XW[i % 2], XE[i % 4]
                wait(dve, y_psum, i - 1)
                dve.wait_ge(xa_sbuf, i + 1)
                STT(out=w[:, 0:P], in0=x[:, 0:P], scalar=-1.0, in1=CON[:, C_MASKT], op0=ALU.mult, op1=ALU.add
                    ).then_inc(wm_ready, 1)
                dve.wait_ge(w_exp, i + 1)
                nc.vector.tensor_copy(APV[:, h:h + 1], x[:, P - 1:P]).then_inc(apv_ready, 1)
                TT(w[:, P:2 * P], x[:, 2 * P:3 * P], w[:, 0:P], ALU.mult)
                TT(w[:, 2 * P:3 * P], QT[:, h, ch * P:(ch + 1) * P], e[:, 0:P], ALU.mult)
                TS(w[:, 3 * P:4 * P], x[:, 3 * P:4 * P], WG[:, i % 2:i % 2 + 1], None, ALU.mult).then_inc(kw_ready, 1)

            def chunk_out(i):
                ch, h = divmod(i, HC)
                y, e = G[i % 2][:, 1], XE[i % 4]
                dve.wait_ge(den_abs, i + 1)
                STT(out=CST[:, h], in0=CST[:, h], scalar=e[:, P - 1:P], in1=y[:, 2 * P:3 * P + 1], op0=ALU.mult,
                    op1=ALU.add).then_inc(cst_ready, 1)
                own.link(TT(e[:, 2 * P:3 * P], e[:, 2 * P:3 * P], e[:, P:2 * P], ALU.max))
                own.link(nc.vector.reciprocal(e[:, 2 * P:3 * P], e[:, 2 * P:3 * P]))
                TT(HCT[:, h, ch * P:(ch + 1) * P], y[:, 0:P], e[:, 2 * P:3 * P], ALU.mult).then_inc(hc_ready, 1)

            def sample_results():
                dve.wait_ge(snum_psum, B)
                own.link(nc.vector.tensor_copy(SM[:, 3], M0[:, 192:224]))
                own.link(nc.vector.tensor_copy(SM[:, 4], M0[:, 128:160]))
                own.link(STT(out=SM[:, 5], in0=SM[:, 4], scalar=-1.0, in1=SM[:, 4], op0=ALU.mult, op1=ALU.max))
                own.link(TT(hb(4), hb(5), SBC[:, :, 2], ALU.max))
                own.link(nc.vector.reciprocal(SM[:, 4], SM[:, 4]))
                TT(HCT[:, :, TP:T], hb(3), hb(4), ALU.mult).then_inc(hcs_ready, 1)

            dve.wait_ge(tile_done, T_PM[3] + 1)
            for s in range(2):
                dve.wait_ge(tmp_out[s], 96)
            for i in range(HC * NB):
                chunk_in(i)
                if i:
                    chunk_out(i - 1)
                if i == 30:
                    sample_results()
            chunk_out(HC * NB - 1)
            dve.wait_ge(og_in, 16)
            dve.wait_ge(hcs_ready, 1)
            dve.wait_ge(hc_ready, HC * NB)
            dve.wait_ge(c_new, B)
            for c in range(NW):
                TT(HCT[:, c], HCT[:, c], XT[:, c], ALU.mult).then_inc(hc_gated, 1)
                if c % 2:
                    dve.wait_ge(hc_gated, c)
                    dve.wait_ge(hc_hi, c)
                    TT(HLO[:, c - 1], HCT[:, c - 1], HHI[:, c - 1].bitcast(F32), ALU.subtract).then_inc(hc_lo, 1)

            residual(T_OO, 80, 3)
            mlp(1)
            norm(4)

        @block.gpsimd
        def _(pool):
            TT = nc.gpsimd.tensor_tensor

            def low(u, value=None):
                if u < U_END or value is not None:
                    pool.wait_ge(w_hi, u + 1 if value is None else value)
                    s = u % SLOTS
                    TT(WLO[:, s], WRAW[:, s], WHI[:, s].bitcast(F32), ALU.subtract).then_inc(w_lo, 1)

            def norm(n):
                for b in range(BANKS):
                    for c in range(1, ND, 2):
                        pool.wait_ge(h_hi, (n * BANKS + b) * ND + c + 1)
                        TT(third(HLO[:, c], b), third(HN[c % 4], b), third(HHI[:, c], b).bitcast(F32), ALU.subtract
                           ).then_inc(h_lo_pool, 1)

            pool.dma_start(PTI[:], a["pti"]).then_inc(pages_in_pool, 16)
            pool.wait_ge(pages_in_pool, 16)
            for s in range(2):
                pool.indirect_dma_start(out=VF[:, s * 1024:(s + 1) * 1024], out_offset=None, in_=a["clf"],
                                        in_offset=bass.IndirectOffsetOnAxis(ap=PTI[:, s:s + 1], axis=0),
                                        ).then_inc(logf_in, 16)
            pool.wait_ge(gw_hi, 1)
            TT(GWL[:], GWR[:], GWH[:].bitcast(F32), ALU.subtract).then_inc(gw_lo, 1)
            for u in range(SLOTS):
                low(u)
            norm(0)
            pool.wait_ge(h_raw, BANKS * ND)
            nc.gpsimd.memset(CVX[:, 0:2], 0.0).then_inc(cvx_zero, 1)

            def key_products(g):
                    b, slot = g // 8, g % 3
                    pool.wait_ge(qb_loaded, 16 * (b + 1))
                    pool.wait_ge(kp_loaded[slot], 16 * (PG - KD) * (g // 3 + 1))
                    ring = KPS[slot]
                    TT(ring, ring, QB[:, b % 2:b % 2 + 1, :].to_broadcast([P, PG - KD, NW * P]), ALU.mult).then_inc(k_mul, 1)

            key = 0
            for u in range(24):
                for g in range(key, key + K_PLAN.get(u, 0)):
                    key_products(g)
                key += K_PLAN.get(u, 0)
                low(U_IE + u + SLOTS)

            for g in range(GROUPS - K_LATE, GROUPS):
                key_products(g)

            pool.wait_ge(smax_ready, 1)
            nc.gpsimd.partition_all_reduce(MXA[:].rearrange("p b h -> p (b h)"), MX[:].rearrange("p b h -> p (b h)"),
                                           P, RMAX).then_inc(smax_all, 1)

            own = Own(pool, own_pool)
            values = values_of(pool, TT, slice_of_pool, 1, v_used_pool, own)
            for g in range(GROUPS):
                values(g)
            pool.wait_ge(v_used_dve, GROUPS)
            for n, j in enumerate((0, 3)):
                pool.wait_ge(back_hi, n + 3)
                TT(HLO[:, j, 0:TP], QT[:, j, 0:TP], HHI[:, j, 0:TP].bitcast(F32), ALU.subtract
                   ).then_inc(back_lo, 1)
            pool.wait_ge(back_hi, NW + 1)
            TT(HLO[:, 0:NW, TP:T], AS[:], HHI[:, 0:NW, TP:T].bitcast(F32), ALU.subtract).then_inc(back_lo, 1)

            for m in range(ND):
                low(U_OE + m + SLOTS)

            def mlp(layer):
                ub, n0 = U_F[layer], layer * NF
                norm(2 * layer + 1)
                pool.wait_ge(sq_summed, (2 * layer + 2) * (ND - 1))
                pool.wait_ge(tile_done, T_N[2 * layer + 1] + 1)
                nc.gpsimd.memset(CV[0][:, 0:2], 0.0)
                nc.gpsimd.memset(CV[1][:, 0:2], 0.0).then_inc(cv_zero, 1)
                pool.wait_ge(fpar_in, 16 * (layer + 1))
                if layer == 0:
                    pool.wait_ge(fconv_out, 16)
                else:
                    pool.wait_ge(outs, 16)

                def params(i, silu):
                    wait(pool, silu_done, silu)
                    wait(pool, fout_ready, silu)
                    src = FPRM[:, bass.ds(i * 2, 2)]
                    nc.gpsimd.tensor_copy(FPB[:], src).then_inc(fpb_ready, 1)

                def states(i, jj, free, fpb):
                    t = T_F[layer] + 2 * jj
                    pool.wait_ge(tile_free[t % 2], free)
                    pool.wait_ge(fpb_ready, fpb)
                    dst = FOUT[:, bass.ds(i * 2 + jj, 1)].rearrange("p a f -> p (a f)")
                    nc.gpsimd.tensor_copy(dst[:, 0:2], CV[jj][:, TP:TP + 2])
                    pairs = dst[:, 2:].rearrange("p (b r) -> p b r", r=2)
                    nc.gpsimd.tensor_copy(pairs[:, :, 0], FPB[:, jj, 4:].rearrange("p (b r) -> p b r", r=2)[:, :, 1])
                    nc.gpsimd.tensor_copy(pairs[:, :, 1], CV[jj][:, TP + 2:T + 2]).then_inc(fout_ready, 1)

                def hidden(jj, hi):
                    pool.wait_ge(hid_hi, hi)
                    TT(HIDL[:, jj], HR[jj], HIDH[:, jj].bitcast(F32), ALU.subtract).then_inc(hid_lo, 1)

                params(0, n0)
                for jj in range(2):
                    t = T_F[layer] + 2 * jj
                    low(ub + 2 * jj + SLOTS)
                    states(0, jj, freed(t), layer * FI + 1)
                    low(ub + 2 * jj + 1 + SLOTS)
                for jj in range(2):
                    hidden(jj, n0 + jj + 1)
                def step(i):
                    def low_at(u):
                        low(u + 6 * i) if isinstance(i, int) else low(u, i * 6 + (u + 1))

                    params(i + 1, i * 2 + (n0 + 2))
                    for jj in range(2):
                        t = T_F[layer] + 4 + 2 * jj
                        u = ub + 4 + 2 * jj + SLOTS
                        low_at(u)
                        states(i + 1, jj, i * 6 + freed(t), i + (layer * FI + 2))
                        low_at(u + 1)
                    for r in range(2):
                        low_at(ub + 8 + r + SLOTS)
                    if not isinstance(i, int):
                        for jj in range(2):
                            hidden(jj, i * 2 + (n0 + jj + 3))

                with pool.Fori(0, FI - 2) as i:
                    step(i)
                step(FI - 2)
                for r in range(2):
                    low(ub + 6 * FI - 2 + r + SLOTS)

            mlp(0)
            norm(2)

            for u in range(20):
                if u >= 16:
                    j = u - 16
                    if j == 0:
                        pool.wait_ge(x_saved, 16)
                        pool.wait_ge(spool_in, 16)
                        nc.gpsimd.memset(PX[:, 0:PREV], 0.0).then_inc(px_zero, 1)
                    else:
                        pool.wait_ge(pz_ready, j)
                        pool.wait_ge(pool_out, 32 * j)
                    nc.gpsimd.tensor_copy(SX[:, :, 0:PREV], SPOOL[:, j]).then_inc(sx_ready, 1)
                low(U_IO + u + SLOTS)
            pool.wait_ge(sbc_ready, 1)
            pool.wait_ge(qn_ready, 1)
            pool.wait_ge(c0_in, 16)
            pool.wait_ge(vb_in, 16 * B)
            weighted_keys = SM[:, 0].rearrange("p (h b a) -> p b h a", h=HC, a=1)
            kept = SBC[:].rearrange("p h k (b a) -> p k b h a", a=1)[:, 0]
            for b in range(B):
                old = C0[:, b * HC:(b + 1) * HC]
                new = VB[:, b].rearrange("p (h e) -> p h e", h=HC)
                TT(old, old, kept[:, b].to_broadcast([P, HC, DK]), ALU.mult)
                own.link(TT(new, new, weighted_keys[:, b].to_broadcast([P, HC, DK]), ALU.mult))
                TT(old, old, new, ALU.add).then_inc(c_new, 1)
            for c in range(NW):
                pool.wait_ge(back_hi, NW + 2 + c)
                TT(HLO[:, NW + c], HF[:, 1, (NW + c) * T:(NW + c + 1) * T], HHI[:, NW + c].bitcast(F32), ALU.subtract
                   ).then_inc(back_lo, 1)
            for c in (1, 3):
                pool.wait_ge(hc_gated, c + 1)
                pool.wait_ge(hc_hi, c + 1)
                TT(HLO[:, c], HCT[:, c], HHI[:, c].bitcast(F32), ALU.subtract).then_inc(hc_lo_pool, 1)
            for m in range(ND):
                low(U_OO + m + SLOTS)
            mlp(1)


_SCRATCH = {"q_scr": (B, NW * P), "v_scr": (B, NW * P), "a_scr": (NW, P, T), "o_scr": (NW, P, T),
            "p_scr": (NW, P, T), "x_scr": (P, ND, T)}
_OUTS = {"y": (ND, P, T), "k": (NW, P, T), "v": (NW, P, T), "logf": (HB, T), "conv_a": (P, NW, 2 + 2 * B),
         "c_p": (P, HC, DK + 1), "c_s": (P, HC * B, DK), "n_s": (P, HC * B), "m_p": (HC, 1), "m_s": (HC, B),
         "pool_p": (NW, P, PREV), "pool_s": (NW, P, B, PREV), "ffn": (2, P, NF, 2 + 2 * B)}


def _chunks(x):
    return np.ascontiguousarray(np.moveaxis(x.reshape((-1, P) + x.shape[1:]), 0, 1))


def _units(w):
    n = w.shape[1] // P
    return w.reshape(ND, P, n, P).transpose(2, 1, 0, 3).reshape(n, P, UNIT)


def _mlp_units(w_up, w_down):
    up, down = _units(w_up), w_down.reshape(NF, P, UNIT)
    out = []
    for i in range(FI + 1):
        if i < FI:
            for j in (2 * i, 2 * i + 1):
                out += [up[j], up[NF + j]]
        if i:
            out += [down[2 * i - 2], down[2 * i - 1]]
    return np.stack(out)


def _weights(x):
    we, wo = x["w_in_even"][0], x["w_in_odd"][0]
    a, w, k = 512, _units(we[:, 0:6 * 512]), 4
    conv = [w[g * k + j] for j in range(k) for g in (0, 2, 1)]
    odd = np.concatenate([wo[:, 0:4 * a], wo[:, 4 * a + 2 * HC:]], axis=1)
    return np.concatenate([w[3 * k:], np.stack(conv), _units(x["w_out_even"][0]), _mlp_units(x["w_up"][0], x["w_down"][0]),
                           _units(odd), _units(x["w_out_odd"][0]), _mlp_units(x["w_up"][1], x["w_down"][1])])


def _params(x):
    p = np.zeros((P, O_END), np.float32)
    for n in range(2):
        p[:, O_GMIX + n * ND:O_GMIX + (n + 1) * ND] = _chunks(x["norm_mix"][n])
        p[:, O_GFFN + n * ND:O_GFFN + (n + 1) * ND] = _chunks(x["norm_ffn"][n])
    p[:, O_GFIN:O_GFIN + ND] = _chunks(x["norm_final"])
    p[:, O_CONVA:O_CONVA + NW * 3] = _chunks(x["conv_a"][0].T).reshape(P, -1)
    p[:, O_PSCALE:O_PSCALE + NW] = _chunks(x["pool_scale_odd"][0])
    p[0:HB, O_GB] = x["b_forget_even"][0]
    p[0:HC, O_GB + 1] = x["b_igate_odd"][0]
    p[HC:2 * HC, O_GB + 1] = x["b_fgate_odd"][0]
    p[:, O_SCONVA:O_SCONVA + NW * B * 2] = _chunks(x["state_conv_a"][0].transpose(2, 0, 1)).reshape(P, -1)
    for g, win in enumerate(WINS):
        for t in range(PREV):
            p[:, O_RCP + g * PREV + t] = 1.0 / min(win, t + 1)
    p[:, O_N0:O_N0 + HC * B] = x["state_mlstm_n"][0].transpose(2, 1, 0).reshape(P, -1)
    p[0:HC, O_M0:O_M0 + B] = x["state_mlstm_m"][0].T
    p[:, O_EPS] = EPS
    return p


def _mlp_params(x):
    taps = x["ffn_conv_w"].transpose(0, 2, 1)
    bias = x["ffn_conv_b"][:, :, None]
    state = x["state_ffn_conv"].transpose(0, 3, 1, 2).reshape(2, FF, 2 * B)
    return np.stack([_chunks(np.concatenate([taps[n], bias[n], state[n]], axis=1)) for n in range(2)])


def _constants():
    i = np.arange(P)
    c = np.zeros((P, NCON, P), np.float32)
    c[:, C_ID] = np.eye(P)
    c[:, C_ONE] = 1.0
    c[:, C_MASK] = np.where(i[None, :] > i[:, None], NEG, 0.0)
    c[:, C_MASKT] = np.where(i[:, None] > i[None, :], NEG, 0.0)
    c[:, C_LATER] = i[:, None] > i[None, :]
    same = i[:, None] // PAGES == i[None, :] // PAGES
    c[:, C_PLATER] = same & (i[:, None] > i[None, :])
    c[:, C_BLK] = i[:, None] // HD == i[None, :] // HD
    s = np.zeros((HB, NW, P), np.float32)
    for h in range(HB):
        s[h, h // 2, (h % 2) * HD:(h % 2 + 1) * HD] = 1.0
    return c, s


def kernel(**inputs):
    import concourse.bacc as bacc
    from concourse.bass_utils import run_bass_kernel_spmd

    x = {k: np.asarray(v) for k, v in inputs.items()}
    con, selc = _constants()
    gw = np.stack([_chunks(x["w_in_even"][0][:, 3072:3080]), _chunks(x["w_in_odd"][0][:, 2048:2056])], axis=1)
    phys = x["cache_k"].shape[1]
    arrays = {
        "xp": _chunks(x["x_prompt"][0].T), "xs": _chunks(x["x_sample"][:, 0].T),
        "ck": x["cache_k"].reshape(phys, P, 512), "cv": x["cache_v"].reshape(phys, P, 512),
        "clf": x["cache_logf"].reshape(phys, P * HB), "pt": x["page_table"].reshape(1, -1),
        "pti": x["page_table"].reshape(2, P).T, "w": _weights(x), "gw": gw, "prm": _params(x),
        "fprm": _mlp_params(x), "con": con, "selc": selc, "pw": x["w_pool_odd"][0].transpose(1, 0, 2),
        "c0": x["state_mlstm_c"][0].transpose(2, 0, 1, 3).reshape(P, HC * B, DK),
        "spool": _chunks(x["state_pool"][0].transpose(2, 0, 1)),
    }
    arrays = {k: np.ascontiguousarray(v) for k, v in arrays.items()}
    nc = bacc.Bacc("TRN2", target_bir_lowering=False, num_devices=1, dynamic_dma_scratch_size=2048)
    ins = {k: nc.dram_tensor(f"in_{k}", v.shape, mybir.dt.from_np(v.dtype), kind="ExternalInput").ap()
           for k, v in arrays.items()}
    outs = {k: nc.dram_tensor(f"out_{k}", s, F32, kind="ExternalOutput").ap() for k, s in _OUTS.items()}
    outs |= {k: nc.dram_tensor(k, s, F32, kind="Internal").ap() for k, s in _SCRATCH.items()}
    trunk(nc, ins, outs)
    r = run_bass_kernel_spmd(nc, [{f"in_{k}": v for k, v in arrays.items()}], core_ids=[0]).results[0]
    g = {k: np.asarray(r[f"out_{k}"]).reshape(s) for k, s in _OUTS.items()}

    def tokens(v):
        v = v.reshape(-1, T).T
        return v[:TP], v[TP:]

    yp, ys = tokens(g["y"])
    kp, ks = tokens(g["k"])
    vp, vs = tokens(g["v"])
    lp, ls = tokens(g["logf"])

    def states(v):
        v = v.transpose(2, 1, 0).reshape(2 + 2 * B, -1)
        return v[None, 0:2], v[2:].reshape(B, 2, -1)

    cp, cs = states(g["conv_a"])
    fp, fs = zip(*(states(g["ffn"][n]) for n in range(2)))
    c_p = g["c_p"].transpose(1, 0, 2)
    pool_p = g["pool_p"].reshape(512, PREV).T
    pool_s = g["pool_s"].reshape(512, B, PREV).transpose(1, 2, 0)
    out = (yp[None], ys[:, None],
           kp.reshape(1, 1, TP, HB, HD), ks.reshape(1, B, 1, HB, HD),
           vp.reshape(1, 1, TP, HB, HD), vs.reshape(1, B, 1, HB, HD),
           lp.reshape(1, 1, TP, HB), ls.reshape(1, B, 1, HB), cp[None], cs[None],
           c_p[None, None, :, :, 0:DK], g["c_s"].reshape(P, B, HC, DK).transpose(1, 2, 0, 3)[None],
           c_p[None, None, :, :, DK], g["n_s"].reshape(P, HC, B).transpose(2, 1, 0)[None],
           g["m_p"].reshape(1, 1, HC), g["m_s"].T[None],
           pool_p[None, None], pool_s[None], np.stack(fp), np.stack(fs))
    return tuple(np.ascontiguousarray(v) for v in out)
```
